# Optimizing a Trainium2 kernel written in Bass

```python
import math
import jax, jax.numpy as jnp
from jax import lax
import numpy as np

D_MODEL = 1024
BATCH = 1
SEQ = 2048
DEPTH = 1
DEC_BATCH = 8
DEC_SEQ = 8
PAST_LEN = 16384
PAGE_SIZE = 128

PLE_DIM = 256
MIX_WIDTH = D_MODEL
POOL_WIDTH = MIX_WIDTH // 2
POOL_WINDOWS = (2, 4, 8, 16)
POOL_GROUPS = len(POOL_WINDOWS)
POOL_GROUP_DIM = POOL_WIDTH // POOL_GROUPS
POOL_BUF = max(POOL_WINDOWS) - 1
GLA_VDIM = MIX_WIDTH - POOL_WIDTH
GLA_HEADS = 4
GLA_HEAD_V = GLA_VDIM // GLA_HEADS
GLA_KDIM = GLA_VDIM // 2
GLA_HEAD_K = GLA_KDIM // GLA_HEADS
GLA_GATE_RANK = 16
GLA_GATE_NORMALIZER = 16.0
GLA_CHUNK = 64
D_FF = 2816
CONV_W = 3
CONV_BUF = CONV_W - 1
EPS = 1e-6

SPLIT_IDX = (
    POOL_WIDTH,
    POOL_WIDTH + GLA_KDIM,
    POOL_WIDTH + 2 * GLA_KDIM,
    POOL_WIDTH + 2 * GLA_KDIM + GLA_VDIM,
    POOL_WIDTH + 2 * GLA_KDIM + GLA_VDIM + GLA_GATE_RANK,
)
IN_PROJ_DIM = SPLIT_IDX[-1] + GLA_VDIM

kernel_name = "pool_gla_hybrid_decode_step"

def rmsnorm(x, g):
    xf = x.astype(jnp.float32)
    y = xf * lax.rsqrt(jnp.mean(xf * xf, axis=-1, keepdims=True) + EPS)
    return (y * g.astype(jnp.float32)).astype(x.dtype)

def pool_mixer(z, buf, start, w_pool, pool_scale):
    B, L, _ = z.shape
    zcat = jnp.concatenate([buf.astype(z.dtype), z], axis=1)
    zf = zcat.astype(jnp.float32)
    cs = jnp.pad(jnp.cumsum(zf, axis=1), ((0, 0), (1, 0), (0, 0)))
    end = cs[:, POOL_BUF + 1:]
    zt = zf[:, POOL_BUF:]
    pos = start + jnp.arange(L)
    outs = []
    for gi, w in enumerate(POOL_WINDOWS):
        sl = slice(gi * POOL_GROUP_DIM, (gi + 1) * POOL_GROUP_DIM)
        lo = POOL_BUF + 1 - w
        wsum = end[..., sl] - cs[:, lo:lo + L, sl]
        cnt = jnp.minimum(pos + 1, w).astype(jnp.float32)[None, :, None]
        outs.append(wsum / cnt - zt[..., sl])
    u = jnp.stack(outs, axis=2)
    y = jnp.einsum('blgc,gcd->blgd', u, w_pool.astype(jnp.float32)).reshape(B, L, POOL_WIDTH)
    y = y * pool_scale.astype(jnp.float32)
    return y.astype(z.dtype), zcat[:, -POOL_BUF:]

def gla_mixer(q, k, v, gk, og, state, gla_norm):
    B, L, _ = q.shape
    f32 = jnp.float32

    def heads(t, d):
        return t.reshape(B, L, GLA_HEADS, d).transpose(0, 2, 1, 3).astype(f32)

    qh = heads(q, GLA_HEAD_K) * (GLA_HEAD_K ** -0.5)
    kh = heads(k, GLA_HEAD_K)
    vh = heads(v, GLA_HEAD_V)
    gh = heads(gk, GLA_HEAD_K)
    C = math.gcd(L, GLA_CHUNK)
    n = L // C

    def chunks(t):
        return jnp.moveaxis(t.reshape(B, GLA_HEADS, n, C, t.shape[-1]), 2, 0)

    causal = jnp.tril(jnp.ones((C, C), dtype=bool))[:, :, None]

    def step(S, inp):
        qc, kc, vc, gc = inp
        b = jnp.cumsum(gc, axis=2)
        o_inter = jnp.einsum('bhtd,bhdv->bhtv', qc * jnp.exp(b), S)
        diff = b[:, :, :, None, :] - b[:, :, None, :, :]
        decay = jnp.exp(jnp.where(causal, diff, -jnp.inf))
        A = jnp.einsum('bhtd,bhsd,bhtsd->bhts', qc, kc, decay)
        o = o_inter + jnp.einsum('bhts,bhsv->bhtv', A, vc)
        b_last = b[:, :, -1, :]
        S = jnp.exp(b_last)[..., None] * S + jnp.einsum(
            'bhsd,bhsv->bhdv', kc * jnp.exp(b_last[:, :, None, :] - b), vc)
        return S, o

    S_fin, o = lax.scan(step, state.astype(f32), (chunks(qh), chunks(kh), chunks(vh), chunks(gh)))
    o = jnp.moveaxis(o, 0, 2).reshape(B, GLA_HEADS, L, GLA_HEAD_V)
    o = rmsnorm(o, gla_norm)
    o = o.transpose(0, 2, 1, 3).reshape(B, L, GLA_VDIM) * jax.nn.silu(og.astype(f32))
    return o.astype(q.dtype), S_fin.astype(state.dtype)

def conv_ffn(x, buf, w_up, w_conv, b_conv, w_down):
    L = x.shape[1]
    u, g = jnp.split(x @ w_up, 2, axis=-1)
    gp = jnp.concatenate([buf.astype(g.dtype), g], axis=1)
    gc = b_conv + gp[:, 0:L] * w_conv[0]
    for j in range(1, CONV_W):
        gc = gc + gp[:, j:j + L] * w_conv[j]
    out = (jax.nn.gelu(gc, approximate=True) * u) @ w_down
    return out, gp[:, -CONV_BUF:]

def decoder_layer(x, p, pool_buf, gla_state, conv_buf, start,
                  g_pre_mix, w_in, w_gk2, b_gk2, w_pool, pool_scale, gla_norm, w_o,
                  g_post_mix, g_pre_ffn, w_up, w_conv, b_conv, w_down, g_post_ffn,
                  w_ple, w_ple_gate):
    h = rmsnorm(x, g_pre_mix)
    z, q, k, v, glow, og = jnp.split(h @ w_in, SPLIT_IDX, axis=-1)
    gk = jax.nn.log_sigmoid((glow @ w_gk2 + b_gk2).astype(jnp.float32)) / GLA_GATE_NORMALIZER
    pool_out, pool_new = pool_mixer(z, pool_buf, start, w_pool, pool_scale)
    gla_out, gla_new = gla_mixer(q, k, v, gk, og, gla_state, gla_norm)
    mix = jnp.concatenate([pool_out.astype(x.dtype), gla_out.astype(x.dtype)], axis=-1) @ w_o
    x = x + rmsnorm(mix, g_post_mix)
    f, conv_new = conv_ffn(rmsnorm(x, g_pre_ffn), conv_buf, w_up, w_conv, b_conv, w_down)
    x = x + rmsnorm(f, g_post_ffn)
    x = x + (p.astype(x.dtype) @ w_ple) * jax.nn.sigmoid(x @ w_ple_gate)
    return x, pool_new, gla_new, conv_new

def setup_inputs(seed: int = 0) -> dict:
    key = jax.random.key(seed)
    ks = list(jax.random.split(key, 32))
    ctr = [0]

    def nrm(shape, scale):
        kk = ks[ctr[0]]
        ctr[0] += 1
        return jax.random.normal(kk, shape, jnp.float32) * scale

    def gain(shape):
        return 1.0 + nrm(shape, 0.02)

    Ld = (DEPTH,)
    return {
        "x_prompt": nrm((BATCH, SEQ, D_MODEL), 1.0),
        "x_sample": nrm((DEC_BATCH, DEC_SEQ, D_MODEL), 1.0),
        "state_pool": nrm(Ld + (DEC_BATCH, POOL_BUF, POOL_WIDTH), 1.0),
        "state_gla": nrm(Ld + (DEC_BATCH, GLA_HEADS, GLA_HEAD_K, GLA_HEAD_V), 1.0),
        "state_conv": nrm(Ld + (DEC_BATCH, CONV_BUF, D_FF), 1.0),
        "p_prompt": nrm(Ld + (BATCH, SEQ, PLE_DIM), 1.0),
        "p_sample": nrm(Ld + (DEC_BATCH, DEC_SEQ, PLE_DIM), 1.0),
        "g_pre_mix": gain(Ld + (D_MODEL,)),
        "w_in": nrm(Ld + (D_MODEL, IN_PROJ_DIM), D_MODEL ** -0.5),
        "w_gk2": nrm(Ld + (GLA_GATE_RANK, GLA_KDIM), GLA_GATE_RANK ** -0.5),
        "b_gk2": nrm(Ld + (GLA_KDIM,), 0.02),
        "w_pool": nrm(Ld + (POOL_GROUPS, POOL_GROUP_DIM, POOL_GROUP_DIM), POOL_GROUP_DIM ** -0.5),
        "pool_scale": gain(Ld + (POOL_WIDTH,)),
        "gla_norm": gain(Ld + (GLA_HEAD_V,)),
        "w_o": nrm(Ld + (MIX_WIDTH, D_MODEL), MIX_WIDTH ** -0.5),
        "g_post_mix": gain(Ld + (D_MODEL,)),
        "g_pre_ffn": gain(Ld + (D_MODEL,)),
        "w_up": nrm(Ld + (D_MODEL, 2 * D_FF), D_MODEL ** -0.5),
        "w_conv": nrm(Ld + (CONV_W, D_FF), CONV_W ** -0.5),
        "b_conv": nrm(Ld + (D_FF,), 0.02),
        "w_down": nrm(Ld + (D_FF, D_MODEL), D_FF ** -0.5),
        "g_post_ffn": gain(Ld + (D_MODEL,)),
        "w_ple": nrm(Ld + (PLE_DIM, D_MODEL), PLE_DIM ** -0.5),
        "w_ple_gate": nrm(Ld + (D_MODEL, D_MODEL), D_MODEL ** -0.5),
    }

def reference(x_prompt, x_sample, state_pool, state_gla, state_conv, p_prompt, p_sample,
              g_pre_mix, w_in, w_gk2, b_gk2, w_pool, pool_scale, gla_norm, w_o,
              g_post_mix, g_pre_ffn, w_up, w_conv, b_conv, w_down, g_post_ffn,
              w_ple, w_ple_gate):
    y_p = x_prompt
    y_s = x_sample
    pool_p, gla_p, conv_p = [], [], []
    pool_s, gla_s, conv_s = [], [], []
    for i in range(DEPTH):
        lw = (g_pre_mix[i], w_in[i], w_gk2[i], b_gk2[i], w_pool[i], pool_scale[i], gla_norm[i],
              w_o[i], g_post_mix[i], g_pre_ffn[i], w_up[i], w_conv[i], b_conv[i], w_down[i],
              g_post_ffn[i], w_ple[i], w_ple_gate[i])
        zp_pool = jnp.zeros((x_prompt.shape[0], POOL_BUF, POOL_WIDTH), x_prompt.dtype)
        zp_gla = jnp.zeros((x_prompt.shape[0], GLA_HEADS, GLA_HEAD_K, GLA_HEAD_V), state_gla.dtype)
        zp_conv = jnp.zeros((x_prompt.shape[0], CONV_BUF, D_FF), x_prompt.dtype)
        y_p, a, b, c = decoder_layer(y_p, p_prompt[i], zp_pool, zp_gla, zp_conv, 0, *lw)
        pool_p.append(a)
        gla_p.append(b)
        conv_p.append(c)
        y_s, a, b, c = decoder_layer(y_s, p_sample[i], state_pool[i], state_gla[i], state_conv[i],
                                     PAST_LEN, *lw)
        pool_s.append(a)
        gla_s.append(b)
        conv_s.append(c)
    return (y_p, y_s,
            jnp.stack(pool_p), jnp.stack(gla_p), jnp.stack(conv_p),
            jnp.stack(pool_s), jnp.stack(gla_s), jnp.stack(conv_s))


_drawn_inputs = setup_inputs


def setup_inputs(seed=0):
    import zlib

    import numpy as np

    out = dict(_drawn_inputs(seed))
    spreads = {}
    factors = {'b_gk2': 6.265,
     'pool_scale': 4.401,
     'gla_norm': 6.177,
     'g_post_mix': 3.602,
     'g_pre_ffn': 2.809,
     'b_conv': 5.246,
     'g_post_ffn': 4.94}
    for name, (base, spread) in spreads.items():
        noise = np.random.default_rng([zlib.crc32(name.encode()), seed]).standard_normal(out[name].shape)
        drawn = base * np.exp(spread * noise) if base else spread * noise
        out[name] = __import__('jax').numpy.asarray(drawn.astype(out[name].dtype))
    for name, factor in factors.items():
        out[name] = (out[name] * factor).astype(out[name].dtype)
    return out
```

```python
from contextlib import ExitStack

import concourse.bass as bass
from concourse import mybir

F32 = mybir.dt.float32
F32R = mybir.dt.float32r
U8 = mybir.dt.uint8
ALU = mybir.AluOpType
ACT = mybir.ActivationFunctionType

P = 128
D = 1024
KD = D // P
SEQ, NSEQ, SLEN = 2048, 8, 8
TILES = 4
TOK = SEQ // TILES
HP = TOK // 2
HALF = HP + SLEN
T = 2 * HALF
NG = 4
POOLW, POOLG, HIST = 512, 4, 15
WINDOWS = (2, 4, 8, 16)
HEADS, KDIM, VDIM = 4, 64, 128
RANK = 16
FF = 2816
NF = FF // P
PLE = 256
EPS = 1e-6
GATE_NORM = 16.0
ZS = 16 + TOK
ZW = ZS + 2 * 24
LEVELS = (64, 32, 16, 8, 4, 2, 1)

W_IN_COLS = ([768, 896] + [512, 640] + [1024 + P * j for j in range(4)] + [P * j for j in range(4)]
             + [1552 + P * j for j in range(4)])
GLOW_COL = 1536
U_IN, U_O, U_UP, U_DOWN, U_PLE, U_GATE, UNITS = 0, 16, 24, 68, 92, 94, 102
DOWN_PARTS = ((0, 8), (8, 7), (15, 7))
TICKS = 108
OUTS = 92
O_IN, O_O, O_UP, O_DOWN, O_PLE, O_GATE = 0, 16, 24, 68, 76, 84


def tick_of(unit):
    if unit < U_PLE:
        return unit
    if unit < U_GATE:
        return U_PLE + 4 * (unit - U_PLE) + 3
    return unit + 6


class Steps:

    def __init__(self, sem, names):
        self.sem, self.names, self.next = sem, list(names), 0
        assert len(set(self.names)) == len(self.names)

    def did(self, instruction, name):
        assert self.names[self.next] == name, (self.names[self.next], name)
        self.next += 1
        instruction.then_inc(self.sem, 1)

    def at(self, i, name):
        return (i + 1) * len(self.names) + self.names.index(name) + 1

    def before(self, i, name):
        return i * len(self.names) + self.names.index(name) + 1


def staggered(*kinds, n=KD):
    return [f"{kind}{s - d}" for s in range(n + len(kinds) - 1) for d, kind in enumerate(kinds)
            if 0 <= s - d < n]


PE_STEPS = (
    [f"x_turned{g}" for g in range(5)]
    + ["states_turned", "sum_pre_mix", "glow", "gk0", "gk1", "diag", "scores64", "scores32", "scores16",
       "scores8", "scores4", "small4", "scores2", "small2", "scores1", "small1", "kd_turned",
       "kd_small_turned", "v_turned0", "v_turned1", "v_small_turned", "out0", "out1", "out2", "pool0",
       "out3", "pool1", "out_small", "state_small", "pool2", "pool3", "head0", "head1", "head2", "head3",
       "pool_state_turned", "sum_post_mix", "sum_pre_ffn", "p_turned01", "p_turned23",
       "p_turned_small", "conv_state_turned", "sum_post_ffn"]
)
ACT_STEPS = (
    [f"x_turned{g}" for g in range(5)] + ["conv_state", "rms_pre_mix"] + [f"h_hi{m}" for m in range(KD)]
    + ["glow", "gk_abs", "gk_exp", "gk_log"] + [f"decay{h}" for h in LEVELS]
    + ["kd_decay", "cum_decay", "kd_copied", "kd_small", "v_copied0", "v_copied1", "v_small",
       "out0", "out1", "silu", "u_hi0", "u_hi1", "out2", "mix_hi0", "u_hi2", "out3", "mix_hi1", "u_hi3",
       "out_small", "mix_hi2", "mix_hi3", "out_squares", "rms_head0", "rms_head1", "rms_head2", "rms_head3"]
    + [f"mix_hi{4 + h}" for h in range(HEADS)]
    + ["pool_state", "rms_post_mix", "rms_pre_ffn"] + [f"f_hi{m}" for m in range(KD)]
    + ["p_hi01", "p_hi23", "p_hi_small", "conv_out", "rms_post_ffn"] + [f"x_hi{m}" for m in range(KD)]
)
VEC_STEPS = (
    ["states", "zeros_pre_mix"] + staggered("h", "h_lo")
    + ["gk_min", "gk", "cumsum0", "cumsum1", "qk", "gap64", "operand64",
       "gap32", "scores_diag", "scores_small_diag", "scores64", "operand32",
       "gap16", "scores32", "operand16", "gap8", "scores16", "operand8", "gap4", "scores8", "operand4",
       "gap2", "scores4", "small4", "operand2", "gap1", "scores2", "small2", "operand1",
       "kd_gap", "scores1", "small1", "kd", "qb", "state0", "state1", "edges_scaled", "u_early",
       "u0", "u1", "u2", "u3", "u_lo0", "u_lo1", "state2", "mix_lo0", "u_lo2", "state3", "mix_lo1", "u_lo3",
       "state_small", "mix_lo2", "mix_lo3"]
    + [f"out_scaled{h}" for h in range(HEADS)] + staggered("out_gated", "mix_lo_head", n=HEADS)
    + ["zeros_mix", "zeros_pre_ffn"] + staggered("mixed", "x_mixed") + staggered("f", "f_lo")
    + ["p_lo01", "p_lo23", "p_lo_small", "zeros_ffn"] + staggered("ffn", "x_ffn", "x_lo")
)
POOL_STEPS = ["window2", "window4", "window8", "window16", "z_tail", "z_history", "z_edges"]
CONSTANTS = 14
BUILT = 3 + 4 * len(LEVELS) + 7 + 1 + 4 + (1 + 3 + 7 + 15) + 3 + 2
CHAIN = 8
SQUARES = 32


def hybrid_layer(nc, x_prompt, x_sample, state_pool, state_gla, state_conv, p_prompt, p_sample,
                 g_pre_mix, w_in, w_gk2, b_gk2, w_pool, pool_scale, gla_norm, w_o, g_post_mix,
                 g_pre_ffn, w_up, w_conv, b_conv, w_down, g_post_ffn, w_ple, w_ple_gate,
                 y_prompt, y_sample, pool_prompt, gla_prompt, conv_prompt, pool_sample, gla_sample,
                 conv_sample):
    ctx = ExitStack()
    with ctx:
        base = [nc.sbuf_base + 31 & ~31]
        top = nc.sbuf_usable_end

        def at(name, shape, dtype, offset):
            return nc.alloc_sbuf_tensor_at(name, shape, dtype, offset=offset)

        def own(name, shape, dtype=F32):
            n = mybir.dt.size(dtype)
            for s in shape[1:]:
                n *= s
            o = base[0]
            base[0] = (o + n + 31) // 32 * 32
            assert base[0] <= top, (name, base[0], top)
            return at(name, shape, dtype, o)

        def region(words):
            o = base[0]
            base[0] += 4 * words
            assert base[0] <= top, (base[0], top)
            return o

        def placed(start, name, shape, dtype, cursor):
            n = 1
            for s in shape[1:]:
                n *= s
            t = at(name, shape, dtype, start + 4 * cursor[0])
            cursor[0] += (n + 7) // 8 * 8
            return t

        ident = own("ident", [P, P])
        ones = own("ones", [P, P])
        masks = own("masks", [P, len(LEVELS), 64], U8)
        keep = own("keep", [P, T])
        gains = own("gains", [P, 4, KD])
        bias_gk = own("bias_gk", [P, 2])
        scale_pool = own("scale_pool", [P, POOLG])
        gain_head = own("gain_head", [P, 1])
        taps = own("taps", [P, 3, NF])
        bias_conv = own("bias_conv", [P, NF])
        eps = own("eps", [P, 1])
        edge = own("edge", [P, POOLG, 16])
        w_gk = own("w_gk", [RANK, 2 * P])
        w_glow_hi = own("w_glow_hi", [P, KD * RANK + P], F32R)
        w_glow_lo = own("w_glow_lo", [P, KD * RANK + P], F32R)
        w_pool_hi = own("w_pool_hi", [P, POOLG, P], F32R)
        w_pool_lo = own("w_pool_lo", [P, POOLG, P], F32R)
        z_past = own("z_past", [P, POOLG, 16])
        g_past = own("g_past", [P, 2, NF])
        g_state = own("g_state", [P, 2, 2, NF])
        g_tail = own("g_tail", [P, 2, 2, NF])
        S = own("S", [P, 2, P])
        S_s = own("S_s", [P, 2, 2, P])
        z_state = own("z_state", [P, 2 * HIST * POOLG])
        started = own("started", [1, 32])
        turned = own("turned", [P, 2, P])
        norm_at = region(2 * T + T)
        squares = at("squares", [P, 2, T], F32, norm_at)
        rms = at("rms", [P, T], F32, norm_at + 4 * 2 * T)
        p_tok = at("p_tok", [P, NG, PLE], F32, norm_at)
        p_small = at("p_small", [16, PLE], F32, norm_at + 4 * 2 * T)
        total = own("total", [P, T])
        xT = own("xT", [P, KD, T])

        stage = [own(f"stage{s}", [P, KD, P]) for s in range(2)]
        w_hi = [own(f"w_hi{s}", [P, KD, P], F32R) for s in range(2)]
        w_lo = [own(f"w_lo{s}", [P, KD, P], F32R) for s in range(2)]

        h_at = region(2 * KD * T)
        h_hi = at("h_hi", [P, KD, T], F32R, h_at)
        h_lo = at("h_lo", [P, KD, T], F32R, h_at + 4 * KD * T)
        ffn_out = at("ffn_out", [P, KD, T], F32, h_at)

        scratch = region(3648)
        c = [0]
        A = placed(scratch, "A", [P, 16, P], F32, c)
        A_s = placed(scratch, "A_s", [SLEN, 8, SLEN], F32, c)
        kd_tok = placed(scratch, "kd_tok", [P, NG, 2, P], F32, c)
        kd_small = placed(scratch, "kd_small", [SLEN, 2, 2 * P], F32, c)
        assert c[0] <= 3648, c
        c = [0]
        gx = placed(scratch, "gx", [P, 2, 268], F32, c)
        cg = placed(scratch, "cg", [P, 2, 266], F32, c)
        yf = placed(scratch, "yf", [P, T], F32, c)
        assert c[0] <= 1600
        normed = placed(scratch, "normed", [P, 2, T], F32, [1600])
        c = [0]
        p_lo = placed(scratch, "p_lo", [P, 2, T], F32R, c)
        p_hi = at("p_hi", [P, 2, T], F32R, scratch + 4 * 1600)

        big = region(2 * NF * T)
        y_hi = at("y_hi", [P, NF, T], F32R, big)
        y_lo = at("y_lo", [P, NF, T], F32R, big + 4 * NF * T)
        c = [0]
        kT = placed(big, "kT", [P, 2, T], F32, c)
        qT = placed(big, "qT", [P, 2, T], F32, c)
        vT = placed(big, "vT", [P, HEADS, T], F32, c)
        ogT = placed(big, "ogT", [P, HEADS, T], F32, c)
        Z = placed(big, "Z", [P, POOLG, ZW], F32, c)
        win_a = placed(big, "win_a", [P, POOLG, ZW], F32, c)
        win_b = placed(big, "win_b", [P, POOLG, ZW], F32, c)
        u_hi = placed(big, "u_hi", [P, 2, T], F32R, c)
        u_lo = placed(big, "u_lo", [P, 2, T], F32R, c)
        cum = placed(big, "cum", [P, 2, T], F32, c)
        gap = placed(big, "gap", [P, 2, T], F32, c)
        opnd = [placed(big, f"opnd{n}", [P, 2, T], F32, c) for n in range(2)]
        v_tok = placed(big, "v_tok", [P, NG, HEADS * P], F32, c)
        v_small = placed(big, "v_small", [SLEN, 2, HEADS * P], F32, c)
        assert c[0] <= 2 * NF * T, c
        outT = at("outT", [P, HEADS, T], F32, big + 4 * 2 * (2 * T))
        out_sq = at("out_sq", [P, HEADS, T], F32, big + 4 * (6 * 2 * T + 2 * POOLG * ZW // 2))
        mixed = at("mixed", [P, KD, T], F32, big)
        c = [0]
        x_tok = placed(big, "x_tok", [P, NG, D], F32, c)
        x_small = placed(big, "x_small", [16, D], F32, c)
        y_tok = placed(big, "y_tok", [P, NG, D], F32, c)
        y_small = placed(big, "y_small", [SLEN, 2, D], F32, c)
        ple = placed(big, "ple", [P, KD, T], F32, c)
        sig = placed(big, "sig", [P, 2, T], F32, c)
        z_state_tok = placed(big, "z_state_tok", [2 * HIST * POOLG, P], F32, c)
        g_state_tok = placed(big, "g_state_tok", [4 * NF, P], F32, c)
        assert c[0] <= 2 * NF * T, c
        raw_pool = at("raw_pool", [P, POOLG, P], F32, big)
        raw_glow = at("raw_glow", [P, KD, RANK], F32, big + 4 * 512)

        G = [ctx.enter_context(nc.psum_tensor(f"G{n}", [P, 2, 512], F32)) for n in range(2)]
        X = [ctx.enter_context(nc.psum_tensor(f"X{n}", [P, 2, 512], F32)) for n in range(2)]

        def halves(ps):
            return ps[:, :, 0:HALF]

        def split2(ap):
            return ap.rearrange("p (a c) -> p a c", a=2)

        def group_cols(c):
            return HALF * (c // 2) + P * (c % 2)

        def sem(name):
            return ctx.enter_context(nc.semaphore(name))

        constants_loaded = sem("constants_loaded")
        built = sem("built")
        split_once = sem("split_once")
        staged = [sem(f"staged{s}") for s in range(2)]
        hi_made = sem("hi_made")
        lo_made = sem("lo_made")
        ticks = sem("ticks")
        evacuated = [sem(f"evacuated{n}") for n in range(2)]
        squared = sem("squared")
        summed = sem("summed")
        x_loaded, states_loaded, s_loaded, p_loaded = sem("x_loaded"), sem("states_loaded"), sem("s_loaded"), sem("p_loaded")
        stored_y, stored_pool, stored_gla, stored_conv = sem("stored_y"), sem("stored_pool"), sem("stored_gla"), sem("stored_conv")
        gate_copied, past_in, past_mid = sem("gate_copied"), sem("past_in"), sem("past_mid")
        tap_now, tapped = sem("tap_now"), sem("tapped")
        gelu_made, hidden_hi, hidden_lo = sem("gelu_made"), sem("hidden_hi"), sem("hidden_lo")
        gated, added, y_turned, y_copied = sem("gated"), sem("added"), sem("y_turned"), sem("y_copied")
        last_turned, last_copied, last_packed = sem("last_turned"), sem("last_copied"), sem("last_packed")
        pe_s, act_s, vec_s, pool_s = sem("pe_steps"), sem("act_steps"), sem("vec_steps"), sem("pool_steps")
        pe_, act_, vec_, pool_ = (Steps(pe_s, PE_STEPS), Steps(act_s, ACT_STEPS),
                                  Steps(vec_s, VEC_STEPS), Steps(pool_s, POOL_STEPS))
        act_chain = sem("act_chain")
        passed = sem("passed")
        credited = sem("credited")

        def tick(i, n):
            return i * TICKS + (n + 3)

        def evac(i, o):
            return evacuated[o % 2], i * (OUTS // 2) + (o // 2 + 2)

        def level_view(t, h, side=None):
            w = HALF if h <= 4 else HP
            v = t[:, :, :].rearrange("p d (a c) -> p (d a) c", a=2)[:, :, 0:w]
            v = v.rearrange("p s (n w) -> p s n w", w=2 * h)
            return v if side is None else v[:, :, :, h * side:h * side + h]

        block = ctx.enter_context(nc.Block())

        @block.sync
        def _(sp):
            def rows(w, first, n, col):
                return w[first:first + P * n, col].rearrange("(k p) c -> p k c", p=P)

            def load_unit(i, n, src, parts=KD):
                sp.wait_ge(lo_made, i * UNITS + (n + 1))
                sp.sem_inc(passed, 1)
                sp.dma_start(stage[n_mod(n)][:, 0:parts, :], src).then_inc(staged[n_mod(n)], 16)

            def n_mod(n):
                return n % 2 if isinstance(n, int) else n_parity[0]

            n_parity = [0]

            n = [0]

            def constant(dst, src):
                sp.dma_start(dst, src).then_inc(constants_loaded, 16)
                n[0] += 16

            with nc.allow_non_contiguous_dma(reason="small vectors, once"):
                constant(raw_glow[:, :, :], rows(w_in[0], 0, KD, slice(GLOW_COL, GLOW_COL + RANK)))
                constant(raw_pool[:, :, :], w_pool[0].rearrange("g c d -> c g d"))
                constant(w_gk[:, :], w_gk2[0])
                for m, g in enumerate((g_pre_mix, g_post_mix, g_pre_ffn, g_post_ffn)):
                    constant(gains[:, m, :], g[0].rearrange("(k p) -> p k", p=P))
                constant(bias_gk[:, :], b_gk2[0].rearrange("(k p) -> p k", p=P))
                constant(scale_pool[:, :], pool_scale[0].rearrange("(k p) -> p k", p=P))
                constant(gain_head[:, :], gla_norm[0].rearrange("(k p) -> p k", p=P))
                for m in range(3):
                    constant(taps[:, m, :], w_conv[0, m].rearrange("(k p) -> p k", p=P))
                constant(bias_conv[:, :], b_conv[0].rearrange("(k p) -> p k", p=P))
            assert n[0] == 16 * CONSTANTS
            load_unit(0, 0, rows(w_in[0], 0, KD, slice(W_IN_COLS[0], W_IN_COLS[0] + P)))

            with sp.Fori(0, TILES) as i:
                sp.wait_ge(split_once, 4)
                sp.wait_ge(y_copied, i * 8 + 8)
                xp = x_prompt[0, bass.ds(i * TOK, TOK), :].rearrange("(g p) d -> p g d", p=P)
                sp.dma_start(x_tok[:, :, :], xp).then_inc(x_loaded, 16)
                xs = x_sample.rearrange("b s d -> (b s) d")[bass.ds(i * 16, 16), :]
                sp.dma_start(x_small[:, :], xs).then_inc(x_loaded, 16)
                zs = state_pool[0].rearrange("b t (g c) -> (b t g) c", g=POOLG)
                sp.dma_start(z_state_tok[:, :], zs[bass.ds(i * 120, 120), :]).then_inc(states_loaded, 16)
                gs = state_conv[0].rearrange("b t (f c) -> (b t f) c", f=NF)
                sp.dma_start(g_state_tok[:, :], gs[bass.ds(i * 88, 88), :]).then_inc(states_loaded, 16)
                sp.wait_ge(stored_gla, i * 16 + 16)
                sg = state_gla[0].rearrange("b (d h) k v -> (h k) b d v", h=2)
                sp.dma_start(S_s[:, :, :, :], sg[:, bass.ds(i * 2, 2), :, :]).then_inc(s_loaded, 16)

                for m in range(1, 16):
                    load_unit(i, m, rows(w_in[0], 0, KD, slice(W_IN_COLS[m], W_IN_COLS[m] + P)))
                with sp.Fori(0, KD // 2) as j:
                    for r in range(2):
                        n_parity[0] = r
                        load_unit(i, j * 2 + (U_O + r), rows(w_o[0], 0, KD, bass.ds(j * 2 * P + r * P, P)))
                sp.wait_ge(act_s, act_.at(i, "pool_state"))
                sp.dma_start(pool_sample[0].rearrange("b t (g c) -> (b t g) c", g=POOLG)
                             [bass.ds(i * 120, 120), :], turned[0:120, 0, :]).then_inc(stored_pool, 16)
                sp.wait_ge(vec_s, vec_.at(i, "state_small"))
                so = gla_sample[0].rearrange("b (d h) k v -> (h k) b d v", h=2)
                sp.dma_start(so[:, bass.ds(i * 2, 2), :, :], S_s[:, :, :, :]).then_inc(stored_gla, 16)
                for r in range(2):
                    load_unit(i, U_UP + r, rows(w_up[0], 0, KD, slice(FF * (1 - r), FF * (1 - r) + P)))
                sp.wait_ge(vec_s, vec_.at(i, f"f{KD - 1}"))
                pp = p_prompt[0, 0, bass.ds(i * TOK, TOK), :].rearrange("(g p) d -> p g d", p=P)
                sp.dma_start(p_tok[:, :, :], pp).then_inc(p_loaded, 16)
                ps = p_sample[0].rearrange("b s d -> (b s) d")[bass.ds(i * 16, 16), :]
                sp.dma_start(p_small[:, :], ps).then_inc(p_loaded, 16)
                with sp.Fori(1, NF) as f:
                    for r in range(2):
                        n_parity[0] = r
                        load_unit(i, f * 2 + (U_UP + r), rows(w_up[0], 0, KD, bass.ds(f * P + FF * (1 - r), P)))
                with sp.Fori(0, KD // 2) as j:
                    for r in range(6):
                        n_parity[0] = r % 2
                        first, parts = DOWN_PARTS[r % 3]
                        load_unit(i, j * 6 + (U_DOWN + r),
                                  rows(w_down[0], first * P, parts, bass.ds(j * 2 * P + r // 3 * P, P)), parts)
                sp.wait_ge(act_s, act_.at(i, "conv_out"))
                sp.dma_start(conv_sample[0].rearrange("b t (f c) -> (b t f) c", f=NF)
                             [bass.ds(i * 88, 88), :], turned[0:88, 1, :]).then_inc(stored_conv, 16)
                for m in range(2):
                    sp.wait_ge(lo_made, i * UNITS + (U_PLE + m + 1))
                    dst = stage[m][:, :, :].rearrange("p (k c) d -> p k (c d)", k=2)
                    sp.dma_start(dst, w_ple[0, :, 512 * m:512 * m + 512].rearrange("(k p) c -> p k c", p=P))\
                      .then_inc(staged[m], 16)
                with sp.Fori(0, KD // 2) as j:
                    for r in range(2):
                        n_parity[0] = r
                        load_unit(i, j * 2 + (U_GATE + r), rows(w_ple_gate[0], 0, KD, bass.ds(j * 2 * P + r * P, P)))
                load_unit(i, UNITS, rows(w_in[0], 0, KD, slice(W_IN_COLS[0], W_IN_COLS[0] + P)))
                sp.wait_ge(y_copied, i * 8 + 16)
                yp = y_prompt[0, bass.ds(i * TOK, TOK), :].rearrange("(g p) d -> p g d", p=P)
                sp.dma_start(yp, y_tok[:, :, :]).then_inc(stored_y, 16)
                ys = y_sample.rearrange("b s d -> s b d")[:, bass.ds(i * 2, 2), :]
                sp.dma_start(ys, y_small[:, :, :]).then_inc(stored_y, 16)

            sp.wait_ge(vec_s, vec_.at(TILES - 1, "state3"))
            sp.dma_start(gla_prompt[0, 0].rearrange("(d h) k v -> (h k) d v", h=2), S[:, :, :]).then_inc(stored_gla, 16)
            sp.wait_ge(last_copied, 1)
            sp.dma_start(pool_prompt[0, 0].rearrange("t (g c) -> (t g) c", g=POOLG),
                         turned[0:60, 0, :]).then_inc(stored_pool, 16)
            sp.wait_ge(last_copied, 2)
            sp.dma_start(conv_prompt[0, 0].rearrange("t (f c) -> (t f) c", f=NF),
                         turned[0:44, 1, :]).then_inc(stored_conv, 16)
            sp.wait_ge(stored_y, TILES * 32 + 32)
            sp.wait_ge(stored_pool, TILES * 16 + 32)
            sp.wait_ge(stored_gla, TILES * 16 + 32)
            sp.wait_ge(stored_conv, TILES * 16 + 32)

        @block.gpsimd
        def _(pool):
            n = [0]

            def build(instruction):
                n[0] += 1
                instruction.then_inc(built, 1)
                pool.wait_ge(built, n[0])

            build(pool.memset(ones[:, :], 1.0))
            build(pool.memset(ident[:, :], 0.0))
            build(pool.affine_select(out=ident[:, :], in_=ident[:, :], compare_op=ALU.not_equal, fill=1.0,
                                     base=0, pattern=[[-1, P]], channel_multiplier=1))
            sel = total
            for n_level, h in enumerate(LEVELS):
                m = sel[:, 0:64].rearrange("p (n h) -> p n h", h=h)
                build(pool.memset(sel[:, 0:64], 1.0))
                build(pool.affine_select(out=m, in_=m, compare_op=ALU.is_ge, fill=0.0, base=0,
                                         pattern=[[-2 * h, 64 // h], [0, h]], channel_multiplier=1))
                build(pool.affine_select(out=m, in_=m, compare_op=ALU.is_ge, fill=0.0, base=h - 1,
                                         pattern=[[2 * h, 64 // h], [0, h]], channel_multiplier=-1))
                build(pool.tensor_copy(masks[:, n_level, :], sel[:, 0:64]))
            build(pool.memset(keep[:, :], 1.0))
            for a in range(2):
                for first in (0, P, HP):
                    build(pool.memset(keep[:, a * HALF + first:a * HALF + first + 1], 0.0))
            build(pool.memset(eps[:, :], EPS))
            for g, w in enumerate(WINDOWS):
                build(pool.memset(edge[:, g, :], 1.0 / w))
                for t in range(w - 1):
                    build(pool.memset(edge[:, g, t:t + 1], 1.0 / (t + 1)))
            build(pool.memset(z_past[:, :, :], 0.0))
            build(pool.memset(g_past[:, :, :], 0.0))
            build(pool.memset(S[:, :, :], 0.0))
            for w in (w_glow_hi, w_glow_lo):
                build(pool.memset(w[:, P:2 * P].bitcast(F32), 0.0))
            assert n[0] == BUILT, n

            with pool.Fori(0, TILES) as i:
                for o in (O_IN + 11, O_IN + 10):
                    pool.wait_ge(*evac(i, o))
                pool.wait_ge(vec_s, vec_.at(i, "states"))
                src, dst = Z, win_a
                for k, w in enumerate(WINDOWS):
                    if k:
                        pool.wait_ge(pool_s, pool_.at(i, f"window{WINDOWS[k - 1]}"))
                    pool_.did(pool.tensor_tensor(dst[:, k:, w - 1:], src[:, k:, w - 1:],
                                                 src[:, k:, w // 2 - 1:ZW - w // 2], ALU.add), f"window{w}")
                    src, dst = dst, (win_b if dst is win_a else win_a)
                tail = Z[:, :, ZS:].rearrange("p g (s t) -> p s t g", s=2)[:, :, 24 - HIST:, :]
                pool_.did(pool.tensor_copy(z_state[:, :].rearrange("p (s t g) -> p s t g", s=2, g=POOLG), tail),
                          "z_tail")
                pool_.did(pool.tensor_copy(z_past[:, :, 1:16], Z[:, :, ZS - HIST:ZS]), "z_history")
                pool.wait_ge(vec_s, vec_.at(i, "u_early"))
                pool.sem_inc(passed, 1)
                for g, w in enumerate(WINDOWS):
                    last = pool.memset(edge[:, g, :], 1.0 / w)
                pool_.did(last, "z_edges")

                pool.wait_ge(pe_s, pe_.at(i, "state_small"))
                pool.sem_inc(passed, 1)
                with pool.Fori(0, NF) as f:
                    pool.wait_ge(tapped, i * 2 * NF + f * 2 + 2)
                    pool.tensor_copy(gx[:, 0, 0:2], g_past[:, :, bass.ds(f, 1)].rearrange("p t o -> p (t o)"))
                    pool.tensor_copy(gx[:, :, 258:260], g_state[:, :, :, bass.ds(f, 1)]
                                     .rearrange("p s t o -> p s (t o)")).then_inc(past_in, 1)
                    pool.wait_ge(gate_copied, i * NF + f + 1)
                    pool.sem_inc(passed, 1)
                    pool.tensor_copy(gx[:, 1, 0:2], gx[:, 0, 256:258]).then_inc(past_mid, 1)
                    pool.wait_ge(past_in, i * NF + f + 1)
                    pool.sem_inc(passed, 1)
                    pool.tensor_copy(g_past[:, :, bass.ds(f, 1)].rearrange("p t o -> p (t o)"), gx[:, 1, 256:258])
                    pool.tensor_copy(g_tail[:, :, :, bass.ds(f, 1)].rearrange("p s t o -> p s (t o)"),
                                     gx[:, :, 266:268]).then_inc(past_mid, 1)

            pool.wait_ge(pool_s, pool_.at(TILES - 1, "z_edges"))
            pool.tensor_copy(z_state[:, 0:60].rearrange("p (t g) -> p t g", g=POOLG),
                             z_past[:, :, 1:16].rearrange("p g t -> p t g")).then_inc(last_packed, 1)

        @block.scalar
        def _(act):
            def mod2(n):
                return n % 2 if isinstance(n, int) else parity[0]

            parity = [0]

            def split(i, n, free, parts=KD):
                s = mod2(n)
                act.wait_ge(staged[s], i * (UNITS // 2 * 16) + stage_count(n))
                act.wait_ge(ticks, tick(i, free))
                act.activation(w_hi[s][:, 0:parts, :], stage[s][:, 0:parts, :], ACT.Copy).then_inc(hi_made, 1)

            def stage_count(n):
                return (n // 2 + 1) * 16 if isinstance(n, int) else half_count[0]

            half_count = [0]

            def root(x, name, width=D):
                act.activation(rms[:, :].rearrange("p (a c) -> p a c", a=2), halves(x), ACT.Ln,
                               scale=1.0 / width, bias=eps[:, 0:1]).then_inc(act_chain, 1)
                link[0] += 1
                act.wait_ge(act_chain, chained())
                act_.did(act.activation(rms[:, :], rms[:, :], ACT.Exp, scale=-0.5), name)

            link = [0]

            def chained():
                return tile[0] * CHAIN + link[0]

            tile = [0]

            def square(src, i, n):
                act.wait_ge(summed, i * SQUARES + (n + 1))
                dst = squares[:, n % 2 if isinstance(n, int) else parity[0], :]
                act.activation(dst if len(src.shape) == 2 else split2(dst), src, ACT.Square).then_inc(squared, 1)

            act.wait_ge(constants_loaded, 16 * CONSTANTS)
            act.activation(w_pool_hi[:, :, :], raw_pool[:, :, :], ACT.Copy).then_inc(split_once, 1)
            act.activation(w_glow_hi[:, 0:P], raw_glow[:, :, :].rearrange("p k c -> p (k c)"), ACT.Copy)\
               .then_inc(split_once, 1)
            act.wait_ge(credited, 1)
            act.wait_ge(built, BUILT)
            act.wait_ge(staged[0], 16)
            act.activation(w_hi[0][:, :, :], stage[0][:, :, :], ACT.Copy).then_inc(hi_made, 1)

            with act.Fori(0, TILES) as i:
                tile[0], link[0] = i, 0
                for g in range(NG):
                    act.wait_ge(pe_s, pe_.at(i, f"x_turned{g}"))
                    act_.did(act.activation(xT[:, :, group_cols(g):group_cols(g) + P],
                                            X[g % 2][:, :, :].rearrange("p b (k c) -> p (b k) c", c=P), ACT.Copy),
                             f"x_turned{g}")
                act.wait_ge(pe_s, pe_.at(i, "x_turned4"))
                act_.did(act.activation(xT[:, :, :].rearrange("p k (a c) -> p k a c", a=2)[:, :, :, HP:],
                                        X[0][:, 0, 0:P].rearrange("p (k a c) -> p k a c", k=KD, a=2), ACT.Copy),
                         "x_turned4")
                act.wait_ge(pe_s, pe_.at(i, "states_turned"))
                act_.did(act.activation(g_state[:, :, :, :].rearrange("p s t f -> p (s t f)"),
                                        X[1][:, 1, 0:4 * NF], ACT.Copy), "conv_state")
                act.wait_ge(act_s, act_.at(i, "conv_state"))
                for m in range(KD):
                    square(xT[:, m, :], i, m)
                act.wait_ge(pe_s, pe_.at(i, "sum_pre_mix"))
                root(X[0], "rms_pre_mix")
                act.wait_ge(ticks, tick(i, -1))
                for m in range(KD):
                    act.wait_ge(vec_s, vec_.at(i, f"h{m}"))
                    act_.did(act.activation(h_hi[:, m, :], normed[:, m % 2, :], ACT.Copy), f"h_hi{m}")

                act.wait_ge(pe_s, pe_.at(i, "glow"))
                act_.did(act.activation(squares[0:RANK, 0, :].rearrange("p (a c) -> p a c", a=2),
                                        halves(X[1])[0:RANK], ACT.Copy), "glow")

                def extras(s):
                    if s == 1:
                        for d in range(2):
                            act.wait_ge(pe_s, pe_.at(i, f"gk{d}"))
                            last = act.activation(split2(opnd[0][:, d, :]), halves(X[d]), ACT.Abs,
                                                  bias=bias_gk[:, d:d + 1])
                        act_.did(last, "gk_abs")
                        act.wait_ge(act_s, act_.at(i, "gk_abs"))
                        act_.did(act.activation(opnd[0][:, :, :], opnd[0][:, :, :], ACT.Exp, scale=-1.0), "gk_exp")
                        act.wait_ge(act_s, act_.at(i, "gk_exp"))
                        act_.did(act.activation(opnd[0][:, :, :], opnd[0][:, :, :], ACT.Ln, bias=1.0), "gk_log")
                    if 4 <= s <= 10:
                        h = LEVELS[s - 4]
                        act.wait_ge(vec_s, vec_.at(i, f"gap{h}"))
                        v = level_view(gap, h)
                        act.activation(v[:, :, :, 0:h], v[:, :, :, 0:h], ACT.Exp, scale=-1.0 / GATE_NORM)
                        act_.did(act.activation(v[:, :, :, h:], v[:, :, :, h:], ACT.Exp, scale=1.0 / GATE_NORM),
                                 f"decay{h}")
                    if s == 11:
                        act.wait_ge(vec_s, vec_.at(i, "kd_gap"))
                        act_.did(act.activation(gap[:, :, :], gap[:, :, :], ACT.Exp, scale=1.0 / GATE_NORM), "kd_decay")
                        act_.did(act.activation(cum[:, :, :], cum[:, :, :], ACT.Exp, scale=1.0 / GATE_NORM), "cum_decay")
                    if s == 12:
                        act.wait_ge(pe_s, pe_.at(i, "kd_turned"))
                        act_.did(act.activation(kd_tok[:, :, :, :].rearrange("p c d k -> p (c d k)"),
                                                X[1][:, :, :].rearrange("p b c -> p (b c)"), ACT.Copy), "kd_copied")
                        act.wait_ge(pe_s, pe_.at(i, "kd_small_turned"))
                        act_.did(act.activation(kd_small[:, :, :].rearrange("p a c -> p (a c)"), X[0][0:SLEN, 0, :],
                                                ACT.Copy), "kd_small")
                    if s == 13:
                        for n in range(2):
                            act.wait_ge(pe_s, pe_.at(i, f"v_turned{n}"))
                            act_.did(act.activation(v_tok[:, 2 * n:2 * n + 2, :], X[n][:, :, :], ACT.Copy), f"v_copied{n}")
                    if s == 14:
                        act.wait_ge(pe_s, pe_.at(i, "v_small_turned"))
                        act_.did(act.activation(v_small[:, :, :], X[0][0:SLEN, :, :], ACT.Copy), "v_small")
                        copy_out(0)
                    if s == 15:
                        copy_out(1)

                def copy_out(c):
                    act.wait_ge(pe_s, pe_.at(i, f"out{c}"))
                    act_.did(act.activation(outT[:, :, group_cols(c):group_cols(c) + P]
                                            .rearrange("p (d b) c -> p b d c", b=2),
                                            X[(c + 1) % 2][:, :, 0:2 * P].rearrange("p b (d c) -> p b d c", c=P),
                                            ACT.Copy), f"out{c}")

                def u_split(g):
                    act.wait_ge(vec_s, vec_.at(i, f"u{g}"))
                    if g >= 2:
                        act.wait_ge(pe_s, pe_.at(i, f"pool{g - 2}"))
                    w = win_a if g % 2 == 0 else win_b
                    act.activation(u_hi[:, g % 2, :].rearrange("p (a c) -> p a c", a=2)[:, :, 0:HP],
                                   w[:, g, 16:ZS].rearrange("p (a c) -> p a c", a=2), ACT.Copy)
                    act_.did(act.activation(u_hi[:, g % 2, :].rearrange("p (a c) -> p a c", a=2)[:, :, HP:],
                                            w[:, g, ZS:].rearrange("p (a c) -> p a c", a=2)[:, :, 16:], ACT.Copy),
                             f"u_hi{g}")

                def pool_split(g, x):
                    act.wait_ge(pe_s, pe_.at(i, f"pool{g}"))
                    act_.did(act.activation(split2(h_hi[:, g, :]), halves(X[x]), ACT.Copy,
                                            scale=scale_pool[:, g:g + 1]), f"mix_hi{g}")

                for m in range(16):
                    split(i, m + 1, tick_of(m - 1) if m else -1)
                    extras(m)
                    act.wait_ge(ticks, tick(i, m))
                    src = halves(G[m % 2])
                    if 8 <= m < 12:
                        g = m - 8
                        act.activation(Z[:, g, 16:ZS].rearrange("p (a c) -> p a c", a=2), src[:, :, 0:HP], ACT.Copy)
                        act.activation(Z[:, g, ZS:].rearrange("p (a c) -> p a c", a=2)[:, :, 16:],
                                       src[:, :, HP:], ACT.Copy).then_inc(evacuated[m % 2], 1)
                    else:
                        dst, at_, scale = ((kT, m, 1.0) if m < 2 else (qT, m - 2, KDIM ** -0.5) if m < 4
                                           else (vT, m - 4, 1.0) if m < 8 else (ogT, m - 12, 1.0))
                        act.activation(split2(dst[:, at_, :]), src, ACT.Copy, scale=scale)\
                           .then_inc(evacuated[m % 2], 1)
                for m in (14, 15):
                    act.wait_ge(*evac(i, m))
                act_.did(act.activation(ogT[:, :, :], ogT[:, :, :], ACT.Silu), "silu")
                u_split(0)
                u_split(1)
                copy_out(2)
                pool_split(0, 0)
                u_split(2)
                copy_out(3)
                pool_split(1, 1)
                u_split(3)
                act.wait_ge(pe_s, pe_.at(i, "out_small"))
                for b in range(2):
                    last = act.activation(outT[:, b:HEADS:2, :].rearrange("p d (a c) -> p d a c", a=2)[:, :, :, HP:],
                                          X[0][:, b, 0:32].rearrange("p (d a c) -> p d a c", d=2, a=2), ACT.Copy)
                act_.did(last, "out_small")
                pool_split(2, 0)
                pool_split(3, 1)
                act.wait_ge(act_s, act_.at(i, "out_small"))
                act_.did(act.activation(out_sq[:, :, :], outT[:, :, :], ACT.Square), "out_squares")
                for h in range(HEADS):
                    act.wait_ge(pe_s, pe_.at(i, f"head{h}"))
                    if h:
                        act.wait_ge(vec_s, vec_.at(i, f"out_scaled{h - 1}"))
                    root(X[h % 2], f"rms_head{h}", VDIM)
                for h in range(HEADS):
                    act.wait_ge(vec_s, vec_.at(i, f"out_gated{h}"))
                    act_.did(act.activation(h_hi[:, 4 + h, :], outT[:, h, :], ACT.Copy), f"mix_hi{4 + h}")
                act.wait_ge(pe_s, pe_.at(i, "pool_state_turned"))
                act.wait_ge(stored_pool, i * 16 + 16)
                act_.did(act.activation(turned[0:120, 0, :], X[0][0:120, 0, 0:P], ACT.Copy), "pool_state")

                with act.Fori(0, KD // 2) as j:
                    for r in range(2):
                        parity[0], half_count[0] = (r + 1) % 2, j * 16 + (U_O + r + 1) // 2 * 16 + 16
                        split(i, j * 2 + (U_O + r + 1), j * 2 + (U_O + r - 1))
                        act.wait_ge(ticks, tick(i, j * 2 + (U_O + r)))
                        parity[0] = r
                        square(halves(G[r]), i, j * 2 + (8 + r))
                        act.activation(split2(mixed[:, bass.ds(j * 2 + r, 1), :].rearrange("p o c -> p (o c)")),
                                       halves(G[r]), ACT.Copy).then_inc(evacuated[r], 1)
                act.wait_ge(pe_s, pe_.at(i, "sum_post_mix"))
                root(X[1], "rms_post_mix")
                for m in range(KD):
                    act.wait_ge(vec_s, vec_.at(i, f"x_mixed{m}"))
                    square(xT[:, m, :], i, 16 + m)
                act.wait_ge(pe_s, pe_.at(i, "sum_pre_ffn"))
                root(X[0], "rms_pre_ffn")
                for m in range(KD):
                    act.wait_ge(vec_s, vec_.at(i, f"f{m}"))
                    act_.did(act.activation(h_hi[:, m, :], normed[:, m % 2, :], ACT.Copy), f"f_hi{m}")

                with act.Fori(0, NF) as f:
                    parity[0], half_count[0] = 1, f * 16 + (U_UP + 1) // 2 * 16 + 16
                    split(i, f * 2 + (U_UP + 1), f * 2 + (U_UP - 1))
                    act.wait_ge(ticks, tick(i, f * 2 + U_UP))
                    act.wait_ge(tapped, i * (2 * NF) + f * 2 + 2)
                    act.wait_ge(past_mid, i * (2 * NF) + f * 2 + 2)
                    act.activation(gx[:, :, 2:258], G[0][:, :, 0:HP], ACT.Copy)
                    act.activation(gx[:, :, 260:268], G[0][:, :, HP:HALF], ACT.Copy).then_inc(gate_copied, 1)
                    act.wait_ge(gate_copied, i * NF + f + 1)
                    act.wait_ge(past_in, i * NF + f + 1)
                    act.activation(cg[:, :, :], gx[:, :, 2:268], ACT.Identity,
                                   scale=taps[:, 2, bass.ds(f, 1)], bias=bias_conv[:, bass.ds(f, 1)])\
                       .then_inc(evacuated[0], 1)
                    act.wait_ge(tapped, i * (2 * NF) + f * 2 + 4)
                    act.activation(cg[:, :, :], cg[:, :, :], ACT.Gelu_apprx_tanh).then_inc(gelu_made, 1)
                    parity[0], half_count[0] = 0, f * 16 + (U_UP + 2) // 2 * 16 + 16
                    split(i, f * 2 + (U_UP + 2), f * 2 + U_UP)
                    act.wait_ge(evacuated[1], i * (OUTS // 2) + f + ((O_UP + 1) // 2 + 2))
                    act.activation(y_hi[:, bass.ds(f, 1), :].rearrange("p o c -> p (o c)"), yf[:, :], ACT.Copy)\
                       .then_inc(hidden_hi, 1)

                def down(j, r):
                    n, parts = U_DOWN + r + 1, DOWN_PARTS[(r + 1) % 3][1]
                    parity[0], half_count[0] = n % 2, j * 48 + (n // 2 + 1) * 16
                    split(i, j * 6 + n, j * 6 + (U_DOWN + r - 1), parts)
                    if r % 3 == 2:
                        act.wait_ge(ticks, tick(i, j * 6 + (U_DOWN + r)))
                        parity[0] = r // 3
                        square(halves(G[r // 3]), i, j * 2 + (24 + r // 3))
                        act.activation(split2(ffn_out[:, bass.ds(j * 2 + r // 3, 1), :].rearrange("p o c -> p (o c)")),
                                       halves(G[r // 3]), ACT.Copy).then_inc(evacuated[r // 3], 1)

                def p_split(x, cols, name):
                    act.wait_ge(pe_s, pe_.at(i, f"p_turned{name}"))
                    for b in range(2):
                        last = act.activation(p_hi[:, :, cols[b]:cols[b] + P],
                                              X[x][:, b, 0:256].rearrange("p (k c) -> p k c", k=2), ACT.Copy)
                    act_.did(last, f"p_hi{name}")

                p_split(0, (group_cols(0), group_cols(1)), "01")
                p_split(1, (group_cols(2), group_cols(3)), "23")
                act.wait_ge(pe_s, pe_.at(i, "p_turned_small"))
                act_.did(act.activation(p_hi[:, :, :].rearrange("p k (a c) -> p k a c", a=2)[:, :, :, HP:],
                                        X[0][:, 0, 0:32].rearrange("p (k a c) -> p k a c", k=2, a=2), ACT.Copy),
                         "p_hi_small")
                act.wait_ge(pe_s, pe_.at(i, "conv_state_turned"))
                act.wait_ge(stored_conv, i * 16 + 16)
                act_.did(act.activation(turned[0:88, 1, :], X[1][0:88, 0, 0:P], ACT.Copy), "conv_out")
                with act.Fori(0, KD // 2) as j:
                    for r in range(6):
                        down(j, r)

                act.wait_ge(pe_s, pe_.at(i, "sum_post_ffn"))
                root(X[0], "rms_post_ffn")

                def copy_ple(m):
                    act.wait_ge(ticks, tick(i, U_PLE + m))
                    act.activation(split2(ple[:, m, :]), halves(G[m % 2]), ACT.Copy).then_inc(evacuated[m % 2], 1)

                def x_split(m):
                    act.wait_ge(vec_s, vec_.at(i, f"x_ffn{m}"))
                    act_.did(act.activation(h_hi[:, m, :], xT[:, m, :], ACT.Copy), f"x_hi{m}")

                split(i, U_PLE + 1, tick_of(U_PLE - 1))
                for m in range(KD):
                    copy_ple(m)
                    if m == 4:
                        split(i, U_GATE, tick_of(U_PLE))
                for m in range(KD):
                    x_split(m)

                def gate(j, r):
                    n = U_GATE + r + 1
                    parity[0], half_count[0] = n % 2, j * 16 + (n // 2 + 1) * 16
                    split(i, j * 2 + n, j * 2 + (tick_of(U_GATE) + r - 1))
                    act.wait_ge(ticks, tick(i, j * 2 + (tick_of(U_GATE) + r)))
                    act.wait_ge(y_turned, i * KD + j * 2 + (r + 1))
                    act.activation(split2(sig[:, r % 2, :]), halves(G[r % 2]), ACT.Sigmoid)\
                       .then_inc(evacuated[r % 2], 1)

                def copy_y(j, r):
                    act.wait_ge(y_turned, i * KD + j * 2 + (r + 3))
                    cols = bass.ds(j * (2 * P) + r * P, P)
                    act.activation(y_tok[:, :, cols], X[r % 2][:, 0, :].rearrange("p (g c) -> p g c", c=P), ACT.Copy)
                    act.activation(y_small[:, :, cols], X[r % 2][0:SLEN, 1, 0:2 * P].rearrange("p (a c) -> p a c", a=2),
                                   ACT.Copy).then_inc(y_copied, 1)

                act.wait_ge(stored_y, i * 32 + 32)
                gate(0, 0)
                with act.Fori(0, KD // 2 - 1) as j:
                    gate(j, 1)
                    copy_y(j, 0)
                    gate(j, 2)
                    copy_y(j, 1)
                gate(0, 7)
                copy_y(0, 6)
                copy_y(0, 7)
                assert link[0] == CHAIN, link

            act.wait_ge(last_turned, 1)
            act.activation(turned[0:60, 0, :], X[0][0:60, 0, 0:P], ACT.Copy).then_inc(last_copied, 1)
            act.wait_ge(last_turned, 2)
            act.activation(turned[0:44, 1, :], X[1][0:44, 0, 0:P], ACT.Copy).then_inc(last_copied, 1)


        @block.vector
        def _(dve):
            par = [0]

            def slot(n):
                return n % 2 if isinstance(n, int) else par[0]

            def exact(t):
                return t.bitcast(F32)

            def split(i, n, parts=KD):
                s = slot(n)
                dve.wait_ge(hi_made, i * UNITS + (n + 1))
                dve.tensor_tensor(w_lo[s][:, 0:parts, :], stage[s][:, 0:parts, :], exact(w_hi[s][:, 0:parts, :]),
                                  ALU.subtract).then_inc(lo_made, 1)

            def step(instruction, name):
                vec_.did(instruction, name)

            def own(i, name):
                dve.wait_ge(vec_s, vec_.at(i, name))

            def add_square(i, n, zeros=None):
                if zeros:
                    own(i, zeros)
                dve.wait_ge(squared, i * SQUARES + (n + 1))
                dve.wait_ge(summed, i * SQUARES + (n + 2))
                dve.tensor_tensor(total[:, :], total[:, :], squares[:, slot(n), :], ALU.add).then_inc(summed, 1)

            starts = [(lo_made, 2), (ticks, 2), (evacuated[0], 1), (evacuated[1], 1), (summed, 2), (tapped, 2),
                      (past_mid, 2), (y_turned, 2), (y_copied, 8), (stored_y, 32), (stored_pool, 16), (stored_gla, 16),
                      (stored_conv, 16), (pe_s, len(PE_STEPS)), (act_s, len(ACT_STEPS)), (vec_s, len(VEC_STEPS)),
                      (pool_s, len(POOL_STEPS))]
            for n, (s_, value) in enumerate(starts):
                dve.memset(started[:, n:n + 1], 0.0).then_inc(s_, value)
            dve.memset(started[:, len(starts):len(starts) + 1], 0.0).then_inc(credited, 1)

            dve.wait_ge(constants_loaded, 16 * CONSTANTS)
            dve.wait_ge(split_once, 2)
            dve.tensor_tensor(w_pool_lo[:, :, :], raw_pool[:, :, :], exact(w_pool_hi[:, :, :]), ALU.subtract)\
               .then_inc(split_once, 1)
            dve.wait_ge(built, BUILT)
            dve.tensor_tensor(w_glow_lo[:, 0:P], raw_glow[:, :, :].rearrange("p k c -> p (k c)"),
                              exact(w_glow_hi[:, 0:P]), ALU.subtract).then_inc(split_once, 1)
            split(0, 0)

            with dve.Fori(0, TILES) as i:
                dve.wait_ge(pe_s, pe_.at(i, "states_turned"))
                dve.wait_ge(pool_s, pool_.before(i, "z_history"))
                dve.memset(Z[:, :, 0:1], 0.0)
                dve.memset(Z[:, :, ZS:].rearrange("p g (s t) -> p g s t", s=2)[:, :, :, 0:1], 0.0)
                dve.tensor_copy(Z[:, :, 1:16], z_past[:, :, 1:16])
                last = None
                for s in range(2):
                    last = dve.tensor_copy(Z[:, :, ZS + 24 * s + 1:ZS + 24 * s + 16],
                                           X[1][:, 0, 60 * s:60 * s + 60].rearrange("p (t g) -> p g t", g=POOLG))
                step(last, "states")
                dve.wait_ge(pe_s, pe_.before(i, "sum_post_ffn"))
                step(dve.memset(total[:, :], 0.0), "zeros_pre_mix")
                for m in range(KD):
                    add_square(i, m, "zeros_pre_mix" if m == 0 else None)

                def scaled(m, gain, name, before, ready):
                    if m >= 2:
                        dve.wait_ge(act_s, act_.at(i, f"{before}_hi{m - 2}"))
                        own(i, f"{before}_lo{m - 2}")
                    elif m == 0:
                        dve.wait_ge(act_s, act_.at(i, ready))
                    step(dve.scalar_tensor_tensor(normed[:, m % 2, :], xT[:, m, :], gains[:, gain, m:m + 1],
                                                  rms[:, :], ALU.mult, ALU.mult), name)

                def rest(m, name, hi_name, own_name):
                    dve.wait_ge(act_s, act_.at(i, hi_name))
                    own(i, own_name)
                    step(dve.tensor_tensor(h_lo[:, m, :], normed[:, m % 2, :], exact(h_hi[:, m, :]),
                                           ALU.subtract), name)

                dve.wait_ge(ticks, tick(i, -1))
                for s in range(KD + 1):
                    if s < KD:
                        scaled(s, 0, f"h{s}", "h", "rms_pre_mix")
                    if s:
                        rest(s - 1, f"h_lo{s - 1}", f"h_hi{s - 1}", f"h{s - 1}")

                def gap_step(h):
                    v = level_view(cum, h)
                    mid = v[:, :, :, h - 1:h].broadcast_to(list(v.shape))
                    step(dve.tensor_tensor(level_view(gap, h), v, mid, ALU.subtract), f"gap{h}")

                def operand_step(h, n):
                    dve.wait_ge(act_s, act_.at(i, f"decay{h}"))
                    if n >= 2:
                        dve.wait_ge(pe_s, pe_.at(i, f"scores{4 * h}" if 4 * h > 4 else f"small{4 * h}"))
                    elif n == 1:
                        dve.wait_ge(pe_s, pe_.at(i, "diag"))
                    dve.tensor_tensor(level_view(opnd[n % 2], h, 0), level_view(kT, h, 0), level_view(gap, h, 0), ALU.mult)
                    step(dve.tensor_tensor(level_view(opnd[n % 2], h, 1), level_view(qT, h, 1), level_view(gap, h, 1),
                                           ALU.mult), f"operand{h}")

                def take_scores(h, x, before):
                    dve.wait_ge(pe_s, pe_.at(i, f"scores{h}"))
                    own(i, before)
                    dve.sem_inc(passed, 1)
                    nb = 64 // h
                    out = A[:, :, :].rearrange("p r (n w) -> p r n w", w=2 * h)[:, :, :, h:]
                    mask = masks[:, LEVELS.index(h), :].rearrange("p (o n h) -> p o n h", o=1, h=h)
                    data = X[x][:, :, :].rearrange("p b (r n h) -> p (b r) n h", n=nb, h=h)
                    step(dve.copy_predicated(out, mask.broadcast_to([P, 16, nb, h]), data), f"scores{h}")

                def take_small(h, x, before):
                    dve.wait_ge(pe_s, pe_.at(i, f"small{h}"))
                    own(i, before)
                    dve.sem_inc(passed, 1)
                    nb = SLEN // 2 // h
                    for b in range(2):
                        out = A_s[:, 4 * b:4 * b + 4, :].rearrange("p r (n w) -> p r n w", w=2 * h)[:, :, :, h:]
                        mask = masks[0:SLEN, LEVELS.index(h), 0:SLEN // 2].rearrange("p (o n h) -> p o n h", o=1, h=h)
                        data = X[x][0:SLEN, b, 0:16].rearrange("p (r n h) -> p r n h", n=nb, h=h)
                        last = dve.copy_predicated(out, mask.broadcast_to([SLEN, 4, nb, h]), data)
                    step(last, f"small{h}")

                def update_state(c):
                    dve.wait_ge(act_s, act_.at(i, f"out{c}"))
                    if c:
                        own(i, f"state{c - 1}")
                    col = group_cols(c) + P - 1
                    for d in range(2):
                        for b in range(2):
                            r = slice(64 * b, 64 * b + 64)
                            last = dve.scalar_tensor_tensor(
                                S[r, d, :], S[r, d, :], cum[r, d, col:col + 1],
                                X[(c + 1) % 2][r, d, 256 + P * b:256 + P * b + P], ALU.mult, ALU.add)
                    step(last, f"state{c}")

                def extras(s):
                    if s == 1:
                        dve.wait_ge(act_s, act_.at(i, "gk_abs"))
                        for d in range(2):
                            last = dve.tensor_scalar(split2(gap[:, d, :]), halves(X[d]), bias_gk[:, d:d + 1], 0.0,
                                                     ALU.add, ALU.min)
                        step(last, "gk_min")
                        own(i, "gk_min")
                        dve.wait_ge(act_s, act_.at(i, "gk_log"))
                        step(dve.tensor_tensor(gap[:, :, :], gap[:, :, :], opnd[0][:, :, :], ALU.subtract), "gk")
                        own(i, "gk")
                        for d in range(2):
                            step(dve.tensor_tensor_scan(cum[:, d, :], keep[:, :], gap[:, d, :], 0.0, ALU.mult, ALU.add),
                                 f"cumsum{d}")
                    if s == 4:
                        for o in (2, 3):
                            dve.wait_ge(*evac(i, o))
                        own(i, "cumsum1")
                        step(dve.tensor_tensor(opnd[1][:, :, :], qT[:, :, :], kT[:, :, :], ALU.mult), "qk")
                        gap_step(64)
                        operand_step(64, 0)
                    if s == 5:
                        own(i, "operand64")
                        gap_step(32)
                        dve.wait_ge(pe_s, pe_.at(i, "diag"))
                        diag = X[0][:, :, 0:8].unsqueeze(3).broadcast_to([P, 2, 8, P])
                        eye = ident[:, :].rearrange("p (o q c) -> p o q c", o=1, q=1).broadcast_to([P, 2, 8, P])
                        step(dve.tensor_tensor(A[:, :, :].rearrange("p (b r) t -> p b r t", b=2), eye, diag, ALU.mult),
                             "scores_diag")
                        diag = X[0][0:SLEN, :, 8:12].unsqueeze(3).broadcast_to([SLEN, 2, 4, SLEN])
                        eye = ident[0:SLEN, 0:SLEN].rearrange("p (o q c) -> p o q c", o=1, q=1)\
                            .broadcast_to([SLEN, 2, 4, SLEN])
                        step(dve.tensor_tensor(A_s[:, :, :].rearrange("p (b r) t -> p b r t", b=2), eye, diag, ALU.mult),
                             "scores_small_diag")
                        take_scores(64, 1, "scores_diag")
                        operand_step(32, 1)
                    if 6 <= s <= 10:
                        n = s - 4
                        h = LEVELS[n]
                        own(i, f"operand{2 * h}")
                        gap_step(h)
                        take_scores(2 * h, (n + 0) % 2, f"scores{4 * h}")
                        if 2 * h <= 4:
                            take_small(2 * h, (n + 1) % 2, f"small{4 * h}" if 4 * h <= 4 else "scores_small_diag")
                        operand_step(h, n)
                    if s == 11:
                        own(i, "operand1")
                        v = cum[:, :, :].rearrange("p d (a c) -> p (d a) c", a=2)
                        g = gap[:, :, :].rearrange("p d (a c) -> p (d a) c", a=2)
                        vp = v[:, :, 0:HP].rearrange("p s (b c) -> p s b c", c=P)
                        dve.tensor_tensor(g[:, :, 0:HP].rearrange("p s (b c) -> p s b c", c=P),
                                          vp[:, :, :, P - 1:P].broadcast_to([P, 4, 2, P]), vp, ALU.subtract)
                        step(dve.tensor_tensor(g[:, :, HP:], v[:, :, HALF - 1:HALF].broadcast_to([P, 4, SLEN]),
                                               v[:, :, HP:], ALU.subtract), "kd_gap")
                        take_scores(1, 1, "scores2")
                        take_small(1, 0, "small2")
                        dve.wait_ge(act_s, act_.at(i, "kd_decay"))
                        step(dve.tensor_tensor(gap[:, :, :], gap[:, :, :], kT[:, :, :], ALU.mult), "kd")
                        dve.wait_ge(act_s, act_.at(i, "cum_decay"))
                        step(dve.tensor_tensor(qT[:, :, :], qT[:, :, :], cum[:, :, :], ALU.mult), "qb")
                    if s == 14:
                        update_state(0)
                    if s == 15:
                        update_state(1)

                for m in range(16):
                    split(i, m + 1)
                    extras(m)

                dve.wait_ge(pool_s, pool_.at(i, "window16"))
                for w_, first in ((win_a, 0), (win_b, 1)):
                    early = w_[:, first:POOLG:2, 16:32]
                    last = dve.tensor_tensor(early, early, edge[:, first:POOLG:2, :], ALU.mult)
                step(last, "edges_scaled")
                own(i, "edges_scaled")
                for w_, first in ((win_a, 0), (win_b, 1)):
                    early = w_[:, first:POOLG:2, 16:32]
                    last = dve.tensor_tensor(early, early, Z[:, first:POOLG:2, 16:32], ALU.subtract)
                step(last, "u_early")
                for g, w in enumerate(WINDOWS):
                    dst = (win_a if g % 2 == 0 else win_b)[:, g, 32:]
                    step(dve.scalar_tensor_tensor(dst, dst, 1.0 / w, Z[:, g, 32:], ALU.mult, ALU.subtract), f"u{g}")

                def u_rest(g):
                    dve.wait_ge(act_s, act_.at(i, f"u_hi{g}"))
                    own(i, f"u{g}")
                    w = win_a if g % 2 == 0 else win_b
                    lo, hi = split2(u_lo[:, g % 2, :]), split2(exact(u_hi[:, g % 2, :]))
                    dve.tensor_tensor(lo[:, :, 0:HP], w[:, g, 16:ZS].rearrange("p (a c) -> p a c", a=2),
                                      hi[:, :, 0:HP], ALU.subtract)
                    step(dve.tensor_tensor(lo[:, :, HP:], w[:, g, ZS:].rearrange("p (a c) -> p a c", a=2)[:, :, 16:],
                                           hi[:, :, HP:], ALU.subtract), f"u_lo{g}")

                def pool_rest(g, x):
                    dve.wait_ge(act_s, act_.at(i, f"mix_hi{g}"))
                    step(dve.scalar_tensor_tensor(split2(h_lo[:, g, :]), halves(X[x]), scale_pool[:, g:g + 1],
                                                  split2(exact(h_hi[:, g, :])), ALU.mult, ALU.subtract), f"mix_lo{g}")

                u_rest(0)
                u_rest(1)
                update_state(2)
                pool_rest(0, 0)
                u_rest(2)
                update_state(3)
                pool_rest(1, 1)
                u_rest(3)
                dve.wait_ge(pe_s, pe_.at(i, "state_small"))
                for a in range(2):
                    for d in range(2):
                        for b in range(2):
                            r = slice(64 * b, 64 * b + 64)
                            col = HALF * a + HALF - 1
                            last = dve.scalar_tensor_tensor(
                                S_s[r, a, d, :], S_s[r, a, d, :], cum[r, d, col:col + 1],
                                X[1][r, a, 256 * d + P * b:256 * d + P * b + P], ALU.mult, ALU.add)
                step(last, "state_small")
                pool_rest(2, 0)
                pool_rest(3, 1)
                for h in range(HEADS):
                    dve.wait_ge(act_s, act_.at(i, f"rms_head{h}"))
                    step(dve.scalar_tensor_tensor(outT[:, h, :], outT[:, h, :], gain_head[:, 0:1], rms[:, :],
                                                  ALU.mult, ALU.mult), f"out_scaled{h}")
                for s in range(HEADS + 1):
                    if s < HEADS:
                        own(i, f"out_scaled{s}")
                        dve.wait_ge(act_s, act_.at(i, "silu"))
                        step(dve.tensor_tensor(outT[:, s, :], outT[:, s, :], ogT[:, s, :], ALU.mult), f"out_gated{s}")
                    if s:
                        dve.wait_ge(act_s, act_.at(i, f"mix_hi{3 + s}"))
                        step(dve.tensor_tensor(h_lo[:, 3 + s, :], outT[:, s - 1, :], exact(h_hi[:, 3 + s, :]),
                                               ALU.subtract), f"mix_lo_head{s - 1}")

                step(dve.memset(total[:, :], 0.0), "zeros_mix")
                own(i, "zeros_mix")
                dve.sem_inc(passed, 1)
                with dve.Fori(0, KD // 2) as j:
                    for r in range(2):
                        par[0] = (r + 1) % 2
                        split(i, j * 2 + (U_O + r + 1))
                        par[0] = r
                        add_square(i, j * 2 + (8 + r))
                dve.wait_ge(pe_s, pe_.at(i, "sum_post_mix"))
                step(dve.memset(total[:, :], 0.0), "zeros_pre_ffn")
                dve.wait_ge(act_s, act_.at(i, "rms_post_mix"))
                for s in range(KD + 2):
                    if s < KD:
                        step(dve.scalar_tensor_tensor(mixed[:, s, :], mixed[:, s, :], gains[:, 1, s:s + 1], rms[:, :],
                                                      ALU.mult, ALU.mult), f"mixed{s}")
                    if 1 <= s <= KD:
                        own(i, f"mixed{s - 1}")
                        step(dve.tensor_tensor(xT[:, s - 1, :], xT[:, s - 1, :], mixed[:, s - 1, :], ALU.add),
                             f"x_mixed{s - 1}")
                    if s >= 2:
                        add_square(i, 16 + s - 2, "zeros_pre_ffn" if s == 2 else None)
                for s in range(KD + 1):
                    if s < KD:
                        scaled(s, 2, f"f{s}", "f", "rms_pre_ffn")
                    if s:
                        rest(s - 1, f"f_lo{s - 1}", f"f_hi{s - 1}", f"f{s - 1}")

                with dve.Fori(0, NF) as f:
                    par[0] = 1
                    split(i, f * 2 + (U_UP + 1))
                    dve.wait_ge(evacuated[0], i * (OUTS // 2) + f + (O_UP // 2 + 2))
                    dve.wait_ge(past_mid, i * (2 * NF) + f * 2 + 3)
                    for t in (1, 0):
                        dve.scalar_tensor_tensor(cg[:, :, :], gx[:, :, t:t + 266], taps[:, t, bass.ds(f, 1)], cg[:, :, :],
                                                 ALU.mult, ALU.add).then_inc(tapped, 1)
                        if t:
                            dve.wait_ge(tapped, i * (2 * NF) + f * 2 + 3)
                    par[0] = 0
                    split(i, f * 2 + (U_UP + 2))
                    dve.wait_ge(gelu_made, i * NF + f + 1)
                    dve.wait_ge(ticks, tick(i, f * 2 + (U_UP + 1)))
                    y2 = split2(yf[:, :])
                    dve.tensor_tensor(y2[:, :, 0:HP], cg[:, :, 0:HP], G[1][:, :, 0:HP], ALU.mult)
                    dve.tensor_tensor(y2[:, :, HP:], cg[:, :, HP + 2:], G[1][:, :, HP:HALF], ALU.mult)\
                       .then_inc(evacuated[1], 1)
                    dve.wait_ge(hidden_hi, i * NF + f + 1)
                    dve.tensor_tensor(y_lo[:, bass.ds(f, 1), :].rearrange("p o c -> p (o c)"), yf[:, :],
                                      exact(y_hi[:, bass.ds(f, 1), :]).rearrange("p o c -> p (o c)"),
                                      ALU.subtract).then_inc(hidden_lo, 1)

                def p_rest(x, cols, name):
                    dve.wait_ge(act_s, act_.at(i, f"p_hi{name}"))
                    for b in range(2):
                        last = dve.tensor_tensor(p_lo[:, :, cols[b]:cols[b] + P],
                                                 X[x][:, b, 0:256].rearrange("p (k c) -> p k c", k=2),
                                                 exact(p_hi[:, :, cols[b]:cols[b] + P]), ALU.subtract)
                    step(last, f"p_lo{name}")

                dve.wait_ge(past_mid, i * (2 * NF) + (2 * NF + 2))
                p_rest(0, (group_cols(0), group_cols(1)), "01")
                p_rest(1, (group_cols(2), group_cols(3)), "23")
                dve.wait_ge(act_s, act_.at(i, "p_hi_small"))
                step(dve.tensor_tensor(p_lo[:, :, :].rearrange("p k (a c) -> p k a c", a=2)[:, :, :, HP:],
                                       X[0][:, 0, 0:32].rearrange("p (k a c) -> p k a c", k=2, a=2),
                                       exact(p_hi[:, :, :]).rearrange("p k (a c) -> p k a c", a=2)[:, :, :, HP:],
                                       ALU.subtract), "p_lo_small")
                step(dve.memset(total[:, :], 0.0), "zeros_ffn")
                own(i, "zeros_ffn")
                dve.sem_inc(passed, 1)
                with dve.Fori(0, KD // 2) as j:
                    for r in range(6):
                        par[0] = (r + 1) % 2
                        split(i, j * 6 + (U_DOWN + r + 1), DOWN_PARTS[(r + 1) % 3][1])
                        if r % 3 == 2:
                            par[0] = r // 3
                            add_square(i, j * 2 + (24 + r // 3))
                split(i, U_PLE + 1)
                dve.wait_ge(act_s, act_.at(i, "rms_post_ffn"))
                for s in range(KD + 2):
                    if s == 4:
                        split(i, U_GATE)
                    if s < KD:
                        step(dve.scalar_tensor_tensor(ffn_out[:, s, :], ffn_out[:, s, :], gains[:, 3, s:s + 1],
                                                      rms[:, :], ALU.mult, ALU.mult), f"ffn{s}")
                    if 1 <= s <= KD:
                        own(i, f"ffn{s - 1}")
                        step(dve.tensor_tensor(xT[:, s - 1, :], xT[:, s - 1, :], ffn_out[:, s - 1, :], ALU.add),
                             f"x_ffn{s - 1}")
                    if s >= 2:
                        dve.wait_ge(act_s, act_.at(i, f"x_hi{s - 2}"))
                        step(dve.tensor_tensor(h_lo[:, s - 2, :], xT[:, s - 2, :], exact(h_hi[:, s - 2, :]),
                                               ALU.subtract), f"x_lo{s - 2}")

                def gate(j, r):
                    n = U_GATE + r + 1
                    par[0] = n % 2
                    split(i, j * 2 + n)
                    m = bass.ds(j * 2 + r, 1) if r < 7 else slice(7, 8)
                    if not isinstance(j, int):
                        flat = lambda t: t[:, m, :].rearrange("p o c -> p (o c)")
                    else:
                        flat = lambda t: t[:, r, :]
                    dve.wait_ge(evacuated[r % 2], i * (OUTS // 2) + j + ((O_GATE + r) // 2 + 2))
                    dve.tensor_tensor(sig[:, r % 2, :], sig[:, r % 2, :], flat(ple), ALU.mult).then_inc(gated, 1)
                    dve.wait_ge(gated, i * KD + j * 2 + (r + 1))
                    dve.tensor_tensor(sig[:, r % 2, :], flat(xT), sig[:, r % 2, :], ALU.add).then_inc(added, 1)

                gate(0, 0)
                with dve.Fori(0, KD // 2 - 1) as j:
                    gate(j, 1)
                    gate(j, 2)
                gate(0, 7)

        @block.tensor
        def _(pe):
            drained = {0: None, 1: None}

            def use(i, x, steps, name):
                if drained[x]:
                    s, n = drained[x]
                    pe.wait_ge(s.sem, s.at(i, n))
                drained[x] = (steps, name)

            def product(ps, lhs_hi, lhs_lo, rhs_hi, rhs_lo, start=True, stop=True):
                for n, (l, r) in enumerate(((lhs_hi, rhs_hi), (lhs_lo, rhs_hi), (lhs_hi, rhs_lo))):
                    for a in range(2):
                        last = pe.matmul(ps[:, a, 0:HALF], l, r[:, HALF * a:HALF * a + HALF],
                                         start=start and n == 0, stop=stop and n == 2)
                return last

            def unit(i, n, s, o, hi, lo, first=0, parts=KD, start=True, stop=True, ready=None):
                pe.wait_ge(lo_made, i * UNITS + (n + 3))
                if start:
                    pe.wait_ge(evacuated[o[0]], i * (OUTS // 2) + o[1])
                for k in range(parts):
                    if ready:
                        pe.wait_ge(vec_s, vec_.at(i, ready(k)))
                    last = product(G[o[0]], w_hi[s][:, k, :], w_lo[s][:, k, :], hi[:, first + k, :],
                                   lo[:, first + k, :], start and k == 0, stop and k == parts - 1)
                last.then_inc(ticks, 1)

            def out_of(o):
                return o % 2, o // 2 + 1

            def ones_sum(x, src, name):
                for a in range(2):
                    last = pe.matmul(X[x][:, a, 0:HALF], ones[:, :], src[:, HALF * a:HALF * a + HALF],
                                     start=True, stop=True)
                pe_.did(last, name)

            def turn(out, in_, n=P):
                return pe.transpose(out, in_, ident[0:n, 0:n])

            pe.wait_ge(built, BUILT)
            pe.wait_ge(split_once, 4)
            pe.wait_ge(credited, 1)

            with pe.Fori(0, TILES) as i:
                pe.wait_ge(x_loaded, i * 32 + 32)
                pe.wait_ge(y_copied, i * 8 + 8)
                drained[0] = drained[1] = None
                for g in range(NG):
                    use(i, g % 2, act_, f"x_turned{g}")
                    for k in range(KD):
                        last = turn(X[g % 2][:, k // 4, P * (k % 4):P * (k % 4) + P], x_tok[:, g, P * k:P * k + P])
                    pe_.did(last, f"x_turned{g}")
                use(i, 0, act_, "x_turned4")
                pe.sem_inc(passed, 1)
                for k in range(KD):
                    last = turn(X[0][:, 0, 16 * k:16 * k + 16], x_small[:, P * k:P * k + P], 16)
                pe_.did(last, "x_turned4")
                pe.wait_ge(states_loaded, i * 32 + 32)
                use(i, 1, vec_, "states")
                turn(X[1][:, 0, 0:120], z_state_tok[:, :], 120)
                pe_.did(turn(X[1][:, 1, 0:4 * NF], g_state_tok[:, :], 4 * NF), "states_turned")
                pe.wait_ge(summed, i * SQUARES + (8 + 2))
                use(i, 0, act_, "rms_pre_mix")
                ones_sum(0, total, "sum_pre_mix")
                pe.wait_ge(act_s, act_.at(i, "conv_state"))
                use(i, 1, act_, "glow")
                for k in range(KD):
                    pe.wait_ge(vec_s, vec_.at(i, f"h_lo{k}"))
                    last = product(X[1], w_glow_hi[:, RANK * k:RANK * k + P], w_glow_lo[:, RANK * k:RANK * k + P],
                                   h_hi[:, k, :], h_lo[:, k, :], k == 0, k == KD - 1)
                pe_.did(last, "glow")

                def head_rows(b):
                    return slice(64 * b, 64 * b + 64)

                def scores(h, x):
                    use(i, x, vec_, f"scores{h}")
                    t = opnd[LEVELS.index(h) % 2]
                    pe.wait_ge(vec_s, vec_.at(i, f"operand{h}"))
                    for b in range(2):
                        for d in range(2):
                            for c in range(NG):
                                keys = t[head_rows(b), d, group_cols(c):group_cols(c) + P]
                                queries = keys.rearrange("p (n w) -> p n w", w=2 * h)[:, :, h:]
                                col = 64 * (4 * d + c)
                                last = pe.matmul(X[x][:, b, col:col + 64], keys, queries, start=True, stop=True)
                    pe_.did(last, f"scores{h}")

                def small_tokens(t, b, d, a):
                    return t[head_rows(b), d, HALF * a + HP:HALF * a + HALF]

                def small_scores(h, x):
                    use(i, x, vec_, f"small{h}")
                    pe.sem_inc(passed, 1)
                    t = opnd[LEVELS.index(h) % 2]
                    for b in range(2):
                        for d in range(2):
                            for a in range(2):
                                keys = small_tokens(t, b, d, a)
                                queries = keys.rearrange("p (n w) -> p n w", w=2 * h)[:, :, h:]
                                col = 4 * (2 * d + a)
                                last = pe.matmul(X[x][0:SLEN, b, col:col + 4], keys, queries, start=True, stop=True)
                    pe_.did(last, f"small{h}")

                def out_chunk(c):
                    x = (c + 1) % 2
                    use(i, x, act_, f"out{c}")
                    if c < 2:
                        pe.wait_ge(act_s, act_.at(i, "v_copied1"))
                    pe.wait_ge(vec_s, vec_.at(i, f"state{c - 1}" if c else "qb"))
                    cols = slice(group_cols(c), group_cols(c) + P)
                    for h in range(HEADS):
                        d, b = h // 2, h % 2
                        out = X[x][:, b, P * d:P * d + P]
                        pe.matmul(out, v_tok[:, c, P * h:P * h + P], A[:, 8 * b + 4 * d + c, :],
                                  start=True, stop=False)
                        pe.matmul(out, S[head_rows(b), d, :], qT[head_rows(b), d, cols], start=False, stop=True)
                    for d in range(2):
                        last = pe.matmul(X[x][:, d, 256:512], kd_tok[:, c, d, :],
                                         v_tok[:, c, 256 * d:256 * d + 256], start=True, stop=True)
                    pe_.did(last, f"out{c}")

                def pool_group(g, x, ready):
                    use(i, x, vec_, f"mix_lo{g}")
                    if ready:
                        pe.wait_ge(vec_s, vec_.at(i, ready))
                    pe_.did(product(X[x], w_pool_hi[:, g, :], w_pool_lo[:, g, :], u_hi[:, g % 2, :], u_lo[:, g % 2, :]),
                            f"pool{g}")

                def extras(s):
                    if s == 0:
                        pe.wait_ge(act_s, act_.at(i, "glow"))
                        for d in range(2):
                            use(i, d, vec_, "gk_min")
                            for a in range(2):
                                last = pe.matmul(X[d][:, a, 0:HALF], w_gk[:, P * d:P * d + P],
                                                 squares[0:RANK, 0, HALF * a:HALF * a + HALF], start=True, stop=True)
                            pe_.did(last, f"gk{d}")
                    if s == 4:
                        use(i, 0, vec_, "scores_small_diag")
                        pe.wait_ge(vec_s, vec_.at(i, "qk"))
                        for b in range(2):
                            for d in range(2):
                                for c in range(NG):
                                    pe.matmul(X[0][:, b, 4 * d + c:4 * d + c + 1],
                                              opnd[1][head_rows(b), d, group_cols(c):group_cols(c) + P],
                                              ones[head_rows(b), 0:1], start=True, stop=True)
                                for a in range(2):
                                    col = 8 + 2 * d + a
                                    last = pe.matmul(X[0][0:SLEN, b, col:col + 1], small_tokens(opnd[1], b, d, a),
                                                     ones[head_rows(b), 0:1], start=True, stop=True)
                        pe_.did(last, "diag")
                        scores(64, 1)
                    if 5 <= s <= 10:
                        n = s - 4
                        h = LEVELS[n]
                        scores(h, (n + 1) % 2)
                        if h <= 4:
                            small_scores(h, n % 2)
                    if s == 11:
                        use(i, 1, act_, "kd_copied")
                        pe.wait_ge(vec_s, vec_.at(i, "kd"))
                        for c in range(NG):
                            for d in range(2):
                                last = turn(X[1][:, c // 2, P * (2 * (c % 2) + d):P * (2 * (c % 2) + d) + P],
                                            gap[:, d, group_cols(c):group_cols(c) + P])
                        pe_.did(last, "kd_turned")
                        use(i, 0, act_, "kd_small")
                        for a in range(2):
                            for d in range(2):
                                col = P * (2 * a + d)
                                last = turn(X[0][0:SLEN, 0, col:col + P], gap[:, d, HALF * a + HP:HALF * a + HALF])
                        pe_.did(last, "kd_small_turned")
                    if s == 12:
                        for o in (6, 7):
                            pe.wait_ge(*evac(i, o))
                        for n in range(2):
                            use(i, n, act_, f"v_copied{n}")
                            for c in (2 * n, 2 * n + 1):
                                for h in range(HEADS):
                                    last = turn(X[n][:, c % 2, P * h:P * h + P],
                                                vT[:, h, group_cols(c):group_cols(c) + P])
                            pe_.did(last, f"v_turned{n}")
                    if s == 13:
                        use(i, 0, act_, "v_small")
                        for a in range(2):
                            for h in range(HEADS):
                                last = turn(X[0][0:SLEN, a, P * h:P * h + P], vT[:, h, HALF * a + HP:HALF * a + HALF])
                        pe_.did(last, "v_small_turned")
                        out_chunk(0)
                    if s == 14:
                        out_chunk(1)

                for m in range(16):
                    unit(i, m, m % 2, out_of(m), h_hi, h_lo, ready=(lambda k: f"h_lo{k}") if m == 0 else None)
                    extras(m)
                out_chunk(2)
                pool_group(0, 0, "u_lo0")
                out_chunk(3)
                pool_group(1, 1, None)
                use(i, 0, act_, "out_small")
                pe.wait_ge(vec_s, vec_.at(i, "state3"))
                pe.wait_ge(s_loaded, i * 16 + 16)
                for h in range(HEADS):
                    d, b = h // 2, h % 2
                    for a in range(2):
                        out = X[0][:, b, 16 * d + 8 * a:16 * d + 8 * a + 8]
                        pe.matmul(out, v_small[:, a, P * h:P * h + P], A_s[:, 4 * b + 2 * d + a, :],
                                  start=True, stop=False)
                        last = pe.matmul(out, S_s[head_rows(b), a, d, :],
                                         qT[head_rows(b), d, HALF * a + HP:HALF * a + HALF], start=False, stop=True)
                pe_.did(last, "out_small")
                use(i, 1, vec_, "state_small")
                for a in range(2):
                    for d in range(2):
                        last = pe.matmul(X[1][:, a, 256 * d:256 * d + 256], kd_small[:, a, P * d:P * d + P],
                                         v_small[:, a, 256 * d:256 * d + 256], start=True, stop=True)
                pe_.did(last, "state_small")
                pool_group(2, 0, "u_lo2")
                pool_group(3, 1, None)
                for h in range(HEADS):
                    use(i, h % 2, act_, f"rms_head{h}")
                    if h == 0:
                        pe.wait_ge(act_s, act_.at(i, "out_squares"))
                    ones_sum(h % 2, out_sq[:, h, :], f"head{h}")
                use(i, 0, act_, "pool_state")
                pe.wait_ge(pool_s, pool_.at(i, "z_tail"))
                pe_.did(turn(X[0][0:120, 0, 0:P], z_state[:, :]), "pool_state_turned")

                def mixed_block(k):
                    return f"mix_lo{k}" if k < 4 else f"mix_lo_head{k - 4}"

                unit(i, U_O, 0, out_of(O_O), h_hi, h_lo, ready=mixed_block)
                with pe.Fori(0, KD // 2 - 1) as j:
                    for r in (1, 2):
                        unit(i, j * 2 + (U_O + r), r % 2, (r % 2, j + ((O_O + r) // 2 + 1)), h_hi, h_lo)
                unit(i, U_O + 7, 1, out_of(O_O + 7), h_hi, h_lo)
                use(i, 1, act_, "rms_post_mix")
                pe.wait_ge(summed, i * SQUARES + (16 + 2))
                ones_sum(1, total, "sum_post_mix")
                use(i, 0, act_, "rms_pre_ffn")
                pe.wait_ge(summed, i * SQUARES + (24 + 2))
                ones_sum(0, total, "sum_pre_ffn")

                unit(i, U_UP, 0, out_of(O_UP), h_hi, h_lo, ready=lambda k: f"f_lo{k}")
                with pe.Fori(0, NF - 1) as f:
                    for r in (1, 2):
                        unit(i, f * 2 + (U_UP + r), r % 2, (r % 2, f + ((O_UP + r) // 2 + 1)), h_hi, h_lo)
                unit(i, U_UP + 2 * NF - 1, 1, out_of(O_UP + 2 * NF - 1), h_hi, h_lo)

                pe.wait_ge(p_loaded, i * 32 + 32)
                for n in range(2):
                    use(i, n, vec_, f"p_lo{'01' if n == 0 else '23'}")
                    for b in range(2):
                        for k in range(2):
                            last = turn(X[n][:, b, P * k:P * k + P], p_tok[:, 2 * n + b, P * k:P * k + P])
                    pe_.did(last, f"p_turned{'01' if n == 0 else '23'}")
                use(i, 0, vec_, "p_lo_small")
                pe.sem_inc(passed, 1)
                for k in range(2):
                    last = turn(X[0][:, 0, 16 * k:16 * k + 16], p_small[:, P * k:P * k + P], 16)
                pe_.did(last, "p_turned_small")
                use(i, 1, act_, "conv_out")
                pe.wait_ge(past_mid, i * (2 * NF) + (2 * NF + 2))
                pe_.did(turn(X[1][0:88, 0, 0:P], g_tail[:, :, :, :].rearrange("p s t f -> p (s t f)")),
                        "conv_state_turned")
                pe.wait_ge(hidden_lo, i * NF + NF)
                pe.sem_inc(passed, 1)
                with pe.Fori(0, KD // 2) as j:
                    for r in range(6):
                        first, parts = DOWN_PARTS[r % 3]
                        unit(i, j * 6 + (U_DOWN + r), r % 2, (r // 3, j + (O_DOWN // 2 + 1)), y_hi, y_lo,
                             first, parts, r % 3 == 0, r % 3 == 2)
                use(i, 0, act_, "rms_post_ffn")
                for m in range(KD):
                    s, q = m // 4, m % 4
                    if q == 0:
                        pe.wait_ge(lo_made, i * UNITS + (U_PLE + s + 3))
                    if m == 1:
                        pe.wait_ge(summed, i * SQUARES + (32 + 2))
                        ones_sum(0, total, "sum_post_ffn")
                    pair, free = out_of(O_PLE + m)
                    pe.wait_ge(evacuated[pair], i * (OUTS // 2) + free)
                    for k in range(2):
                        last = product(G[pair], w_hi[s][:, 4 * k + q, :], w_lo[s][:, 4 * k + q, :],
                                       p_hi[:, k, :], p_lo[:, k, :], k == 0, k == 1)
                    last.then_inc(ticks, 1)

                def turn_y(j, r):
                    pe.wait_ge(added, i * KD + j * 2 + (r + 1))
                    pe.wait_ge(y_copied, i * 8 + j * 2 + (r + 7))
                    x = r % 2
                    block_ = sig[:, x, :]
                    for c in range(NG):
                        turn(X[x][:, 0, P * c:P * c + P], block_[:, group_cols(c):group_cols(c) + P])
                    for a in range(2):
                        last = turn(X[x][0:SLEN, 1, P * a:P * a + P], block_[:, HALF * a + HP:HALF * a + HALF])
                    last.then_inc(y_turned, 1)

                unit(i, U_GATE, 0, out_of(O_GATE), h_hi, h_lo, ready=lambda k: f"x_lo{k}")
                for x in range(2):
                    s, n = drained[x]
                    pe.wait_ge(s.sem, s.at(i, n))
                pe.sem_inc(passed, 1)
                with pe.Fori(0, KD // 2 - 1) as j:
                    for r in (1, 2):
                        unit(i, j * 2 + (U_GATE + r), r % 2, (r % 2, j + ((O_GATE + r) // 2 + 1)), h_hi, h_lo)
                        turn_y(j, r - 1)
                unit(i, U_GATE + 7, 1, out_of(O_GATE + 7), h_hi, h_lo)
                turn_y(0, 6)
                turn_y(0, 7)

            pe.wait_ge(y_copied, TILES * 8 + 8)
            pe.wait_ge(last_packed, 1)
            turn(X[0][0:60, 0, 0:P], z_state[:, 0:60]).then_inc(last_turned, 1)
            turn(X[1][0:44, 0, 0:P], g_past[:, :, :].rearrange("p t f -> p (t f)")).then_inc(last_turned, 1)


_INS = ['x_prompt', 'x_sample', 'state_pool', 'state_gla', 'state_conv', 'p_prompt', 'p_sample', 'g_pre_mix',
        'w_in', 'w_gk2', 'b_gk2', 'w_pool', 'pool_scale', 'gla_norm', 'w_o', 'g_post_mix', 'g_pre_ffn', 'w_up',
        'w_conv', 'b_conv', 'w_down', 'g_post_ffn', 'w_ple', 'w_ple_gate']
_OUTS = [(1, SEQ, D), (NSEQ, SLEN, D), (1, 1, HIST, POOLW), (1, 1, HEADS, KDIM, VDIM), (1, 1, 2, FF),
         (1, NSEQ, HIST, POOLW), (1, NSEQ, HEADS, KDIM, VDIM), (1, NSEQ, 2, FF)]


def kernel(**inputs):
    import numpy as _np
    import concourse.bacc as _bacc
    from concourse.bass_utils import run_bass_kernel_spmd as _run

    nc = _bacc.Bacc("TRN2", target_bir_lowering=False, num_devices=1)
    arrays, args = {}, []
    for name in _INS:
        a = _np.ascontiguousarray(inputs[name])
        arrays[f"in_{name}_dram"] = a
        args.append(nc.dram_tensor(f"in_{name}_dram", a.shape, F32, kind="ExternalInput").ap())
    for n, shape in enumerate(_OUTS):
        args.append(nc.dram_tensor(f"out_{n}_dram", shape, F32, kind="ExternalOutput").ap())
    hybrid_layer(nc, *args)
    r = _run(nc, [arrays], core_ids=[0])
    return tuple(r.results[0][f"out_{n}_dram"] for n in range(len(_OUTS)))
```

```python
from contextlib import ExitStack

import concourse.bass as bass
from concourse import mybir

F32 = mybir.dt.float32
F32R = mybir.dt.float32r
U8 = mybir.dt.uint8
ALU = mybir.AluOpType
ACT = mybir.ActivationFunctionType

P = 128
D = 1024
KD = D // P
SEQ, NSEQ, SLEN = 2048, 8, 8
TILES = 4
TOK = SEQ // TILES
HP = TOK // 2
HALF = HP + SLEN
T = 2 * HALF
NG = 4
POOLW, POOLG, HIST = 512, 4, 15
WINDOWS = (2, 4, 8, 16)
HEADS, KDIM, VDIM = 4, 64, 128
RANK = 16
FF = 2816
NF = FF // P
PLE = 256
EPS = 1e-6
LN_EXP = "natural_log_exp_and_others"
GATE_NORM = 16.0
ZS = 16 + TOK
ZW = ZS + 2 * 24
LEVELS = (64, 32, 16, 8, 4, 2, 1)

W_IN_COLS = ([768, 896] + [512, 640] + [1024 + P * j for j in range(4)] + [P * j for j in range(4)]
             + [1552 + P * j for j in range(4)])
GLOW_COL = 1536
U_IN, U_O, U_UP, U_DOWN, U_PLE, U_GATE, UNITS = 0, 16, 24, 68, 92, 94, 102
DOWN_PARTS = ((0, 8), (8, 7), (15, 7))
TICKS = 108
OUTS = 92
O_IN, O_O, O_UP, O_DOWN, O_PLE, O_GATE = 0, 16, 24, 68, 76, 84


def tick_of(unit):
    if unit < U_PLE:
        return unit
    if unit < U_GATE:
        return U_PLE + 4 * (unit - U_PLE) + 3
    return unit + 6


class Steps:

    def __init__(self, sem, names):
        self.sem, self.names, self.next = sem, list(names), 0
        assert len(set(self.names)) == len(self.names)

    def did(self, instruction, name):
        assert self.names[self.next] == name, (self.names[self.next], name)
        self.next += 1
        instruction.then_inc(self.sem, 1)

    def at(self, i, name):
        return (i + 1) * len(self.names) + self.names.index(name) + 1

    def before(self, i, name):
        return i * len(self.names) + self.names.index(name) + 1


def staggered(*kinds, n=KD):
    return [f"{kind}{s - d}" for s in range(n + len(kinds) - 1) for d, kind in enumerate(kinds)
            if 0 <= s - d < n]


PE_STEPS = (
    ["states_turned", "glow", "gk0", "gk1", "diag", "scores64", "scores32", "scores16", "scores8",
     "scores4", "small4", "v_turned0", "scores2", "small2", "v_turned1", "scores1", "small1",
     "v_small_turned", "kd_turned", "kd_small_turned", "out0", "out1", "out2", "out3", "pool0",
     "out_small", "pool1", "state_small", "pool2", "head0", "pool3", "head1", "head2", "head3",
     "pool_state_turned", "sum_post_mix", "p_turned01", "p_turned23", "p_turned_small",
     "conv_state_turned", "sum_post_ffn"]
)
ACT_STEPS = (
    [f"h_hi{m}" for m in range(KD)]
    + ["pool_history", "conv_state", "glow", "gk_abs", "gk_exp", "gk_log", "decay64", "decay32",
       "decay16", "decay8", "decay4", "v_copied0", "decay2", "v_copied1", "decay1", "v_small",
       "kd_decay", "cum_decay", "kd_copied", "kd_small", "out0", "out1", "u_hi0", "u_hi1", "out2", "silu",
       "out3", "mix_hi0", "u_hi2", "out_small", "mix_hi1", "u_hi3", "out_squares", "mix_hi2",
       "rms_head0", "mix_hi3", "rms_head1", "mix_hi4", "rms_head2", "mix_hi5", "rms_head3", "mix_hi6",
       "mix_hi7", "pool_state", "rms_post_mix", "rms_pre_ffn"]
    + [f"f_hi{m}" for m in range(KD)]
    + ["p_hi01", "p_hi23", "p_hi_small", "conv_out", "rms_post_ffn"] + [f"x_hi{m}" for m in range(KD)]
)
VEC_STEPS = (
    staggered("h", "h_lo")
    + ["gk_min", "gk", "cumsum0", "cumsum1", "states", "qk", "gap64", "operand64",
       "gap32", "scores_diag", "scores_small_diag", "scores64", "operand32",
       "gap16", "scores32", "operand16", "gap8", "scores16", "operand8", "gap4", "scores8", "operand4",
       "gap2", "scores4", "small4", "operand2", "gap1", "scores2", "small2", "operand1",
       "kd_gap", "scores1", "small1", "kd", "qb", "state0", "edges_scaled", "u_early",
       "u0", "u1", "u2", "u3", "state1", "u_lo0", "u_lo1", "state2", "state3", "mix_lo0", "u_lo2",
       "mix_lo1", "u_lo3", "state_small", "mix_lo2", "out_scaled0", "out_gated0", "mix_lo3",
       "out_scaled1", "out_gated1", "mix_lo4", "out_scaled2", "out_gated2", "mix_lo5",
       "out_scaled3", "out_gated3", "mix_lo6", "mix_lo7", "zeros_mix"]
    + staggered("mixed", "x_mixed") + staggered("f", "f_lo")
    + ["p_lo01", "p_lo23", "p_lo_small", "zeros_ffn"] + staggered("ffn", "x_ffn", "x_lo")
)
POOL_STEPS = ["window2", "window4", "window8", "window16", "z_tail", "z_history", "z_edges"]
CONSTANTS = 14
BUILT = 3 + 4 * len(LEVELS) + 7 + 1 + 4 + (1 + 3 + 7 + 15) + 3 + 2
HEAD_BANKS = (0, 0, 1, 0)
CHAIN = 8
SQUARES = 32


def hybrid_layer(nc, x_prompt, x_sample, state_pool, state_gla, state_conv, p_prompt, p_sample,
                 g_pre_mix, w_in, w_gk2, b_gk2, w_pool, pool_scale, gla_norm, w_o, g_post_mix,
                 g_pre_ffn, w_up, w_conv, b_conv, w_down, g_post_ffn, w_ple, w_ple_gate,
                 y_prompt, y_sample, pool_prompt, gla_prompt, conv_prompt, pool_sample, gla_sample,
                 conv_sample):
    ctx = ExitStack()
    with ctx:
        base = [nc.sbuf_base + 31 & ~31]
        top = nc.sbuf_usable_end

        def at(name, shape, dtype, offset):
            return nc.alloc_sbuf_tensor_at(name, shape, dtype, offset=offset)

        def own(name, shape, dtype=F32):
            n = mybir.dt.size(dtype)
            for s in shape[1:]:
                n *= s
            o = base[0]
            base[0] = (o + n + 31) // 32 * 32
            assert base[0] <= top, (name, base[0], top)
            return at(name, shape, dtype, o)

        def region(words):
            o = base[0]
            base[0] += 4 * words
            assert base[0] <= top, (base[0], top)
            return o

        def placed(start, name, shape, dtype, cursor):
            n = 1
            for s in shape[1:]:
                n *= s
            t = at(name, shape, dtype, start + 4 * cursor[0])
            cursor[0] += (n + 7) // 8 * 8
            return t

        ident = own("ident", [P, P])
        ones = own("ones", [P, P])
        masks = own("masks", [P, len(LEVELS), 64], U8)
        keep = own("keep", [P, T])
        gains = own("gains", [P, 4, KD])
        bias_gk = own("bias_gk", [P, 2])
        scale_pool = own("scale_pool", [P, POOLG])
        gain_head = own("gain_head", [P, 1])
        taps = own("taps", [P, 3, NF])
        bias_conv = own("bias_conv", [P, NF])
        eps = own("eps", [P, 1])
        edge = own("edge", [P, POOLG, 16])
        w_gk = own("w_gk", [RANK, 2 * P])
        w_glow_hi = own("w_glow_hi", [P, KD * RANK + P], F32R)
        w_glow_lo = own("w_glow_lo", [P, KD * RANK + P], F32R)
        w_pool_hi = own("w_pool_hi", [P, POOLG, P], F32R)
        w_pool_lo = own("w_pool_lo", [P, POOLG, P], F32R)
        z_past = own("z_past", [P, POOLG, 16])
        g_past = own("g_past", [P, 2, NF])
        g_state = own("g_state", [P, 2, 2, NF])
        g_tail = own("g_tail", [P, 2, 2, NF])
        S = own("S", [P, 2, P])
        S_s = own("S_s", [P, 2, 2, P])
        z_in = own("z_in", [P, 2 * HIST * POOLG])
        z_state = own("z_state", [P, 2 * HIST * POOLG])
        started = own("started", [1, 32])
        turned = own("turned", [P, 2, P])
        norm_at = region(2 * T + T)
        squares = at("squares", [P, 2, T], F32, norm_at)
        rms = at("rms", [P, T], F32, norm_at + 4 * 2 * T)
        p_tok = at("p_tok", [P, NG, PLE], F32, norm_at)
        p_small = at("p_small", [16, PLE], F32, norm_at + 4 * 2 * T)
        total = own("total", [P, T])
        xT = own("xT", [P, KD, T])

        stage = [own(f"stage{s}", [P, KD, P]) for s in range(2)]
        w_hi = [own(f"w_hi{s}", [P, KD, P], F32R) for s in range(2)]
        w_lo = [own(f"w_lo{s}", [P, KD, P], F32R) for s in range(2)]

        h_at = region(2 * KD * T)
        h_hi = at("h_hi", [P, KD, T], F32R, h_at)
        h_lo = at("h_lo", [P, KD, T], F32R, h_at + 4 * KD * T)
        ffn_out = at("ffn_out", [P, KD, T], F32, h_at)

        scratch = region(3648)
        c = [0]
        A = placed(scratch, "A", [P, 16, P], F32, c)
        A_s = placed(scratch, "A_s", [SLEN, 8, SLEN], F32, c)
        kd_tok = placed(scratch, "kd_tok", [P, NG, 2, P], F32, c)
        kd_small = placed(scratch, "kd_small", [SLEN, 2, 2 * P], F32, c)
        assert c[0] <= 3648, c
        c = [0]
        gx = placed(scratch, "gx", [P, 2, 268], F32, c)
        cg = placed(scratch, "cg", [P, 2, 266], F32, c)
        yf = placed(scratch, "yf", [P, T], F32, c)
        assert c[0] <= 1600
        normed = placed(scratch, "normed", [P, 2, T], F32, [1600])
        c = [0]
        p_lo = placed(scratch, "p_lo", [P, 2, T], F32R, c)
        p_hi = at("p_hi", [P, 2, T], F32R, scratch + 4 * 1600)

        big = region(2 * NF * T)
        y_hi = at("y_hi", [P, NF, T], F32R, big)
        y_lo = at("y_lo", [P, NF, T], F32R, big + 4 * NF * T)
        c = [0]
        kT = placed(big, "kT", [P, 2, T], F32, c)
        qT = placed(big, "qT", [P, 2, T], F32, c)
        vT = placed(big, "vT", [P, HEADS, T], F32, c)
        ogT = placed(big, "ogT", [P, HEADS, T], F32, c)
        Z = placed(big, "Z", [P, POOLG, ZW], F32, c)
        win_a = placed(big, "win_a", [P, POOLG, ZW], F32, c)
        win_b = placed(big, "win_b", [P, POOLG, ZW], F32, c)
        u_hi = placed(big, "u_hi", [P, 2, T], F32R, c)
        u_lo = placed(big, "u_lo", [P, 2, T], F32R, c)
        cum = placed(big, "cum", [P, 2, T], F32, c)
        gap = placed(big, "gap", [P, 2, T], F32, c)
        opnd = [placed(big, f"opnd{n}", [P, 2, T], F32, c) for n in range(2)]
        v_tok = placed(big, "v_tok", [P, NG, HEADS * P], F32, c)
        v_small = placed(big, "v_small", [SLEN, 2, HEADS * P], F32, c)
        assert c[0] <= 2 * NF * T, c
        outT = at("outT", [P, HEADS, T], F32, big + 4 * 2 * (2 * T))
        out_sq = at("out_sq", [P, HEADS, T], F32, big + 4 * (6 * 2 * T + 2 * POOLG * ZW // 2))
        mixed = at("mixed", [P, KD, T], F32, big)
        c = [0]
        x_tok = placed(big, "x_tok", [P, NG, D], F32, c)
        x_small = placed(big, "x_small", [SLEN, 2, D], F32, c)
        y_tok = placed(big, "y_tok", [P, NG, D], F32, c)
        y_small = placed(big, "y_small", [SLEN, 2, D], F32, c)
        ple = placed(big, "ple", [P, KD, T], F32, c)
        sig = placed(big, "sig", [P, 2, T], F32, c)
        z_state_tok = placed(big, "z_state_tok", [2 * HIST * POOLG, P], F32, c)
        g_state_tok = placed(big, "g_state_tok", [4 * NF, P], F32, c)
        assert c[0] <= 2 * NF * T, c
        x_next = at("x_next", [P, KD, T], F32, big + 4 * (2 * NF * T - KD * T))
        assert c[0] <= 2 * NF * T - KD * T
        raw_pool = at("raw_pool", [P, POOLG, P], F32, big)
        raw_glow = at("raw_glow", [P, KD, RANK], F32, big + 4 * 512)

        G = [ctx.enter_context(nc.psum_tensor(f"G{n}", [P, 2, 512], F32)) for n in range(2)]
        X = [ctx.enter_context(nc.psum_tensor(f"X{n}", [P, 2, 512], F32)) for n in range(2)]

        def halves(ps):
            return ps[:, :, 0:HALF]

        def split2(ap):
            return ap.rearrange("p (a c) -> p a c", a=2)

        def group_cols(c):
            return HALF * (c // 2) + P * (c % 2)

        def sem(name):
            return ctx.enter_context(nc.semaphore(name))

        constants_loaded = sem("constants_loaded")
        built = sem("built")
        split_once = sem("split_once")
        staged = [sem(f"staged{s}") for s in range(2)]
        hi_made = sem("hi_made")
        lo_made = sem("lo_made")
        ticks = sem("ticks")
        evacuated = [sem(f"evacuated{n}") for n in range(2)]
        squared = sem("squared")
        summed = sem("summed")
        x_loaded, states_loaded, s_loaded, p_loaded = sem("x_loaded"), sem("states_loaded"), sem("s_loaded"), sem("p_loaded")
        stored_y, stored_pool, stored_gla, stored_conv = sem("stored_y"), sem("stored_pool"), sem("stored_gla"), sem("stored_conv")
        gate_copied, past_in, past_mid = sem("gate_copied"), sem("past_in"), sem("past_mid")
        tap_now, tapped = sem("tap_now"), sem("tapped")
        gelu_made, hidden_hi, hidden_lo = sem("gelu_made"), sem("hidden_hi"), sem("hidden_lo")
        gated, added, y_turned, y_copied = sem("gated"), sem("added"), sem("y_turned"), sem("y_copied")
        last_turned, last_copied, last_packed = sem("last_turned"), sem("last_copied"), sem("last_packed")
        pe_s, act_s, vec_s, pool_s = sem("pe_steps"), sem("act_steps"), sem("vec_steps"), sem("pool_steps")
        pe_, act_, vec_, pool_ = (Steps(pe_s, PE_STEPS), Steps(act_s, ACT_STEPS),
                                  Steps(vec_s, VEC_STEPS), Steps(pool_s, POOL_STEPS))
        x_turned, x_moved = sem("x_turned"), sem("x_moved")
        x_summed, x_rms = sem("x_summed"), sem("x_rms")
        logs = sem("logs")
        passed = sem("passed")
        credited = sem("credited")

        def tick(i, n):
            return i * TICKS + (n + 3)

        def evac(i, o):
            return evacuated[o % 2], i * (OUTS // 2) + (o // 2 + 2)

        def level_view(t, h, side=None):
            w = HALF if h <= 4 else HP
            v = t[:, :, :].rearrange("p d (a c) -> p (d a) c", a=2)[:, :, 0:w]
            v = v.rearrange("p s (n w) -> p s n w", w=2 * h)
            return v if side is None else v[:, :, :, h * side:h * side + h]

        block = ctx.enter_context(nc.Block())

        @block.sync
        def _(sp):
            def rows(w, first, n, col):
                return w[first:first + P * n, col].rearrange("(k p) c -> p k c", p=P)

            def load_unit(i, n, src, parts=KD):
                sp.wait_ge(lo_made, i * UNITS + (n + 1))
                sp.sem_inc(passed, 1)
                sp.dma_start(stage[n_mod(n)][:, 0:parts, :], src).then_inc(staged[n_mod(n)], 16)

            def n_mod(n):
                return n % 2 if isinstance(n, int) else n_parity[0]

            n_parity = [0]

            n = [0]

            def constant(dst, src):
                sp.dma_start(dst, src).then_inc(constants_loaded, 16)
                n[0] += 16

            with nc.allow_non_contiguous_dma(reason="small vectors, once"):
                constant(raw_glow[:, :, :], rows(w_in[0], 0, KD, slice(GLOW_COL, GLOW_COL + RANK)))
                constant(raw_pool[:, :, :], w_pool[0].rearrange("g c d -> c g d"))
                constant(w_gk[:, :], w_gk2[0])
                for m, g in enumerate((g_pre_mix, g_post_mix, g_pre_ffn, g_post_ffn)):
                    constant(gains[:, m, :], g[0].rearrange("(k p) -> p k", p=P))
                constant(bias_gk[:, :], b_gk2[0].rearrange("(k p) -> p k", p=P))
                constant(scale_pool[:, :], pool_scale[0].rearrange("(k p) -> p k", p=P))
                constant(gain_head[:, :], gla_norm[0].rearrange("(k p) -> p k", p=P))
                for m in range(3):
                    constant(taps[:, m, :], w_conv[0, m].rearrange("(k p) -> p k", p=P))
                constant(bias_conv[:, :], b_conv[0].rearrange("(k p) -> p k", p=P))
            assert n[0] == 16 * CONSTANTS
            load_unit(0, 0, rows(w_in[0], 0, KD, slice(W_IN_COLS[0], W_IN_COLS[0] + P)))

            def load_x(tile, groups, small):
                for g in groups:
                    xp = x_prompt[0, bass.ds(tile * TOK + g * P, P), :]
                    sp.dma_start(x_tok[:, g, :], xp).then_inc(x_loaded, 16)
                if small:
                    xs = x_sample.rearrange("b s d -> s b d")[:, bass.ds(tile * 2, 2), :]
                    sp.dma_start(x_small[:, :, :], xs).then_inc(x_loaded, 16)
                    zs = state_pool[0].rearrange("b t (g c) -> (b t g) c", g=POOLG)
                    sp.dma_start(z_state_tok[:, :], zs[bass.ds(tile * 120, 120), :]).then_inc(states_loaded, 16)
                    gs = state_conv[0].rearrange("b t (f c) -> (b t f) c", f=NF)
                    sp.dma_start(g_state_tok[:, :], gs[bass.ds(tile * 88, 88), :]).then_inc(states_loaded, 16)

            sp.wait_ge(split_once, 4)
            load_x(0, range(NG), True)

            with sp.Fori(0, TILES) as i:
                sp.wait_ge(stored_gla, i * 16 + 16)
                sg = state_gla[0].rearrange("b (d h) k v -> (h k) b d v", h=2)
                sp.dma_start(S_s[:, :, :, :], sg[:, bass.ds(i * 2, 2), :, :]).then_inc(s_loaded, 16)

                for m in range(1, 16):
                    load_unit(i, m, rows(w_in[0], 0, KD, slice(W_IN_COLS[m], W_IN_COLS[m] + P)))
                with sp.Fori(0, KD // 2) as j:
                    for r in range(2):
                        n_parity[0] = r
                        load_unit(i, j * 2 + (U_O + r), rows(w_o[0], 0, KD, bass.ds(j * 2 * P + r * P, P)))
                sp.wait_ge(act_s, act_.at(i, "pool_state"))
                sp.dma_start(pool_sample[0].rearrange("b t (g c) -> (b t g) c", g=POOLG)
                             [bass.ds(i * 120, 120), :], turned[0:120, 0, :]).then_inc(stored_pool, 16)
                sp.wait_ge(vec_s, vec_.at(i, "state_small"))
                so = gla_sample[0].rearrange("b (d h) k v -> (h k) b d v", h=2)
                sp.dma_start(so[:, bass.ds(i * 2, 2), :, :], S_s[:, :, :, :]).then_inc(stored_gla, 16)
                for r in range(2):
                    load_unit(i, U_UP + r, rows(w_up[0], 0, KD, slice(FF * (1 - r), FF * (1 - r) + P)))
                sp.wait_ge(vec_s, vec_.at(i, f"f{KD - 1}"))
                pp = p_prompt[0, 0, bass.ds(i * TOK, TOK), :].rearrange("(g p) d -> p g d", p=P)
                sp.dma_start(p_tok[:, :, :], pp).then_inc(p_loaded, 16)
                ps = p_sample[0].rearrange("b s d -> (b s) d")[bass.ds(i * 16, 16), :]
                sp.dma_start(p_small[:, :], ps).then_inc(p_loaded, 16)
                with sp.Fori(1, NF) as f:
                    for r in range(2):
                        n_parity[0] = r
                        load_unit(i, f * 2 + (U_UP + r), rows(w_up[0], 0, KD, bass.ds(f * P + FF * (1 - r), P)))
                with sp.Fori(0, KD // 2) as j:
                    for r in range(6):
                        n_parity[0] = r % 2
                        first, parts = DOWN_PARTS[r % 3]
                        load_unit(i, j * 6 + (U_DOWN + r),
                                  rows(w_down[0], first * P, parts, bass.ds(j * 2 * P + r // 3 * P, P)), parts)
                sp.wait_ge(act_s, act_.at(i, "conv_out"))
                sp.dma_start(conv_sample[0].rearrange("b t (f c) -> (b t f) c", f=NF)
                             [bass.ds(i * 88, 88), :], turned[0:88, 1, :]).then_inc(stored_conv, 16)
                for m in range(2):
                    sp.wait_ge(lo_made, i * UNITS + (U_PLE + m + 1))
                    dst = stage[m][:, :, :].rearrange("p (k c) d -> p k (c d)", k=2)
                    sp.dma_start(dst, w_ple[0, :, 512 * m:512 * m + 512].rearrange("(k p) c -> p k c", p=P))\
                      .then_inc(staged[m], 16)
                sp.wait_ge(ticks, tick(i, U_PLE - 1))
                sp.sem_inc(passed, 1)
                after = (i + 1) % TILES
                load_x(after, (0, 1), False)
                load_unit(i, U_GATE, rows(w_ple_gate[0], 0, KD, slice(0, P)))
                load_x(after, (2, 3), True)
                with sp.Fori(0, KD // 2 - 1) as j:
                    for r in (1, 2):
                        n_parity[0] = r % 2
                        load_unit(i, j * 2 + (U_GATE + r), rows(w_ple_gate[0], 0, KD, bass.ds(j * 2 * P + r * P, P)))
                load_unit(i, U_GATE + KD - 1, rows(w_ple_gate[0], 0, KD, slice(P * (KD - 1), P * KD)))
                load_unit(i, UNITS, rows(w_in[0], 0, KD, slice(W_IN_COLS[0], W_IN_COLS[0] + P)))
                sp.wait_ge(y_copied, i * 8 + 16)
                yp = y_prompt[0, bass.ds(i * TOK, TOK), :].rearrange("(g p) d -> p g d", p=P)
                sp.dma_start(yp, y_tok[:, :, :]).then_inc(stored_y, 16)
                ys = y_sample.rearrange("b s d -> s b d")[:, bass.ds(i * 2, 2), :]
                sp.dma_start(ys, y_small[:, :, :]).then_inc(stored_y, 16)

            sp.wait_ge(vec_s, vec_.at(TILES - 1, "state3"))
            sp.dma_start(gla_prompt[0, 0].rearrange("(d h) k v -> (h k) d v", h=2), S[:, :, :]).then_inc(stored_gla, 16)
            sp.wait_ge(last_copied, 1)
            sp.dma_start(pool_prompt[0, 0].rearrange("t (g c) -> (t g) c", g=POOLG),
                         turned[0:60, 0, :]).then_inc(stored_pool, 16)
            sp.wait_ge(last_copied, 2)
            sp.dma_start(conv_prompt[0, 0].rearrange("t (f c) -> (t f) c", f=NF),
                         turned[0:44, 1, :]).then_inc(stored_conv, 16)
            sp.wait_ge(states_loaded, TILES * 32 + 32)
            sp.wait_ge(stored_y, TILES * 32 + 32)
            sp.wait_ge(stored_pool, TILES * 16 + 32)
            sp.wait_ge(stored_gla, TILES * 16 + 32)
            sp.wait_ge(stored_conv, TILES * 16 + 32)

        @block.gpsimd
        def _(pool):
            n = [0]

            def build(instruction):
                n[0] += 1
                instruction.then_inc(built, 1)
                pool.wait_ge(built, n[0])

            build(pool.memset(ones[:, :], 1.0))
            build(pool.memset(ident[:, :], 0.0))
            build(pool.affine_select(out=ident[:, :], in_=ident[:, :], compare_op=ALU.not_equal, fill=1.0,
                                     base=0, pattern=[[-1, P]], channel_multiplier=1))
            sel = total
            for n_level, h in enumerate(LEVELS):
                m = sel[:, 0:64].rearrange("p (n h) -> p n h", h=h)
                build(pool.memset(sel[:, 0:64], 1.0))
                build(pool.affine_select(out=m, in_=m, compare_op=ALU.is_ge, fill=0.0, base=0,
                                         pattern=[[-2 * h, 64 // h], [0, h]], channel_multiplier=1))
                build(pool.affine_select(out=m, in_=m, compare_op=ALU.is_ge, fill=0.0, base=h - 1,
                                         pattern=[[2 * h, 64 // h], [0, h]], channel_multiplier=-1))
                build(pool.tensor_copy(masks[:, n_level, :], sel[:, 0:64]))
            build(pool.memset(keep[:, :], 1.0))
            for a in range(2):
                for first in (0, P, HP):
                    build(pool.memset(keep[:, a * HALF + first:a * HALF + first + 1], 0.0))
            build(pool.memset(eps[:, :], EPS))
            for g, w in enumerate(WINDOWS):
                build(pool.memset(edge[:, g, :], 1.0 / w))
                for t in range(w - 1):
                    build(pool.memset(edge[:, g, t:t + 1], 1.0 / (t + 1)))
            build(pool.memset(z_past[:, :, :], 0.0))
            build(pool.memset(g_past[:, :, :], 0.0))
            build(pool.memset(S[:, :, :], 0.0))
            for w in (w_glow_hi, w_glow_lo):
                build(pool.memset(w[:, P:2 * P].bitcast(F32), 0.0))
            assert n[0] == BUILT, n

            with pool.Fori(0, TILES) as i:
                pool.wait_ge(y_turned, i * KD + 2)
                pool.sem_inc(passed, 1)
                pool.wait_ge(squared, i * SQUARES + KD)
                pool.sem_inc(passed, 1)
                pool.tensor_copy(xT[:, :, :], x_next[:, :, :]).then_inc(x_moved, 1)
                for o in (O_IN + 11, O_IN + 10):
                    pool.wait_ge(*evac(i, o))
                pool.wait_ge(vec_s, vec_.at(i, "states"))
                src, dst = Z, win_a
                for k, w in enumerate(WINDOWS):
                    if k:
                        pool.wait_ge(pool_s, pool_.at(i, f"window{WINDOWS[k - 1]}"))
                    pool_.did(pool.tensor_tensor(dst[:, k:, w - 1:], src[:, k:, w - 1:],
                                                 src[:, k:, w // 2 - 1:ZW - w // 2], ALU.add), f"window{w}")
                    src, dst = dst, (win_b if dst is win_a else win_a)
                tail = Z[:, :, ZS:].rearrange("p g (s t) -> p s t g", s=2)[:, :, 24 - HIST:, :]
                pool_.did(pool.tensor_copy(z_state[:, :].rearrange("p (s t g) -> p s t g", s=2, g=POOLG), tail),
                          "z_tail")
                pool_.did(pool.tensor_copy(z_past[:, :, 1:16], Z[:, :, ZS - HIST:ZS]), "z_history")
                pool.wait_ge(vec_s, vec_.at(i, "u_early"))
                pool.sem_inc(passed, 1)
                for g, w in enumerate(WINDOWS):
                    last = pool.memset(edge[:, g, :], 1.0 / w)
                pool_.did(last, "z_edges")

                pool.wait_ge(pe_s, pe_.at(i, "state_small"))
                pool.sem_inc(passed, 1)
                with pool.Fori(0, NF) as f:
                    pool.wait_ge(tapped, i * 2 * NF + f * 2 + 2)
                    pool.tensor_copy(gx[:, 0, 0:2], g_past[:, :, bass.ds(f, 1)].rearrange("p t o -> p (t o)"))
                    pool.tensor_copy(gx[:, :, 258:260], g_state[:, :, :, bass.ds(f, 1)]
                                     .rearrange("p s t o -> p s (t o)")).then_inc(past_in, 1)
                    pool.wait_ge(gate_copied, i * NF + f + 1)
                    pool.sem_inc(passed, 1)
                    pool.tensor_copy(gx[:, 1, 0:2], gx[:, 0, 256:258]).then_inc(past_mid, 1)
                    pool.wait_ge(past_in, i * NF + f + 1)
                    pool.sem_inc(passed, 1)
                    pool.tensor_copy(g_past[:, :, bass.ds(f, 1)].rearrange("p t o -> p (t o)"), gx[:, 1, 256:258])
                    pool.tensor_copy(g_tail[:, :, :, bass.ds(f, 1)].rearrange("p s t o -> p s (t o)"),
                                     gx[:, :, 266:268]).then_inc(past_mid, 1)

            pool.wait_ge(pool_s, pool_.at(TILES - 1, "z_edges"))
            pool.tensor_copy(z_state[:, 0:60].rearrange("p (t g) -> p t g", g=POOLG),
                             z_past[:, :, 1:16].rearrange("p g t -> p t g")).then_inc(last_packed, 1)

        @block.scalar
        def _(act):
            def mod2(n):
                return n % 2 if isinstance(n, int) else parity[0]

            parity = [0]

            def split(i, n, free, parts=KD):
                s = mod2(n)
                act.wait_ge(staged[s], i * (UNITS // 2 * 16) + stage_count(n))
                act.wait_ge(ticks, tick(i, free))
                act.activation(w_hi[s][:, 0:parts, :], stage[s][:, 0:parts, :], ACT.Copy).then_inc(hi_made, 1)

            def stage_count(n):
                return (n // 2 + 1) * 16 if isinstance(n, int) else half_count[0]

            half_count = [0]

            def root(x, i, n, out=None, width=D):
                out = rms[:, :] if out is None else out
                act.activation(split2(out), halves(x), ACT.Ln, scale=1.0 / width, bias=eps[:, 0:1]).then_inc(logs, 1)
                act.wait_ge(logs, i * CHAIN + (n + 2))
                return act.activation(out, out, ACT.Exp, scale=-0.5)

            def square(src, i, n):
                act.wait_ge(summed, i * SQUARES + (n + 1))
                dst = squares[:, n % 2 if isinstance(n, int) else parity[0], :]
                act.activation(dst if len(src.shape) == 2 else split2(dst), src, ACT.Square).then_inc(squared, 1)

            act.wait_ge(constants_loaded, 16 * CONSTANTS)
            act.activation(w_pool_hi[:, :, :], raw_pool[:, :, :], ACT.Copy).then_inc(split_once, 1)
            act.activation(w_glow_hi[:, 0:P], raw_glow[:, :, :].rearrange("p k c -> p (k c)"), ACT.Copy)\
               .then_inc(split_once, 1)
            act.wait_ge(credited, 1)
            act.wait_ge(built, BUILT)
            act.wait_ge(staged[0], 16)
            act.activation(w_hi[0][:, :, :], stage[0][:, :, :], ACT.Copy).then_inc(hi_made, 1)

            def take_x(i, k, number=None):
                act.wait_ge(x_turned, i * KD + (k + 1))
                x = X[k % 2 if isinstance(k, int) else parity[0]]
                block_ = x_next[:, k, :] if isinstance(k, int) else \
                    x_next[:, bass.ds(k, 1), :].rearrange("p o c -> p (o c)")
                act.activation(split2(block_), halves(x), ACT.Copy)
                act.wait_ge(summed, i * SQUARES + (k + 1))
                act.activation(split2(squares[:, k % 2 if isinstance(k, int) else parity[0], :]), halves(x),
                               ACT.Square).then_inc(squared, 1)

            act.preload_act_table_set(LN_EXP)
            for k in range(KD):
                take_x(0, k)
            act.wait_ge(x_summed, 1)
            root(X[1], 0, -1).then_inc(x_rms, 1)
            with act.Fori(0, TILES) as i:
                act.wait_ge(ticks, tick(i, -1))
                for m in range(KD):
                    act.wait_ge(vec_s, vec_.at(i, f"h{m}"))
                    act_.did(act.activation(h_hi[:, m, :], normed[:, m % 2, :], ACT.Copy), f"h_hi{m}")

                act.wait_ge(pe_s, pe_.at(i, "states_turned"))
                act_.did(act.activation(z_in[:, :], X[0][:, 0, 0:2 * HIST * POOLG], ACT.Copy), "pool_history")
                act_.did(act.activation(g_state[:, :, :, :].rearrange("p s t f -> p (s t f)"),
                                        X[0][:, 1, 0:4 * NF], ACT.Copy), "conv_state")
                act.wait_ge(pe_s, pe_.at(i, "glow"))
                act_.did(act.activation(squares[0:RANK, 0, :].rearrange("p (a c) -> p a c", a=2),
                                        halves(X[1])[0:RANK], ACT.Copy), "glow")

                def extras(s):
                    if s == 1:
                        for d in range(2):
                            act.wait_ge(pe_s, pe_.at(i, f"gk{d}"))
                            last = act.activation(split2(opnd[0][:, d, :]), halves(X[d]), ACT.Abs,
                                                  bias=bias_gk[:, d:d + 1])
                        act_.did(last, "gk_abs")
                        act.wait_ge(act_s, act_.at(i, "gk_abs"))
                        act_.did(act.activation(opnd[0][:, :, :], opnd[0][:, :, :], ACT.Exp, scale=-1.0), "gk_exp")
                        act.wait_ge(act_s, act_.at(i, "gk_exp"))
                        act_.did(act.activation(opnd[0][:, :, :], opnd[0][:, :, :], ACT.Ln, bias=1.0), "gk_log")
                    if s in (9, 10):
                        if s == 9:
                            act.wait_ge(x_moved, i + 1)
                        act.wait_ge(pe_s, pe_.at(i, f"v_turned{s - 9}"))
                        act_.did(act.activation(v_tok[:, 2 * s - 18:2 * s - 16, :], G[(s + 1) % 2][:, :, :], ACT.Copy),
                                 f"v_copied{s - 9}")
                    if s == 11:
                        act.wait_ge(pe_s, pe_.at(i, "v_small_turned"))
                        act_.did(act.activation(v_small[:, :, :], G[0][0:SLEN, :, :], ACT.Copy), "v_small")
                    if 4 <= s <= 10:
                        h = LEVELS[s - 4]
                        act.wait_ge(vec_s, vec_.at(i, f"gap{h}"))
                        v = level_view(gap, h)
                        act.activation(v[:, :, :, 0:h], v[:, :, :, 0:h], ACT.Exp, scale=-1.0 / GATE_NORM)
                        act_.did(act.activation(v[:, :, :, h:], v[:, :, :, h:], ACT.Exp, scale=1.0 / GATE_NORM),
                                 f"decay{h}")
                    if s == 11:
                        act.wait_ge(vec_s, vec_.at(i, "kd_gap"))
                        act_.did(act.activation(gap[:, :, :], gap[:, :, :], ACT.Exp, scale=1.0 / GATE_NORM), "kd_decay")
                        act_.did(act.activation(cum[:, :, :], cum[:, :, :], ACT.Exp, scale=1.0 / GATE_NORM), "cum_decay")
                    if s == 12:
                        act.wait_ge(pe_s, pe_.at(i, "kd_turned"))
                        act_.did(act.activation(kd_tok[:, :, :, :].rearrange("p c d k -> p (c d k)"),
                                                X[1][:, :, :].rearrange("p b c -> p (b c)"), ACT.Copy), "kd_copied")
                        act.wait_ge(pe_s, pe_.at(i, "kd_small_turned"))
                        act_.did(act.activation(kd_small[:, :, :].rearrange("p a c -> p (a c)"), X[0][0:SLEN, 0, :],
                                                ACT.Copy), "kd_small")
                    if s == 13:
                        copy_out(0)
                    if s == 14:
                        copy_out(1)
                        u_split(0)
                        u_split(1)
                    if s == 15:
                        copy_out(2)
                        for m in (13, 14):
                            act.wait_ge(*evac(i, m))
                        act.activation(ogT[:, 0:3, :], ogT[:, 0:3, :], ACT.Silu)

                def copy_out(c):
                    act.wait_ge(pe_s, pe_.at(i, f"out{c}"))
                    act_.did(act.activation(outT[:, :, group_cols(c):group_cols(c) + P]
                                            .rearrange("p (d b) c -> p b d c", b=2),
                                            X[(c + 1) % 2][:, :, 0:2 * P].rearrange("p b (d c) -> p b d c", c=P),
                                            ACT.Copy), f"out{c}")

                def u_split(g):
                    act.wait_ge(vec_s, vec_.at(i, f"u{g}"))
                    if g >= 2:
                        act.wait_ge(pe_s, pe_.at(i, f"pool{g - 2}"))
                    w = win_a if g % 2 == 0 else win_b
                    act.activation(u_hi[:, g % 2, :].rearrange("p (a c) -> p a c", a=2)[:, :, 0:HP],
                                   w[:, g, 16:ZS].rearrange("p (a c) -> p a c", a=2), ACT.Copy)
                    act_.did(act.activation(u_hi[:, g % 2, :].rearrange("p (a c) -> p a c", a=2)[:, :, HP:],
                                            w[:, g, ZS:].rearrange("p (a c) -> p a c", a=2)[:, :, 16:], ACT.Copy),
                             f"u_hi{g}")

                def pool_split(g):
                    act.wait_ge(pe_s, pe_.at(i, f"pool{g}"))
                    act_.did(act.activation(split2(h_hi[:, g, :]), halves(X[1]), ACT.Copy,
                                            scale=scale_pool[:, g:g + 1]), f"mix_hi{g}")

                for m in range(16):
                    split(i, m + 1, tick_of(m - 1) if m else -1)
                    extras(m)
                    act.wait_ge(ticks, tick(i, m))
                    src = halves(G[m % 2])
                    if 8 <= m < 12:
                        g = m - 8
                        act.activation(Z[:, g, 16:ZS].rearrange("p (a c) -> p a c", a=2), src[:, :, 0:HP], ACT.Copy)
                        act.activation(Z[:, g, ZS:].rearrange("p (a c) -> p a c", a=2)[:, :, 16:],
                                       src[:, :, HP:], ACT.Copy).then_inc(evacuated[m % 2], 1)
                    else:
                        dst, at_, scale = ((kT, m, 1.0) if m < 2 else (qT, m - 2, KDIM ** -0.5) if m < 4
                                           else (vT, m - 4, 1.0) if m < 8 else (ogT, m - 12, 1.0))
                        act.activation(split2(dst[:, at_, :]), src, ACT.Copy, scale=scale)\
                           .then_inc(evacuated[m % 2], 1)
                split(i, U_O + 1, 15)
                act.wait_ge(*evac(i, 15))
                act_.did(act.activation(ogT[:, 3, :], ogT[:, 3, :], ACT.Silu), "silu")
                act.sem_inc(passed, 1)
                act.preload_act_table_set(LN_EXP)
                copy_out(3)
                pool_split(0)
                u_split(2)
                act.wait_ge(pe_s, pe_.at(i, "out_small"))
                for b in range(2):
                    last = act.activation(outT[:, b:HEADS:2, :].rearrange("p d (a c) -> p d a c", a=2)[:, :, :, HP:],
                                          X[0][:, b, 0:32].rearrange("p (d a c) -> p d a c", d=2, a=2), ACT.Copy)
                act_.did(last, "out_small")
                pool_split(1)
                u_split(3)
                act.wait_ge(act_s, act_.at(i, "out_small"))
                act.wait_ge(vec_s, vec_.at(i, "u_lo2"))
                act_.did(act.activation(out_sq[:, :, :], outT[:, :, :], ACT.Square), "out_squares")
                pool_split(2)

                def head_split(h):
                    act.wait_ge(vec_s, vec_.at(i, f"out_gated{h}"))
                    act_.did(act.activation(h_hi[:, 4 + h, :], outT[:, h, :], ACT.Copy), f"mix_hi{4 + h}")

                for h in range(HEADS):
                    act.wait_ge(pe_s, pe_.at(i, f"head{h}"))
                    if h >= 2:
                        act.wait_ge(vec_s, vec_.at(i, f"out_scaled{h - 2}"))
                    act_.did(root(X[HEAD_BANKS[h]], i, h, squares[:, h % 2, :], VDIM), f"rms_head{h}")
                    if h == 0:
                        pool_split(3)
                    else:
                        head_split(h - 1)
                head_split(HEADS - 1)
                act.wait_ge(pe_s, pe_.at(i, "pool_state_turned"))
                act.wait_ge(stored_pool, i * 16 + 16)
                act_.did(act.activation(turned[0:120, 0, :], X[1][0:120, 0, 0:P], ACT.Copy), "pool_state")

                with act.Fori(0, KD // 2) as j:
                    for r in range(2):
                        parity[0], half_count[0] = r, j * 16 + (U_O + r + 2) // 2 * 16 + 16
                        act.wait_ge(ticks, tick(i, j * 2 + (U_O + r)))
                        square(halves(G[r]), i, j * 2 + (8 + r))
                        act.activation(split2(mixed[:, bass.ds(j * 2 + r, 1), :].rearrange("p o c -> p (o c)")),
                                       halves(G[r]), ACT.Copy).then_inc(evacuated[r], 1)
                        split(i, j * 2 + (U_O + r + 2), j * 2 + (U_O + r))
                act.wait_ge(pe_s, pe_.at(i, "sum_post_mix"))
                act_.did(root(X[1], i, 4), "rms_post_mix")
                for m in range(KD):
                    act.wait_ge(vec_s, vec_.at(i, f"x_mixed{m}"))
                    square(xT[:, m, :], i, 16 + m)
                act.wait_ge(summed, i * SQUARES + (24 + 2))
                act_.did(root(X[0], i, 5), "rms_pre_ffn")
                for m in range(KD):
                    act.wait_ge(vec_s, vec_.at(i, f"f{m}"))
                    act_.did(act.activation(h_hi[:, m, :], normed[:, m % 2, :], ACT.Copy), f"f_hi{m}")

                act.sem_inc(passed, 1)
                act.preload_act_table(ACT.Gelu_apprx_tanh)
                def ffn_block(f, last=False):
                    parity[0], half_count[0] = 0, f * 16 + (U_UP + 2) // 2 * 16 + 16
                    split(i, f * 2 + (U_UP + 2), f * 2 + U_UP)
                    act.wait_ge(tapped, i * (2 * NF) + f * 2 + 2)
                    act.wait_ge(past_mid, i * (2 * NF) + f * 2 + 2)
                    act.activation(gx[:, :, 2:258], G[0][:, :, 0:HP], ACT.Copy)
                    act.activation(gx[:, :, 260:268], G[0][:, :, HP:HALF], ACT.Copy).then_inc(gate_copied, 1)
                    act.wait_ge(gate_copied, i * NF + f + 1)
                    act.wait_ge(past_in, i * NF + f + 1)
                    act.activation(cg[:, :, :], gx[:, :, 2:268], ACT.Identity,
                                   scale=taps[:, 2, bass.ds(f, 1)], bias=bias_conv[:, bass.ds(f, 1)])\
                       .then_inc(evacuated[0], 1)
                    act.wait_ge(tapped, i * (2 * NF) + f * 2 + 4)
                    act.activation(cg[:, :, :], cg[:, :, :], ACT.Gelu_apprx_tanh).then_inc(gelu_made, 1)
                    if not last:
                        parity[0], half_count[0] = 1, f * 16 + (U_UP + 3) // 2 * 16 + 16
                        split(i, f * 2 + (U_UP + 3), f * 2 + (U_UP + 1))
                    act.wait_ge(evacuated[1], i * (OUTS // 2) + f + ((O_UP + 1) // 2 + 2))
                    act.activation(y_hi[:, bass.ds(f, 1), :].rearrange("p o c -> p (o c)"), yf[:, :], ACT.Copy)\
                       .then_inc(hidden_hi, 1)

                with act.Fori(0, NF - 1) as f:
                    ffn_block(f)
                ffn_block(NF - 1, last=True)

                act.sem_inc(passed, 1)
                act.preload_act_table_set(LN_EXP)

                def down(j, r):
                    n, parts = U_DOWN + r + 1, DOWN_PARTS[(r + 1) % 3][1]
                    parity[0], half_count[0] = n % 2, j * 48 + (n // 2 + 1) * 16
                    split(i, j * 6 + n, j * 6 + (U_DOWN + r - 1), parts)
                    if r % 3 == 2:
                        act.wait_ge(ticks, tick(i, j * 6 + (U_DOWN + r)))
                        parity[0] = r // 3
                        square(halves(G[r // 3]), i, j * 2 + (24 + r // 3))
                        act.activation(split2(ffn_out[:, bass.ds(j * 2 + r // 3, 1), :].rearrange("p o c -> p (o c)")),
                                       halves(G[r // 3]), ACT.Copy).then_inc(evacuated[r // 3], 1)

                def p_split(x, cols, name):
                    act.wait_ge(pe_s, pe_.at(i, f"p_turned{name}"))
                    for b in range(2):
                        last = act.activation(p_hi[:, :, cols[b]:cols[b] + P],
                                              X[x][:, b, 0:256].rearrange("p (k c) -> p k c", k=2), ACT.Copy)
                    act_.did(last, f"p_hi{name}")

                p_split(0, (group_cols(0), group_cols(1)), "01")
                p_split(1, (group_cols(2), group_cols(3)), "23")
                act.wait_ge(pe_s, pe_.at(i, "p_turned_small"))
                act_.did(act.activation(p_hi[:, :, :].rearrange("p k (a c) -> p k a c", a=2)[:, :, :, HP:],
                                        X[0][:, 0, 0:32].rearrange("p (k a c) -> p k a c", k=2, a=2), ACT.Copy),
                         "p_hi_small")
                act.wait_ge(pe_s, pe_.at(i, "conv_state_turned"))
                act.wait_ge(stored_conv, i * 16 + 16)
                act_.did(act.activation(turned[0:88, 1, :], X[1][0:88, 0, 0:P], ACT.Copy), "conv_out")
                with act.Fori(0, KD // 2) as j:
                    for r in range(6):
                        down(j, r)


                def copy_ple(m):
                    act.wait_ge(ticks, tick(i, U_PLE + m))
                    act.activation(split2(ple[:, m, :]), halves(G[m % 2]), ACT.Copy).then_inc(evacuated[m % 2], 1)

                def x_split(m):
                    act.wait_ge(vec_s, vec_.at(i, f"x_ffn{m}"))
                    act_.did(act.activation(h_hi[:, m, :], xT[:, m, :], ACT.Copy), f"x_hi{m}")

                split(i, U_PLE + 1, tick_of(U_PLE - 1))
                for m in range(KD):
                    copy_ple(m)
                    if m == 1:
                        act.wait_ge(pe_s, pe_.at(i, "sum_post_ffn"))
                        act_.did(root(X[0], i, 6), "rms_post_ffn")
                    if m == 3:
                        split(i, U_GATE, tick_of(U_PLE))
                    if m == KD - 1:
                        split(i, U_GATE + 1, tick_of(U_PLE + 1))
                    if m >= 3:
                        x_split(m - 3)
                for m in range(KD - 3, KD):
                    x_split(m)
                act.wait_ge(stored_y, i * 32 + 32)
                act.sem_inc(passed, 1)
                act.preload_act_table(ACT.Sigmoid)

                def gate(j, r):
                    act.wait_ge(ticks, tick(i, j * 2 + (tick_of(U_GATE) + r)))
                    act.wait_ge(y_turned, i * KD + j * 2 + (r + 1))
                    act.activation(split2(sig[:, r % 2, :]), halves(G[r % 2]), ACT.Sigmoid)\
                       .then_inc(evacuated[r % 2], 1)

                def copy_y(j, r):
                    act.wait_ge(y_turned, i * KD + j * 2 + (r + 3))
                    cols = bass.ds(j * (2 * P) + r * P, P)
                    act.activation(y_tok[:, :, cols], X[r % 2][:, 0, :].rearrange("p (g c) -> p g c", c=P), ACT.Copy)
                    act.activation(y_small[:, :, cols], X[r % 2][0:SLEN, 1, 0:2 * P].rearrange("p (a c) -> p a c", a=2),
                                   ACT.Copy).then_inc(y_copied, 1)

                gate(0, 0)
                split(i, U_GATE + 2, tick_of(U_GATE))
                gate(0, 1)
                take_x(i + 1, 0)
                take_x(i + 1, 1)
                copy_y(0, 0)
                with act.Fori(0, KD // 2 - 1) as j:
                    for r in (2, 3):
                        n = U_GATE + r + 1
                        parity[0] = r % 2
                        take_x(i + 1, j * 2 + r)
                        parity[0], half_count[0] = n % 2, j * 16 + (n // 2 + 1) * 16
                        split(i, j * 2 + n, j * 2 + (tick_of(U_GATE) + r - 1))
                        gate(j, r)
                        copy_y(j, r - 1)
                act.sem_inc(passed, 1)
                act.preload_act_table_set(LN_EXP)
                act.wait_ge(x_summed, i + 2)
                root(X[1], i, 7).then_inc(x_rms, 1)
                copy_y(0, 7)

            act.wait_ge(last_turned, 1)
            act.activation(turned[0:60, 0, :], X[0][0:60, 0, 0:P], ACT.Copy).then_inc(last_copied, 1)
            act.wait_ge(last_turned, 2)
            act.activation(turned[0:44, 1, :], X[1][0:44, 0, 0:P], ACT.Copy).then_inc(last_copied, 1)


        @block.vector
        def _(dve):
            par = [0]

            def slot(n):
                return n % 2 if isinstance(n, int) else par[0]

            def exact(t):
                return t.bitcast(F32)

            def split(i, n, parts=KD):
                s = slot(n)
                dve.wait_ge(hi_made, i * UNITS + (n + 1))
                dve.tensor_tensor(w_lo[s][:, 0:parts, :], stage[s][:, 0:parts, :], exact(w_hi[s][:, 0:parts, :]),
                                  ALU.subtract).then_inc(lo_made, 1)

            def step(instruction, name):
                vec_.did(instruction, name)

            def own(i, name):
                dve.wait_ge(vec_s, vec_.at(i, name))

            def add_square(i, n):
                dve.wait_ge(squared, i * SQUARES + (n + 1))
                dve.wait_ge(summed, i * SQUARES + (n + 2))
                dve.tensor_tensor(total[:, :], total[:, :], squares[:, slot(n), :], ALU.add).then_inc(summed, 1)

            def sum_x(i, n, k=None):
                if k == 0:
                    dve.wait_ge(squared, i * SQUARES + 1)
                    dve.tensor_copy(total[:, :], squares[:, 0, :]).then_inc(summed, 1)
                else:
                    add_square(i, n)

            starts = [(lo_made, 2), (ticks, 2), (evacuated[0], 1), (evacuated[1], 1), (summed, 2), (tapped, 2),
                      (past_mid, 2), (y_turned, 2), (y_copied, 8), (stored_y, 32), (stored_pool, 16), (stored_gla, 16),
                      (stored_conv, 16), (pe_s, len(PE_STEPS)), (act_s, len(ACT_STEPS)), (vec_s, len(VEC_STEPS)),
                      (pool_s, len(POOL_STEPS))]
            for n, (s_, value) in enumerate(starts):
                dve.memset(started[:, n:n + 1], 0.0).then_inc(s_, value)
            dve.memset(started[:, len(starts):len(starts) + 1], 0.0).then_inc(credited, 1)

            dve.wait_ge(constants_loaded, 16 * CONSTANTS)
            dve.wait_ge(split_once, 2)
            dve.tensor_tensor(w_pool_lo[:, :, :], raw_pool[:, :, :], exact(w_pool_hi[:, :, :]), ALU.subtract)\
               .then_inc(split_once, 1)
            dve.wait_ge(built, BUILT)
            dve.tensor_tensor(w_glow_lo[:, 0:P], raw_glow[:, :, :].rearrange("p k c -> p (k c)"),
                              exact(w_glow_hi[:, 0:P]), ALU.subtract).then_inc(split_once, 1)
            split(0, 0)
            for k in range(KD):
                sum_x(0, k, k)

            with dve.Fori(0, TILES) as i:
                def scaled(m, x, gain, name, before, ready=None):
                    if m >= 2:
                        dve.wait_ge(act_s, act_.at(i, f"{before}_hi{m - 2}"))
                        own(i, f"{before}_lo{m - 2}")
                    elif ready:
                        dve.wait_ge(act_s, act_.at(i, ready))
                    step(dve.scalar_tensor_tensor(normed[:, m % 2, :], x[:, m, :], gains[:, gain, m:m + 1],
                                                  rms[:, :], ALU.mult, ALU.mult), name)

                def rest(m, name, hi_name, own_name):
                    dve.wait_ge(act_s, act_.at(i, hi_name))
                    own(i, own_name)
                    step(dve.tensor_tensor(h_lo[:, m, :], normed[:, m % 2, :], exact(h_hi[:, m, :]),
                                           ALU.subtract), name)

                dve.wait_ge(x_rms, i + 1)
                dve.wait_ge(ticks, tick(i, -1))
                for s in range(KD + 1):
                    if s < KD:
                        scaled(s, x_next, 0, f"h{s}", "h")
                    if s:
                        rest(s - 1, f"h_lo{s - 1}", f"h_hi{s - 1}", f"h{s - 1}")

                def gap_step(h):
                    v = level_view(cum, h)
                    mid = v[:, :, :, h - 1:h].broadcast_to(list(v.shape))
                    step(dve.tensor_tensor(level_view(gap, h), v, mid, ALU.subtract), f"gap{h}")

                def operand_step(h, n):
                    dve.wait_ge(act_s, act_.at(i, f"decay{h}"))
                    if n >= 2:
                        dve.wait_ge(pe_s, pe_.at(i, f"scores{4 * h}" if 4 * h > 4 else f"small{4 * h}"))
                    elif n == 1:
                        dve.wait_ge(pe_s, pe_.at(i, "diag"))
                    dve.tensor_tensor(level_view(opnd[n % 2], h, 0), level_view(kT, h, 0), level_view(gap, h, 0), ALU.mult)
                    step(dve.tensor_tensor(level_view(opnd[n % 2], h, 1), level_view(qT, h, 1), level_view(gap, h, 1),
                                           ALU.mult), f"operand{h}")

                def take_scores(h, x, before):
                    dve.wait_ge(pe_s, pe_.at(i, f"scores{h}"))
                    own(i, before)
                    dve.sem_inc(passed, 1)
                    nb = 64 // h
                    out = A[:, :, :].rearrange("p r (n w) -> p r n w", w=2 * h)[:, :, :, h:]
                    mask = masks[:, LEVELS.index(h), :].rearrange("p (o n h) -> p o n h", o=1, h=h)
                    data = X[x][:, :, :].rearrange("p b (r n h) -> p (b r) n h", n=nb, h=h)
                    step(dve.copy_predicated(out, mask.broadcast_to([P, 16, nb, h]), data), f"scores{h}")

                def take_small(h, x, before):
                    dve.wait_ge(pe_s, pe_.at(i, f"small{h}"))
                    own(i, before)
                    dve.sem_inc(passed, 1)
                    nb = SLEN // 2 // h
                    for b in range(2):
                        out = A_s[:, 4 * b:4 * b + 4, :].rearrange("p r (n w) -> p r n w", w=2 * h)[:, :, :, h:]
                        mask = masks[0:SLEN, LEVELS.index(h), 0:SLEN // 2].rearrange("p (o n h) -> p o n h", o=1, h=h)
                        data = X[x][0:SLEN, b, 0:16].rearrange("p (r n h) -> p r n h", n=nb, h=h)
                        last = dve.copy_predicated(out, mask.broadcast_to([SLEN, 4, nb, h]), data)
                    step(last, f"small{h}")

                def update_state(c):
                    dve.wait_ge(act_s, act_.at(i, f"out{c}"))
                    if c:
                        own(i, f"state{c - 1}")
                    col = group_cols(c) + P - 1
                    for d in range(2):
                        for b in range(2):
                            r = slice(64 * b, 64 * b + 64)
                            last = dve.scalar_tensor_tensor(
                                S[r, d, :], S[r, d, :], cum[r, d, col:col + 1],
                                X[(c + 1) % 2][r, d, 256 + P * b:256 + P * b + P], ALU.mult, ALU.add)
                    step(last, f"state{c}")

                def extras(s):
                    if s == 1:
                        dve.wait_ge(act_s, act_.at(i, "gk_abs"))
                        for d in range(2):
                            last = dve.tensor_scalar(split2(gap[:, d, :]), halves(X[d]), bias_gk[:, d:d + 1], 0.0,
                                                     ALU.add, ALU.min)
                        step(last, "gk_min")
                        own(i, "gk_min")
                        dve.wait_ge(act_s, act_.at(i, "gk_log"))
                        step(dve.tensor_tensor(gap[:, :, :], gap[:, :, :], opnd[0][:, :, :], ALU.subtract), "gk")
                        own(i, "gk")
                        for d in range(2):
                            step(dve.tensor_tensor_scan(cum[:, d, :], keep[:, :], gap[:, d, :], 0.0, ALU.mult, ALU.add),
                                 f"cumsum{d}")
                    if s == 2:
                        dve.wait_ge(stored_y, i * 32 + 32)
                        dve.wait_ge(act_s, act_.at(i, "pool_history"))
                        dve.wait_ge(pool_s, pool_.before(i, "z_history"))
                        dve.memset(Z[:, :, 0:1], 0.0)
                        dve.memset(Z[:, :, ZS:].rearrange("p g (s t) -> p g s t", s=2)[:, :, :, 0:1], 0.0)
                        dve.tensor_copy(Z[:, :, 1:16], z_past[:, :, 1:16])
                        for q in range(2):
                            last = dve.tensor_copy(Z[:, :, ZS + 24 * q + 1:ZS + 24 * q + 16],
                                                   z_in[:, 60 * q:60 * q + 60].rearrange("p (t g) -> p g t", g=POOLG))
                        step(last, "states")
                    if s == 4:
                        dve.wait_ge(x_moved, i + 1)
                        for o in (2, 3):
                            dve.wait_ge(*evac(i, o))
                        own(i, "cumsum1")
                        step(dve.tensor_tensor(opnd[1][:, :, :], qT[:, :, :], kT[:, :, :], ALU.mult), "qk")
                        gap_step(64)
                        operand_step(64, 0)
                    if s == 5:
                        own(i, "operand64")
                        gap_step(32)
                        dve.wait_ge(pe_s, pe_.at(i, "diag"))
                        diag = X[0][:, :, 0:8].unsqueeze(3).broadcast_to([P, 2, 8, P])
                        eye = ident[:, :].rearrange("p (o q c) -> p o q c", o=1, q=1).broadcast_to([P, 2, 8, P])
                        step(dve.tensor_tensor(A[:, :, :].rearrange("p (b r) t -> p b r t", b=2), eye, diag, ALU.mult),
                             "scores_diag")
                        diag = X[0][0:SLEN, :, 8:12].unsqueeze(3).broadcast_to([SLEN, 2, 4, SLEN])
                        eye = ident[0:SLEN, 0:SLEN].rearrange("p (o q c) -> p o q c", o=1, q=1)\
                            .broadcast_to([SLEN, 2, 4, SLEN])
                        step(dve.tensor_tensor(A_s[:, :, :].rearrange("p (b r) t -> p b r t", b=2), eye, diag, ALU.mult),
                             "scores_small_diag")
                        take_scores(64, 1, "scores_diag")
                        operand_step(32, 1)
                    if 6 <= s <= 10:
                        n = s - 4
                        h = LEVELS[n]
                        own(i, f"operand{2 * h}")
                        gap_step(h)
                        take_scores(2 * h, (n + 0) % 2, f"scores{4 * h}")
                        if 2 * h <= 4:
                            take_small(2 * h, (n + 1) % 2, f"small{4 * h}" if 4 * h <= 4 else "scores_small_diag")
                        operand_step(h, n)
                    if s == 11:
                        own(i, "operand1")
                        v = cum[:, :, :].rearrange("p d (a c) -> p (d a) c", a=2)
                        g = gap[:, :, :].rearrange("p d (a c) -> p (d a) c", a=2)
                        vp = v[:, :, 0:HP].rearrange("p s (b c) -> p s b c", c=P)
                        dve.tensor_tensor(g[:, :, 0:HP].rearrange("p s (b c) -> p s b c", c=P),
                                          vp[:, :, :, P - 1:P].broadcast_to([P, 4, 2, P]), vp, ALU.subtract)
                        step(dve.tensor_tensor(g[:, :, HP:], v[:, :, HALF - 1:HALF].broadcast_to([P, 4, SLEN]),
                                               v[:, :, HP:], ALU.subtract), "kd_gap")
                        take_scores(1, 1, "scores2")
                        take_small(1, 0, "small2")
                        dve.wait_ge(act_s, act_.at(i, "kd_decay"))
                        step(dve.tensor_tensor(gap[:, :, :], gap[:, :, :], kT[:, :, :], ALU.mult), "kd")
                        dve.wait_ge(act_s, act_.at(i, "cum_decay"))
                        step(dve.tensor_tensor(qT[:, :, :], qT[:, :, :], cum[:, :, :], ALU.mult), "qb")
                    if s == 13:
                        update_state(0)
                        pooled()
                    if s == 14:
                        update_state(1)
                        u_rest(0)
                        u_rest(1)
                    if s == 15:
                        update_state(2)

                def pooled():
                    dve.wait_ge(pool_s, pool_.at(i, "window16"))
                    for w_, first in ((win_a, 0), (win_b, 1)):
                        early = w_[:, first:POOLG:2, 16:32]
                        last = dve.tensor_tensor(early, early, edge[:, first:POOLG:2, :], ALU.mult)
                    step(last, "edges_scaled")
                    own(i, "edges_scaled")
                    for w_, first in ((win_a, 0), (win_b, 1)):
                        early = w_[:, first:POOLG:2, 16:32]
                        last = dve.tensor_tensor(early, early, Z[:, first:POOLG:2, 16:32], ALU.subtract)
                    step(last, "u_early")
                    for g, w in enumerate(WINDOWS):
                        dst = (win_a if g % 2 == 0 else win_b)[:, g, 32:]
                        step(dve.scalar_tensor_tensor(dst, dst, 1.0 / w, Z[:, g, 32:], ALU.mult, ALU.subtract), f"u{g}")

                def u_rest(g):
                    dve.wait_ge(act_s, act_.at(i, f"u_hi{g}"))
                    own(i, f"u{g}")
                    w = win_a if g % 2 == 0 else win_b
                    lo, hi = split2(u_lo[:, g % 2, :]), split2(exact(u_hi[:, g % 2, :]))
                    dve.tensor_tensor(lo[:, :, 0:HP], w[:, g, 16:ZS].rearrange("p (a c) -> p a c", a=2),
                                      hi[:, :, 0:HP], ALU.subtract)
                    step(dve.tensor_tensor(lo[:, :, HP:], w[:, g, ZS:].rearrange("p (a c) -> p a c", a=2)[:, :, 16:],
                                           hi[:, :, HP:], ALU.subtract), f"u_lo{g}")

                def pool_rest(g):
                    dve.wait_ge(act_s, act_.at(i, f"mix_hi{g}"))
                    step(dve.scalar_tensor_tensor(split2(h_lo[:, g, :]), halves(X[1]), scale_pool[:, g:g + 1],
                                                  split2(exact(h_hi[:, g, :])), ALU.mult, ALU.subtract), f"mix_lo{g}")

                for m in range(16):
                    split(i, m + 1)
                    extras(m)
                split(i, U_O + 1)
                update_state(3)
                pool_rest(0)
                u_rest(2)
                pool_rest(1)
                u_rest(3)
                dve.wait_ge(pe_s, pe_.at(i, "state_small"))
                for a in range(2):
                    for d in range(2):
                        for b in range(2):
                            r = slice(64 * b, 64 * b + 64)
                            col = HALF * a + HALF - 1
                            last = dve.scalar_tensor_tensor(
                                S_s[r, a, d, :], S_s[r, a, d, :], cum[r, d, col:col + 1],
                                X[0][r, a, 256 * d + P * b:256 * d + P * b + P], ALU.mult, ALU.add)
                step(last, "state_small")
                pool_rest(2)
                for h in range(HEADS + 1):
                    if h < HEADS:
                        dve.wait_ge(act_s, act_.at(i, f"rms_head{h}"))
                        step(dve.scalar_tensor_tensor(outT[:, h, :], outT[:, h, :], gain_head[:, 0:1],
                                                      squares[:, h % 2, :], ALU.mult, ALU.mult), f"out_scaled{h}")
                        own(i, f"out_scaled{h}")
                        step(dve.tensor_tensor(outT[:, h, :], outT[:, h, :], ogT[:, h, :], ALU.mult), f"out_gated{h}")
                    if h == 0:
                        pool_rest(3)
                    else:
                        dve.wait_ge(act_s, act_.at(i, f"mix_hi{3 + h}"))
                        step(dve.tensor_tensor(h_lo[:, 3 + h, :], outT[:, h - 1, :], exact(h_hi[:, 3 + h, :]),
                                               ALU.subtract), f"mix_lo{3 + h}")

                step(dve.memset(total[:, :], 0.0), "zeros_mix")
                own(i, "zeros_mix")
                dve.sem_inc(passed, 1)
                with dve.Fori(0, KD // 2) as j:
                    for r in range(2):
                        par[0] = r
                        add_square(i, j * 2 + (8 + r))
                        split(i, j * 2 + (U_O + r + 2))
                dve.wait_ge(act_s, act_.at(i, "rms_post_mix"))
                for s in range(KD + 1):
                    if s < KD:
                        step(dve.scalar_tensor_tensor(mixed[:, s, :], mixed[:, s, :], gains[:, 1, s:s + 1], rms[:, :],
                                                      ALU.mult, ALU.mult), f"mixed{s}")
                    if 1 <= s <= KD:
                        own(i, f"mixed{s - 1}")
                        if s == 1:
                            dve.wait_ge(x_moved, i + 1)
                        step(dve.tensor_tensor(xT[:, s - 1, :], xT[:, s - 1, :], mixed[:, s - 1, :], ALU.add),
                             f"x_mixed{s - 1}")
                for s in range(KD + 1):
                    if s < KD:
                        scaled(s, xT, 2, f"f{s}", "f", "rms_pre_ffn")
                    if s:
                        rest(s - 1, f"f_lo{s - 1}", f"f_hi{s - 1}", f"f{s - 1}")

                def ffn_block(f, last=False):
                    par[0] = 0
                    split(i, f * 2 + (U_UP + 2))
                    dve.wait_ge(evacuated[0], i * (OUTS // 2) + f + (O_UP // 2 + 2))
                    dve.wait_ge(past_mid, i * (2 * NF) + f * 2 + 3)
                    for t in (1, 0):
                        dve.scalar_tensor_tensor(cg[:, :, :], gx[:, :, t:t + 266], taps[:, t, bass.ds(f, 1)], cg[:, :, :],
                                                 ALU.mult, ALU.add).then_inc(tapped, 1)
                        if t:
                            dve.wait_ge(tapped, i * (2 * NF) + f * 2 + 3)
                    dve.wait_ge(gelu_made, i * NF + f + 1)
                    dve.wait_ge(ticks, tick(i, f * 2 + (U_UP + 1)))
                    y2 = split2(yf[:, :])
                    dve.tensor_tensor(y2[:, :, 0:HP], cg[:, :, 0:HP], G[1][:, :, 0:HP], ALU.mult)
                    dve.tensor_tensor(y2[:, :, HP:], cg[:, :, HP + 2:], G[1][:, :, HP:HALF], ALU.mult)\
                       .then_inc(evacuated[1], 1)
                    if not last:
                        par[0] = 1
                        split(i, f * 2 + (U_UP + 3))
                    dve.wait_ge(hidden_hi, i * NF + f + 1)
                    dve.tensor_tensor(y_lo[:, bass.ds(f, 1), :].rearrange("p o c -> p (o c)"), yf[:, :],
                                      exact(y_hi[:, bass.ds(f, 1), :]).rearrange("p o c -> p (o c)"),
                                      ALU.subtract).then_inc(hidden_lo, 1)

                with dve.Fori(0, NF - 1) as f:
                    ffn_block(f)
                ffn_block(NF - 1, last=True)

                def p_rest(x, cols, name):
                    dve.wait_ge(act_s, act_.at(i, f"p_hi{name}"))
                    for b in range(2):
                        last = dve.tensor_tensor(p_lo[:, :, cols[b]:cols[b] + P],
                                                 X[x][:, b, 0:256].rearrange("p (k c) -> p k c", k=2),
                                                 exact(p_hi[:, :, cols[b]:cols[b] + P]), ALU.subtract)
                    step(last, f"p_lo{name}")

                dve.wait_ge(past_mid, i * (2 * NF) + (2 * NF + 2))
                p_rest(0, (group_cols(0), group_cols(1)), "01")
                p_rest(1, (group_cols(2), group_cols(3)), "23")
                dve.wait_ge(act_s, act_.at(i, "p_hi_small"))
                step(dve.tensor_tensor(p_lo[:, :, :].rearrange("p k (a c) -> p k a c", a=2)[:, :, :, HP:],
                                       X[0][:, 0, 0:32].rearrange("p (k a c) -> p k a c", k=2, a=2),
                                       exact(p_hi[:, :, :]).rearrange("p k (a c) -> p k a c", a=2)[:, :, :, HP:],
                                       ALU.subtract), "p_lo_small")
                step(dve.memset(total[:, :], 0.0), "zeros_ffn")
                own(i, "zeros_ffn")
                dve.sem_inc(passed, 1)
                with dve.Fori(0, KD // 2) as j:
                    for r in range(6):
                        par[0] = (r + 1) % 2
                        split(i, j * 6 + (U_DOWN + r + 1), DOWN_PARTS[(r + 1) % 3][1])
                        if r % 3 == 2:
                            par[0] = r // 3
                            add_square(i, j * 2 + (24 + r // 3))
                split(i, U_PLE + 1)
                dve.wait_ge(act_s, act_.at(i, "rms_post_ffn"))
                for s in range(KD + 2):
                    if s == 3:
                        split(i, U_GATE)
                    if s == 5:
                        split(i, U_GATE + 1)
                    if s < KD:
                        step(dve.scalar_tensor_tensor(ffn_out[:, s, :], ffn_out[:, s, :], gains[:, 3, s:s + 1],
                                                      rms[:, :], ALU.mult, ALU.mult), f"ffn{s}")
                    if 1 <= s <= KD:
                        own(i, f"ffn{s - 1}")
                        step(dve.tensor_tensor(xT[:, s - 1, :], xT[:, s - 1, :], ffn_out[:, s - 1, :], ALU.add),
                             f"x_ffn{s - 1}")
                    if s >= 2:
                        dve.wait_ge(act_s, act_.at(i, f"x_hi{s - 2}"))
                        step(dve.tensor_tensor(h_lo[:, s - 2, :], xT[:, s - 2, :], exact(h_hi[:, s - 2, :]),
                                               ALU.subtract), f"x_lo{s - 2}")

                def gate(j, r):
                    if isinstance(j, int):
                        flat = lambda t: t[:, r, :]
                    else:
                        flat = lambda t: t[:, bass.ds(j * 2 + r, 1), :].rearrange("p o c -> p (o c)")
                    dve.wait_ge(evacuated[r % 2], i * (OUTS // 2) + j + ((O_GATE + r) // 2 + 2))
                    dve.tensor_tensor(sig[:, r % 2, :], sig[:, r % 2, :], flat(ple), ALU.mult).then_inc(gated, 1)
                    dve.wait_ge(gated, i * KD + j * 2 + (r + 1))
                    dve.tensor_tensor(sig[:, r % 2, :], flat(xT), sig[:, r % 2, :], ALU.add).then_inc(added, 1)

                gate(0, 0)
                split(i, U_GATE + 2)
                gate(0, 1)
                sum_x(i + 1, 0, 0)
                sum_x(i + 1, 1)
                with dve.Fori(0, KD // 2 - 1) as j:
                    for r in (2, 3):
                        par[0] = r % 2
                        sum_x(i + 1, j * 2 + r)
                        par[0] = (r + 1) % 2
                        split(i, j * 2 + (U_GATE + r + 1))
                        gate(j, r)
        @block.tensor
        def _(pe):
            drained = {0: None, 1: None}

            def use(i, x, steps, name):
                if drained[x]:
                    s, n = drained[x]
                    pe.wait_ge(s.sem, s.at(i, n))
                drained[x] = (steps, name)

            def product(ps, lhs_hi, lhs_lo, rhs_hi, rhs_lo, start=True, stop=True):
                for n, (l, r) in enumerate(((lhs_hi, rhs_hi), (lhs_lo, rhs_hi), (lhs_hi, rhs_lo))):
                    for a in range(2):
                        last = pe.matmul(ps[:, a, 0:HALF], l, r[:, HALF * a:HALF * a + HALF],
                                         start=start and n == 0, stop=stop and n == 2)
                return last

            def unit(i, n, s, o, hi, lo, first=0, parts=KD, start=True, stop=True, ready=None):
                pe.wait_ge(lo_made, i * UNITS + (n + 3))
                if start:
                    pe.wait_ge(evacuated[o[0]], i * (OUTS // 2) + o[1])
                for k in range(parts):
                    if ready:
                        pe.wait_ge(vec_s, vec_.at(i, ready(k)))
                    last = product(G[o[0]], w_hi[s][:, k, :], w_lo[s][:, k, :], hi[:, first + k, :],
                                   lo[:, first + k, :], start and k == 0, stop and k == parts - 1)
                last.then_inc(ticks, 1)

            def unit_pair(i, n, o, hi, lo, ready):
                for s in range(2):
                    pe.wait_ge(lo_made, i * UNITS + (n + s + 3))
                    pe.wait_ge(evacuated[s], i * (OUTS // 2) + out_of(o)[1])
                for k in range(KD):
                    pe.wait_ge(vec_s, vec_.at(i, ready(k)))
                    for s in range(2):
                        last = product(G[s], w_hi[s][:, k, :], w_lo[s][:, k, :], hi[:, k, :], lo[:, k, :],
                                       k == 0, k == KD - 1)
                        if k == KD - 1:
                            last.then_inc(ticks, 1)

            def out_of(o):
                return o % 2, o // 2 + 1

            def ones_sum(x, src):
                for a in range(2):
                    last = pe.matmul(X[x][:, a, 0:HALF], ones[:, :], src[:, HALF * a:HALF * a + HALF],
                                     start=True, stop=True)
                return last

            def turn(out, in_, n=P):
                return pe.transpose(out, in_, ident[0:n, 0:n])

            pe.wait_ge(built, BUILT)
            pe.wait_ge(split_once, 4)
            pe.wait_ge(credited, 1)

            def turn_x(k, x):
                cols = slice(k * P, k * P + P)
                for g in range(NG):
                    turn(X[x][:, g // 2, P * (g % 2):P * (g % 2) + P], x_tok[:, g, cols])
                for a in range(2):
                    last = turn(X[x][:, a, HP:HALF], x_small[:, a, cols], SLEN)
                last.then_inc(x_turned, 1)

            pe.wait_ge(x_loaded, 16 * (NG + 1))
            for k in range(KD):
                if k >= 2:
                    pe.wait_ge(squared, k - 1)
                turn_x(k, k % 2)
            pe.wait_ge(summed, 8 + 2)
            pe.wait_ge(squared, KD)
            ones_sum(1, total).then_inc(x_summed, 1)

            with pe.Fori(0, TILES) as i:
                drained[0] = drained[1] = None
                pe.wait_ge(states_loaded, i * 32 + 32)
                pe.wait_ge(y_copied, i * 8 + 8)
                use(i, 0, act_, "conv_state")
                turn(X[0][:, 0, 0:120], z_state_tok[:, :], 120)
                pe_.did(turn(X[0][:, 1, 0:4 * NF], g_state_tok[:, :], 4 * NF), "states_turned")
                use(i, 1, act_, "glow")
                pe.wait_ge(x_rms, i + 1)
                pe.wait_ge(lo_made, i * UNITS + 3)
                pe.wait_ge(evacuated[0], i * (OUTS // 2) + 1)
                for k in range(KD):
                    pe.wait_ge(vec_s, vec_.at(i, f"h_lo{k}"))
                    last = product(X[1], w_glow_hi[:, RANK * k:RANK * k + P], w_glow_lo[:, RANK * k:RANK * k + P],
                                   h_hi[:, k, :], h_lo[:, k, :], k == 0, k == KD - 1)
                    if k == KD - 1:
                        pe_.did(last, "glow")
                    last = product(G[0], w_hi[0][:, k, :], w_lo[0][:, k, :], h_hi[:, k, :], h_lo[:, k, :],
                                   k == 0, k == KD - 1)
                last.then_inc(ticks, 1)

                def head_rows(b):
                    return slice(64 * b, 64 * b + 64)

                def scores(h, x):
                    use(i, x, vec_, f"scores{h}")
                    t = opnd[LEVELS.index(h) % 2]
                    pe.wait_ge(vec_s, vec_.at(i, f"operand{h}"))
                    for b in range(2):
                        for d in range(2):
                            for c in range(NG):
                                keys = t[head_rows(b), d, group_cols(c):group_cols(c) + P]
                                queries = keys.rearrange("p (n w) -> p n w", w=2 * h)[:, :, h:]
                                col = 64 * (4 * d + c)
                                last = pe.matmul(X[x][:, b, col:col + 64], keys, queries, start=True, stop=True)
                    pe_.did(last, f"scores{h}")

                def small_tokens(t, b, d, a):
                    return t[head_rows(b), d, HALF * a + HP:HALF * a + HALF]

                def small_scores(h, x):
                    use(i, x, vec_, f"small{h}")
                    pe.sem_inc(passed, 1)
                    t = opnd[LEVELS.index(h) % 2]
                    for b in range(2):
                        for d in range(2):
                            for a in range(2):
                                keys = small_tokens(t, b, d, a)
                                queries = keys.rearrange("p (n w) -> p n w", w=2 * h)[:, :, h:]
                                col = 4 * (2 * d + a)
                                last = pe.matmul(X[x][0:SLEN, b, col:col + 4], keys, queries, start=True, stop=True)
                    pe_.did(last, f"small{h}")

                def out_chunk(c):
                    x = (c + 1) % 2
                    use(i, x, act_, f"out{c}")
                    pe.wait_ge(vec_s, vec_.at(i, f"state{c - 1}" if c else "qb"))
                    cols = slice(group_cols(c), group_cols(c) + P)
                    for h in range(HEADS):
                        d, b = h // 2, h % 2
                        out = X[x][:, b, P * d:P * d + P]
                        pe.matmul(out, v_tok[:, c, P * h:P * h + P], A[:, 8 * b + 4 * d + c, :],
                                  start=True, stop=False)
                        pe.matmul(out, S[head_rows(b), d, :], qT[head_rows(b), d, cols], start=False, stop=True)
                    for d in range(2):
                        last = pe.matmul(X[x][:, d, 256:512], kd_tok[:, c, d, :],
                                         v_tok[:, c, 256 * d:256 * d + 256], start=True, stop=True)
                    pe_.did(last, f"out{c}")

                def pool_group(g, ready=None):
                    use(i, 1, vec_, f"mix_lo{g}")
                    if ready:
                        pe.wait_ge(vec_s, vec_.at(i, ready))
                    pe_.did(product(X[1], w_pool_hi[:, g, :], w_pool_lo[:, g, :], u_hi[:, g % 2, :], u_lo[:, g % 2, :]),
                            f"pool{g}")

                def extras(s):
                    if s == 0:
                        pe.wait_ge(act_s, act_.at(i, "glow"))
                        for d in range(2):
                            use(i, d, vec_, "gk_min")
                            for a in range(2):
                                last = pe.matmul(X[d][:, a, 0:HALF], w_gk[:, P * d:P * d + P],
                                                 squares[0:RANK, 0, HALF * a:HALF * a + HALF], start=True, stop=True)
                            pe_.did(last, f"gk{d}")
                    if s == 4:
                        use(i, 0, vec_, "scores_small_diag")
                        pe.wait_ge(vec_s, vec_.at(i, "qk"))
                        for b in range(2):
                            for d in range(2):
                                for c in range(NG):
                                    pe.matmul(X[0][:, b, 4 * d + c:4 * d + c + 1],
                                              opnd[1][head_rows(b), d, group_cols(c):group_cols(c) + P],
                                              ones[head_rows(b), 0:1], start=True, stop=True)
                                for a in range(2):
                                    col = 8 + 2 * d + a
                                    last = pe.matmul(X[0][0:SLEN, b, col:col + 1], small_tokens(opnd[1], b, d, a),
                                                     ones[head_rows(b), 0:1], start=True, stop=True)
                        pe_.did(last, "diag")
                        scores(64, 1)
                    if 5 <= s <= 10:
                        n = s - 4
                        h = LEVELS[n]
                        scores(h, (n + 1) % 2)
                        if h <= 4:
                            small_scores(h, n % 2)
                    if s in (8, 9):
                        if s == 8:
                            for o in (6, 7):
                                pe.wait_ge(*evac(i, o))
                        pe.wait_ge(*evac(i, s))
                        for c in (2 * s - 16, 2 * s - 15):
                            for h in range(HEADS):
                                last = turn(G[s % 2][:, c % 2, P * h:P * h + P],
                                            vT[:, h, group_cols(c):group_cols(c) + P])
                        pe_.did(last, f"v_turned{s - 8}")
                    if s == 10:
                        pe.wait_ge(*evac(i, s))
                        for a in range(2):
                            for h in range(HEADS):
                                last = turn(G[0][0:SLEN, a, P * h:P * h + P], vT[:, h, HALF * a + HP:HALF * a + HALF])
                        pe_.did(last, "v_small_turned")
                    if s == 11:
                        use(i, 1, act_, "kd_copied")
                        pe.wait_ge(vec_s, vec_.at(i, "kd"))
                        for c in range(NG):
                            for d in range(2):
                                last = turn(X[1][:, c // 2, P * (2 * (c % 2) + d):P * (2 * (c % 2) + d) + P],
                                            gap[:, d, group_cols(c):group_cols(c) + P])
                        pe_.did(last, "kd_turned")
                        use(i, 0, act_, "kd_small")
                        for a in range(2):
                            for d in range(2):
                                col = P * (2 * a + d)
                                last = turn(X[0][0:SLEN, 0, col:col + P], gap[:, d, HALF * a + HP:HALF * a + HALF])
                        pe_.did(last, "kd_small_turned")
                    if s >= 12:
                        out_chunk(s - 12)

                for m in range(16):
                    if 10 <= m <= 12:
                        pe.wait_ge(act_s, act_.at(i, ("v_copied0", "v_copied1", "v_small")[m - 10]))
                    if m:
                        unit(i, m, m % 2, out_of(m), h_hi, h_lo)
                    extras(m)
                pool_group(0, "state2")
                use(i, 0, act_, "out_small")
                pe.wait_ge(vec_s, vec_.at(i, "state3"))
                pe.wait_ge(s_loaded, i * 16 + 16)
                for h in range(HEADS):
                    d, b = h // 2, h % 2
                    for a in range(2):
                        out = X[0][:, b, 16 * d + 8 * a:16 * d + 8 * a + 8]
                        pe.matmul(out, v_small[:, a, P * h:P * h + P], A_s[:, 4 * b + 2 * d + a, :],
                                  start=True, stop=False)
                        last = pe.matmul(out, S_s[head_rows(b), a, d, :],
                                         qT[head_rows(b), d, HALF * a + HP:HALF * a + HALF], start=False, stop=True)
                pe_.did(last, "out_small")
                pool_group(1)
                use(i, 0, vec_, "state_small")
                for a in range(2):
                    for d in range(2):
                        last = pe.matmul(X[0][:, a, 256 * d:256 * d + 256], kd_small[:, a, P * d:P * d + P],
                                         v_small[:, a, 256 * d:256 * d + 256], start=True, stop=True)
                pe_.did(last, "state_small")
                pool_group(2)
                for h in range(HEADS):
                    use(i, HEAD_BANKS[h], act_, f"rms_head{h}")
                    if h == 0:
                        pe.wait_ge(act_s, act_.at(i, "out_squares"))
                    pe_.did(ones_sum(HEAD_BANKS[h], out_sq[:, h, :]), f"head{h}")
                    if h == 0:
                        pool_group(3)
                use(i, 1, act_, "pool_state")
                pe.wait_ge(pool_s, pool_.at(i, "z_tail"))
                pe_.did(turn(X[1][0:120, 0, 0:P], z_state[:, :]), "pool_state_turned")

                def mixed_block(k):
                    return f"mix_lo{k}"

                unit_pair(i, U_O, O_O, h_hi, h_lo, mixed_block)
                with pe.Fori(0, KD // 2 - 1) as j:
                    for r in (2, 3):
                        unit(i, j * 2 + (U_O + r), r % 2, (r % 2, j + ((O_O + r) // 2 + 1)), h_hi, h_lo)
                use(i, 1, act_, "rms_post_mix")
                pe.wait_ge(summed, i * SQUARES + (16 + 2))
                pe_.did(ones_sum(1, total), "sum_post_mix")
                use(i, 0, act_, "rms_pre_ffn")
                for m in range(KD):
                    pe.wait_ge(squared, i * SQUARES + (16 + m + 1))
                    for a in range(2):
                        last = pe.matmul(X[0][:, a, 0:HALF], ones[:, :], squares[:, m % 2, HALF * a:HALF * a + HALF],
                                         start=m == 0, stop=m == KD - 1)
                    last.then_inc(summed, 1)

                unit_pair(i, U_UP, O_UP, h_hi, h_lo, lambda k: f"f_lo{k}")
                with pe.Fori(0, NF - 1) as f:
                    for r in (2, 3):
                        unit(i, f * 2 + (U_UP + r), r % 2, (r % 2, f + ((O_UP + r) // 2 + 1)), h_hi, h_lo)

                pe.wait_ge(p_loaded, i * 32 + 32)
                for n in range(2):
                    use(i, n, vec_, f"p_lo{'01' if n == 0 else '23'}")
                    for b in range(2):
                        for k in range(2):
                            last = turn(X[n][:, b, P * k:P * k + P], p_tok[:, 2 * n + b, P * k:P * k + P])
                    pe_.did(last, f"p_turned{'01' if n == 0 else '23'}")
                use(i, 0, vec_, "p_lo_small")
                pe.sem_inc(passed, 1)
                for k in range(2):
                    last = turn(X[0][:, 0, 16 * k:16 * k + 16], p_small[:, P * k:P * k + P], 16)
                pe_.did(last, "p_turned_small")
                use(i, 1, act_, "conv_out")
                pe.wait_ge(past_mid, i * (2 * NF) + (2 * NF + 2))
                pe_.did(turn(X[1][0:88, 0, 0:P], g_tail[:, :, :, :].rearrange("p s t f -> p (s t f)")),
                        "conv_state_turned")
                pe.wait_ge(hidden_lo, i * NF + NF)
                pe.sem_inc(passed, 1)
                with pe.Fori(0, KD // 2) as j:
                    for r in range(6):
                        first, parts = DOWN_PARTS[r % 3]
                        unit(i, j * 6 + (U_DOWN + r), r % 2, (r // 3, j + (O_DOWN // 2 + 1)), y_hi, y_lo,
                             first, parts, r % 3 == 0, r % 3 == 2)
                use(i, 0, act_, "rms_post_ffn")
                for m in range(KD):
                    s, q = m // 4, m % 4
                    if q == 0:
                        pe.wait_ge(lo_made, i * UNITS + (U_PLE + s + 3))
                    if m == 1:
                        pe.wait_ge(summed, i * SQUARES + (32 + 2))
                        pe_.did(ones_sum(0, total), "sum_post_ffn")
                    pair, free = out_of(O_PLE + m)
                    pe.wait_ge(evacuated[pair], i * (OUTS // 2) + free)
                    for k in range(2):
                        last = product(G[pair], w_hi[s][:, 4 * k + q, :], w_lo[s][:, 4 * k + q, :],
                                       p_hi[:, k, :], p_lo[:, k, :], k == 0, k == 1)
                    last.then_inc(ticks, 1)

                def turn_y(r):
                    pe.wait_ge(added, i * KD + (r + 1))
                    pe.wait_ge(squared, (i + 1) * SQUARES + (r + 1))
                    x = r % 2
                    block_ = sig[:, x, :]
                    for c in range(NG):
                        turn(X[x][:, 0, P * c:P * c + P], block_[:, group_cols(c):group_cols(c) + P])
                    for a in range(2):
                        last = turn(X[x][0:SLEN, 1, P * a:P * a + P], block_[:, HALF * a + HP:HALF * a + HALF])
                    last.then_inc(y_turned, 1)

                unit_pair(i, U_GATE, O_GATE, h_hi, h_lo, lambda k: f"x_lo{k}")
                for x in range(2):
                    steps, n = drained[x]
                    pe.wait_ge(steps.sem, steps.at(i, n))
                pe.sem_inc(passed, 1)
                pe.wait_ge(x_loaded, (i + 2) * (16 * (NG + 1)))
                turn_x(0, 0)
                turn_x(1, 1)
                turn_y(0)
                for m in range(2, KD):
                    pe.wait_ge(y_copied, i * 8 + (m + 7))
                    turn_x(m, m % 2)
                    unit(i, U_GATE + m, m % 2, out_of(O_GATE + m), h_hi, h_lo)
                    turn_y(m - 1)
                pe.wait_ge(summed, (i + 1) * SQUARES + (8 + 2))
                ones_sum(1, total).then_inc(x_summed, 1)
                pe.wait_ge(x_rms, i + 2)
                turn_y(7)

            pe.wait_ge(y_copied, TILES * 8 + 8)
            pe.wait_ge(last_packed, 1)
            turn(X[0][0:60, 0, 0:P], z_state[:, 0:60]).then_inc(last_turned, 1)
            turn(X[1][0:44, 0, 0:P], g_past[:, :, :].rearrange("p t f -> p (t f)")).then_inc(last_turned, 1)


_INS = ['x_prompt', 'x_sample', 'state_pool', 'state_gla', 'state_conv', 'p_prompt', 'p_sample', 'g_pre_mix',
        'w_in', 'w_gk2', 'b_gk2', 'w_pool', 'pool_scale', 'gla_norm', 'w_o', 'g_post_mix', 'g_pre_ffn', 'w_up',
        'w_conv', 'b_conv', 'w_down', 'g_post_ffn', 'w_ple', 'w_ple_gate']
_OUTS = [(1, SEQ, D), (NSEQ, SLEN, D), (1, 1, HIST, POOLW), (1, 1, HEADS, KDIM, VDIM), (1, 1, 2, FF),
         (1, NSEQ, HIST, POOLW), (1, NSEQ, HEADS, KDIM, VDIM), (1, NSEQ, 2, FF)]


def kernel(**inputs):
    import numpy as _np
    import concourse.bacc as _bacc
    from concourse.bass_utils import run_bass_kernel_spmd as _run

    nc = _bacc.Bacc("TRN2", target_bir_lowering=False, num_devices=1)
    arrays, args = {}, []
    for name in _INS:
        a = _np.ascontiguousarray(inputs[name])
        arrays[f"in_{name}_dram"] = a
        args.append(nc.dram_tensor(f"in_{name}_dram", a.shape, F32, kind="ExternalInput").ap())
    for n, shape in enumerate(_OUTS):
        args.append(nc.dram_tensor(f"out_{n}_dram", shape, F32, kind="ExternalOutput").ap())
    hybrid_layer(nc, *args)
    r = _run(nc, [arrays], core_ids=[0])
    return tuple(r.results[0][f"out_{n}_dram"] for n in range(len(_OUTS)))
```

```python
from contextlib import ExitStack

import concourse.bass as bass
from concourse import mybir

F32 = mybir.dt.float32
F32R = mybir.dt.float32r
U8 = mybir.dt.uint8
ALU = mybir.AluOpType
ACT = mybir.ActivationFunctionType

P = 128
D = 1024
KD = D // P
SEQ, NSEQ, SLEN = 2048, 8, 8
TILES = 4
TOK = SEQ // TILES
HP = TOK // 2
HALF = HP + SLEN
T = 2 * HALF
NG = 4
POOLW, POOLG, HIST = 512, 4, 15
WINDOWS = (2, 4, 8, 16)
HEADS, KDIM, VDIM = 4, 64, 128
RANK = 16
FF = 2816
NF = FF // P
PLE = 256
EPS = 1e-6
LN_EXP = "natural_log_exp_and_others"
GATE_NORM = 16.0
ZS = 16 + TOK
ZW = ZS + 2 * 24
LEVELS = (64, 32, 16, 8, 4, 2, 1)

W_IN_COLS = ([768, 896] + [512, 640] + [1024 + P * j for j in range(4)] + [P * j for j in range(4)]
             + [1552 + P * j for j in range(4)])
GLOW_COL = 1536
U_IN, U_O, U_UP, U_DOWN, U_PLE, U_GATE, UNITS = 0, 16, 24, 68, 92, 94, 102
DOWN_PARTS = ((0, 8), (8, 7), (15, 7))
TICKS = 108
OUTS = 92
O_IN, O_O, O_UP, O_DOWN, O_PLE, O_GATE = 0, 16, 24, 68, 76, 84


def tick_of(unit):
    if unit < U_PLE:
        return unit
    if unit < U_GATE:
        return U_PLE + 4 * (unit - U_PLE) + 3
    return unit + 6


class Steps:

    def __init__(self, sem, names):
        self.sem, self.names, self.next = sem, list(names), 0
        assert len(set(self.names)) == len(self.names)

    def did(self, instruction, name):
        assert self.names[self.next] == name, (self.names[self.next], name)
        self.next += 1
        instruction.then_inc(self.sem, 1)

    def at(self, i, name):
        return (i + 1) * len(self.names) + self.names.index(name) + 1

    def before(self, i, name):
        return i * len(self.names) + self.names.index(name) + 1


def staggered(*kinds, n=KD):
    return [f"{kind}{s - d}" for s in range(n + len(kinds) - 1) for d, kind in enumerate(kinds)
            if 0 <= s - d < n]


POOL_ADDS = (1, 3, 4, 6)
POOL_RESTS = (1, 3, 5)
PE_STEPS = (
    ["states_turned", "glow", "gk0", "gk1", "diag", "scores64", "scores32", "scores16", "scores8",
     "scores4", "small4", "v_turned0", "scores2", "small2", "v_turned1", "scores1", "small1",
     "v_small_turned", "kd_turned", "kd_small_turned", "out0", "out1", "out2", "out3", "pool0",
     "out_small", "pool1", "state_small", "pool2", "head0", "pool3", "head1", "head2", "head3",
     "pool_state_turned", "o_half", "p_turned01", "p_turned23",
     "sum_post_ffn"]
)
ACT_STEPS = (
    [f"h_hi{m}" for m in range(KD)]
    + ["pool_history", "conv_state", "glow", "gk_abs", "gk_exp", "gk_log", "decay64", "decay32",
       "decay16", "decay8", "decay4", "v_copied0", "decay2", "v_copied1", "decay1", "v_small",
       "kd_decay", "cum_decay", "kd_copied", "kd_small", "out0", "out1", "u_hi0", "u_hi1", "out2", "silu",
       "out3", "mix_hi0", "u_hi2", "out_small", "mix_hi1", "u_hi3", "out_squares", "mix_hi2",
       "rms_head0", "mix_hi3", "rms_head1", "mix_hi4", "rms_head2", "mix_hi5", "rms_head3", "mix_hi6",
       "mix_hi7", "pool_state", "rms_post_mix0", "rms_post_mix1", "rms_pre_ffn0", "f_hi_h0_0",
       "f_hi_h0_1", "rms_pre_ffn1"]
    + [f"f_hi_h0_{m}" for m in range(2, KD)] + [f"f_hi_h1_{m}" for m in range(KD)]
    + ["p_hi01", "p_hi_small", "p_hi23", "conv_out", "rms_post_ffn"] + [f"x_hi{m}" for m in range(KD)]
)
VEC_STEPS = (
    staggered("h", "h_lo")
    + ["gk_min", "gk", "cumsum0", "cumsum1", "states", "qk", "gap64", "operand64",
       "gap32", "scores_diag", "scores_small_diag", "scores64", "operand32",
       "gap16", "scores32", "operand16", "gap8", "scores16", "operand8", "gap4", "scores8", "operand4",
       "gap2", "scores4", "small4", "operand2", "gap1", "scores2", "small2", "operand1",
       "kd_gap", "scores1", "small1", "kd", "qb", "state0", "edges_scaled", "u_early",
       "u0", "u1", "u2", "u3", "state1", "u_lo0", "u_lo1", "state2", "state3", "mix_lo0", "u_lo2",
       "mix_lo1", "u_lo3", "state_small", "mix_lo2", "out_scaled0", "out_gated0", "mix_lo3",
       "out_scaled1", "out_gated1", "mix_lo4", "out_scaled2", "out_gated2", "mix_lo5",
       "out_scaled3", "out_gated3", "mix_lo6", "mix_lo7", "zeros_mix"]
    + [f"mixed_h{a}_{m}" for a in range(2) for m in range(KD)]
    + [name for a in range(2) for name in staggered(f"f_h{a}_", f"f_lo_h{a}_")
       if name not in [f"f_lo_h{a}_{m}" for m in POOL_RESTS]]
    + ["p_lo01", "p_lo23", "p_lo_small", "zeros_ffn"] 
    + [name for name in staggered("ffn", "x_ffn", "x_lo") if name not in [f"x_ffn{m}" for m in POOL_ADDS]]
)
POOL_STEPS = ["query_zeros", "window2", "window4", "window8", "window16", "z_tail", "z_history", "z_edges"] + [
    f"x_mixed_h{a}_{m}" for a in range(2) for m in range(KD)] + [
    f"f_lo_h{a}_{m}" for a in range(2) for m in POOL_RESTS] + [f"x_ffn{m}" for m in POOL_ADDS]
CONSTANTS = 14
BUILT = 3 + 4 * len(LEVELS) + 7 + 1 + 4 + (1 + 3 + 7 + 15) + 3 + 2
HEAD_BANKS = (0, 0, 1, 0)
LAG = 3
CHAIN = 10
SQ_MIX, SQ_HALVES, SQ_X, SQ_FFN, SQUARES = 8, 14, 18, 34, 42


def hybrid_layer(nc, x_prompt, x_sample, state_pool, state_gla, state_conv, p_prompt, p_sample,
                 g_pre_mix, w_in, w_gk2, b_gk2, w_pool, pool_scale, gla_norm, w_o, g_post_mix,
                 g_pre_ffn, w_up, w_conv, b_conv, w_down, g_post_ffn, w_ple, w_ple_gate,
                 y_prompt, y_sample, pool_prompt, gla_prompt, conv_prompt, pool_sample, gla_sample,
                 conv_sample):
    ctx = ExitStack()
    with ctx:
        base = [nc.sbuf_base + 31 & ~31]
        top = nc.sbuf_usable_end

        def at(name, shape, dtype, offset):
            return nc.alloc_sbuf_tensor_at(name, shape, dtype, offset=offset)

        def own(name, shape, dtype=F32):
            n = mybir.dt.size(dtype)
            for s in shape[1:]:
                n *= s
            o = base[0]
            base[0] = (o + n + 31) // 32 * 32
            assert base[0] <= top, (name, base[0], top)
            return at(name, shape, dtype, o)

        def region(words):
            o = base[0]
            base[0] += 4 * words
            assert base[0] <= top, (base[0], top)
            return o

        def placed(start, name, shape, dtype, cursor):
            n = 1
            for s in shape[1:]:
                n *= s
            t = at(name, shape, dtype, start + 4 * cursor[0])
            cursor[0] += (n + 7) // 8 * 8
            return t

        ident = own("ident", [P, P])
        ones = own("ones", [P, P])
        masks = own("masks", [P, len(LEVELS), 64], U8)
        keep = own("keep", [P, T])
        gains = own("gains", [P, 4, KD])
        bias_gk = own("bias_gk", [P, 2])
        scale_pool = own("scale_pool", [P, POOLG])
        gain_head = own("gain_head", [P, 1])
        taps = own("taps", [P, 3, NF])
        bias_conv = own("bias_conv", [P, NF])
        eps = own("eps", [P, 1])
        edge = own("edge", [P, POOLG, 16])
        w_gk = own("w_gk", [RANK, 2 * P])
        w_glow_hi = own("w_glow_hi", [P, KD * RANK + P], F32R)
        w_glow_lo = own("w_glow_lo", [P, KD * RANK + P], F32R)
        w_pool_hi = own("w_pool_hi", [P, POOLG, P], F32R)
        w_pool_lo = own("w_pool_lo", [P, POOLG, P], F32R)
        z_past = own("z_past", [P, POOLG, 16])
        g_past = own("g_past", [P, 2, NF])
        g_state = own("g_state", [P, 2, 2, NF])
        g_tail = own("g_tail", [P, 2, 2, NF])
        S = own("S", [P, 2, P])
        S_s = own("S_s", [P, 2, 2, P])
        z_in = own("z_in", [P, 2 * HIST * POOLG])
        z_state = own("z_state", [P, 2 * HIST * POOLG])
        started = own("started", [1, 32])
        turned = own("turned", [P, 2, P])
        norm_at = region(2 * T + T)
        squares = at("squares", [P, 2, T], F32, norm_at)
        rms = at("rms", [P, T], F32, norm_at + 4 * 2 * T)
        p_tok = at("p_tok", [P, NG, PLE], F32, norm_at)
        p_small = at("p_small", [16, PLE], F32, norm_at + 4 * 2 * T)
        total = own("total", [P, T])
        xT = own("xT", [P, KD, T])

        stage = [own(f"stage{s}", [P, KD, P]) for s in range(2)]
        w_hi = [own(f"w_hi{s}", [P, KD, P], F32R) for s in range(2)]
        w_lo = [own(f"w_lo{s}", [P, KD, P], F32R) for s in range(2)]

        h_at = region(2 * KD * T)
        h_hi = at("h_hi", [P, KD, T], F32R, h_at)
        h_lo = at("h_lo", [P, KD, T], F32R, h_at + 4 * KD * T)
        ffn_out = at("ffn_out", [P, KD, T], F32, h_at)

        scratch = region(3648)
        c = [0]
        A = placed(scratch, "A", [P, 16, P], F32, c)
        A_s = placed(scratch, "A_s", [SLEN, 8, SLEN], F32, c)
        kd_tok = placed(scratch, "kd_tok", [P, NG, 2, P], F32, c)
        kd_small = placed(scratch, "kd_small", [SLEN, 2, 2 * P], F32, c)
        assert c[0] <= 3648, c
        c = [0]
        gx = placed(scratch, "gx", [P, 2, 268], F32, c)
        cg = placed(scratch, "cg", [P, 2, 266], F32, c)
        yf = placed(scratch, "yf", [P, T], F32, c)
        assert c[0] <= 1600
        normed = placed(scratch, "normed", [P, 2, T], F32, [1600])
        c = [0]
        p_lo = placed(scratch, "p_lo", [P, 2, T], F32R, c)
        p_hi = at("p_hi", [P, 2, T], F32R, scratch + 4 * 1600)

        big = region(2 * NF * T)
        y_hi = at("y_hi", [P, NF, T], F32R, big)
        y_lo = at("y_lo", [P, NF, T], F32R, big + 4 * NF * T)
        c = [0]
        kT = placed(big, "kT", [P, 2, T], F32, c)
        qT = placed(big, "qT", [P, 2, T], F32, c)
        vT = placed(big, "vT", [P, HEADS, T], F32, c)
        ogT = placed(big, "ogT", [P, HEADS, T], F32, c)
        Z = placed(big, "Z", [P, POOLG, ZW], F32, c)
        win_a = placed(big, "win_a", [P, POOLG, ZW], F32, c)
        win_b = placed(big, "win_b", [P, POOLG, ZW], F32, c)
        u_hi = placed(big, "u_hi", [P, 2, T], F32R, c)
        u_lo = placed(big, "u_lo", [P, 2, T], F32R, c)
        cum = placed(big, "cum", [P, 2, T], F32, c)
        gap = placed(big, "gap", [P, 2, T], F32, c)
        opnd = [placed(big, f"opnd{n}", [P, 2, T], F32, c) for n in range(2)]
        v_tok = placed(big, "v_tok", [P, NG, HEADS * P], F32, c)
        v_small = placed(big, "v_small", [SLEN, 2, HEADS * P], F32, c)
        assert c[0] <= 2 * NF * T, c
        queries = [at(f"queries{n}", [P, 2, 2, 2, P], F32, big + 4 * (6 * 2 * T + 3 * POOLG * ZW + n * 2 * T))
                   for n in range(2)]
        outT = at("outT", [P, HEADS, T], F32, big + 4 * 2 * (2 * T))
        out_sq = at("out_sq", [P, HEADS, T], F32, big + 4 * (6 * 2 * T + 2 * POOLG * ZW // 2))
        mixed = at("mixed", [P, KD, T], F32, big)
        c = [0]
        x_tok = placed(big, "x_tok", [P, NG, D], F32, c)
        x_small = placed(big, "x_small", [SLEN, 2, D], F32, c)
        y_tok = placed(big, "y_tok", [P, NG, D], F32, c)
        y_small = placed(big, "y_small", [SLEN, 2, D], F32, c)
        ple = placed(big, "ple", [P, KD, T], F32, c)
        sig = placed(big, "sig", [P, 2, T], F32, c)
        z_state_tok = placed(big, "z_state_tok", [2 * HIST * POOLG, P], F32, c)
        g_state_tok = placed(big, "g_state_tok", [4 * NF, P], F32, c)
        assert c[0] <= 2 * NF * T, c
        x_next = at("x_next", [P, KD, T], F32, big + 4 * (2 * NF * T - KD * T))
        assert c[0] <= 2 * NF * T - KD * T
        raw_at = big + 4 * (NG * D + 2 * D)
        raw_pool = at("raw_pool", [P, POOLG, P], F32, raw_at)
        raw_glow = at("raw_glow", [P, KD, RANK], F32, raw_at + 4 * 512)

        G = [ctx.enter_context(nc.psum_tensor(f"G{n}", [P, 2, 512], F32)) for n in range(2)]
        X = [ctx.enter_context(nc.psum_tensor(f"X{n}", [P, 2, 512], F32)) for n in range(2)]

        def halves(ps):
            return ps[:, :, 0:HALF]

        def split2(ap):
            return ap.rearrange("p (a c) -> p a c", a=2)

        def half(a):
            return slice(HALF * a, HALF * a + HALF)

        def normed_half(m):
            return normed[:, m % 2, half(m // 2 % 2)]

        def group_cols(c):
            return HALF * (c // 2) + P * (c % 2)

        def sem(name):
            return ctx.enter_context(nc.semaphore(name))

        constants_loaded = sem("constants_loaded")
        built = sem("built")
        split_once = sem("split_once")
        staged = [sem(f"staged{s}") for s in range(2)]
        hi_made = sem("hi_made")
        lo_made = sem("lo_made")
        ticks = sem("ticks")
        evacuated = [sem(f"evacuated{n}") for n in range(2)]
        squared = sem("squared")
        summed = sem("summed")
        x_loaded, states_loaded, s_loaded, p_loaded = sem("x_loaded"), sem("states_loaded"), sem("s_loaded"), sem("p_loaded")
        stored_y, stored_pool, stored_gla, stored_conv = sem("stored_y"), sem("stored_pool"), sem("stored_gla"), sem("stored_conv")
        gate_copied, past_in, past_mid = sem("gate_copied"), sem("past_in"), sem("past_mid")
        tap_now, tapped = sem("tap_now"), sem("tapped")
        gelu_made, hidden_hi, hidden_lo = sem("gelu_made"), sem("hidden_hi"), sem("hidden_lo")
        gated, added, y_turned, y_copied = sem("gated"), sem("added"), sem("y_turned"), sem("y_copied")
        last_turned, last_copied, last_packed = sem("last_turned"), sem("last_copied"), sem("last_packed")
        pe_s, act_s, vec_s, pool_s = sem("pe_steps"), sem("act_steps"), sem("vec_steps"), sem("pool_steps")
        pe_, act_, vec_, pool_ = (Steps(pe_s, PE_STEPS), Steps(act_s, ACT_STEPS),
                                  Steps(vec_s, VEC_STEPS), Steps(pool_s, POOL_STEPS))
        x_turned, x_moved = sem("x_turned"), sem("x_moved")
        x_summed, x_rms = sem("x_summed"), sem("x_rms")
        logs = sem("logs")
        passed = sem("passed")
        credited = sem("credited")

        def tick(i, n):
            return i * TICKS + (n + 3)

        def evac(i, o):
            return evacuated[o % 2], i * (OUTS // 2) + (o // 2 + 2)

        def f_lo_done(i, a, m):
            name = f"f_lo_h{a}_{m}"
            return (pool_s, pool_.at(i, name)) if m in POOL_RESTS else (vec_s, vec_.at(i, name))

        def level_view(t, h, side=None):
            w = HALF if h <= 4 else HP
            v = t[:, :, :].rearrange("p d (a c) -> p (d a) c", a=2)[:, :, 0:w]
            v = v.rearrange("p s (n w) -> p s n w", w=2 * h)
            return v if side is None else v[:, :, :, h * side:h * side + h]

        block = ctx.enter_context(nc.Block())

        @block.sync
        def _(sp):
            def rows(w, first, n, col):
                return w[first:first + P * n, col].rearrange("(k p) c -> p k c", p=P)

            def load_unit(i, n, src, parts=KD):
                sp.wait_ge(lo_made, i * UNITS + (n + 1))
                sp.sem_inc(passed, 1)
                sp.dma_start(stage[n_mod(n)][:, 0:parts, :], src).then_inc(staged[n_mod(n)], 16)

            def n_mod(n):
                return n % 2 if isinstance(n, int) else n_parity[0]

            n_parity = [0]

            def load_x(tile, groups, small):
                for g in groups:
                    xp = x_prompt[0, bass.ds(tile * TOK + g * P, P), :]
                    sp.dma_start(x_tok[:, g, :], xp).then_inc(x_loaded, 16)
                if small:
                    xs = x_sample.rearrange("b s d -> s b d")[:, bass.ds(tile * 2, 2), :]
                    sp.dma_start(x_small[:, :, :], xs).then_inc(x_loaded, 16)
                    zs = state_pool[0].rearrange("b t (g c) -> (b t g) c", g=POOLG)
                    sp.dma_start(z_state_tok[:, :], zs[bass.ds(tile * 120, 120), :]).then_inc(states_loaded, 16)
                    gs = state_conv[0].rearrange("b t (f c) -> (b t f) c", f=NF)
                    sp.dma_start(g_state_tok[:, :], gs[bass.ds(tile * 88, 88), :]).then_inc(states_loaded, 16)

            load_x(0, range(NG), True)
            n = [0]

            def constant(dst, src):
                sp.dma_start(dst, src).then_inc(constants_loaded, 16)
                n[0] += 16

            with nc.allow_non_contiguous_dma(reason="small vectors, once"):
                constant(raw_glow[:, :, :], rows(w_in[0], 0, KD, slice(GLOW_COL, GLOW_COL + RANK)))
                constant(raw_pool[:, :, :], w_pool[0].rearrange("g c d -> c g d"))
                constant(w_gk[:, :], w_gk2[0])
                for m, g in enumerate((g_pre_mix, g_post_mix, g_pre_ffn, g_post_ffn)):
                    constant(gains[:, m, :], g[0].rearrange("(k p) -> p k", p=P))
                constant(bias_gk[:, :], b_gk2[0].rearrange("(k p) -> p k", p=P))
                constant(scale_pool[:, :], pool_scale[0].rearrange("(k p) -> p k", p=P))
                constant(gain_head[:, :], gla_norm[0].rearrange("(k p) -> p k", p=P))
                for m in range(3):
                    constant(taps[:, m, :], w_conv[0, m].rearrange("(k p) -> p k", p=P))
                constant(bias_conv[:, :], b_conv[0].rearrange("(k p) -> p k", p=P))
            assert n[0] == 16 * CONSTANTS
            load_unit(0, 0, rows(w_in[0], 0, KD, slice(W_IN_COLS[0], W_IN_COLS[0] + P)))

            with sp.Fori(0, TILES) as i:
                sp.wait_ge(stored_gla, i * 16 + 16)
                sg = state_gla[0].rearrange("b (d h) k v -> (h k) b d v", h=2)
                sp.dma_start(S_s[:, :, :, :], sg[:, bass.ds(i * 2, 2), :, :]).then_inc(s_loaded, 16)

                for m in range(1, 16):
                    load_unit(i, m, rows(w_in[0], 0, KD, slice(W_IN_COLS[m], W_IN_COLS[m] + P)))
                with sp.Fori(0, KD // 2) as j:
                    for r in range(2):
                        n_parity[0] = r
                        load_unit(i, j * 2 + (U_O + r), rows(w_o[0], 0, KD, bass.ds(j * 2 * P + r * P, P)))
                sp.wait_ge(act_s, act_.at(i, "pool_state"))
                sp.dma_start(pool_sample[0].rearrange("b t (g c) -> (b t g) c", g=POOLG)
                             [bass.ds(i * 120, 120), :], turned[0:120, 0, :]).then_inc(stored_pool, 16)
                sp.wait_ge(vec_s, vec_.at(i, "state_small"))
                so = gla_sample[0].rearrange("b (d h) k v -> (h k) b d v", h=2)
                sp.dma_start(so[:, bass.ds(i * 2, 2), :, :], S_s[:, :, :, :]).then_inc(stored_gla, 16)
                for r in range(2):
                    load_unit(i, U_UP + r, rows(w_up[0], 0, KD, slice(FF * (1 - r), FF * (1 - r) + P)))
                for r in range(2):
                    load_unit(i, U_UP + 2 + r, rows(w_up[0], 0, KD, slice(P + FF * (1 - r), P + FF * (1 - r) + P)))
                sp.wait_ge(vec_s, vec_.at(i, f"f_h1_{KD - 1}"))
                pp = p_prompt[0, 0, bass.ds(i * TOK, TOK), :].rearrange("(g p) d -> p g d", p=P)
                sp.dma_start(p_tok[:, :, :], pp).then_inc(p_loaded, 16)
                ps = p_sample[0].rearrange("b s d -> (b s) d")[bass.ds(i * 16, 16), :]
                sp.dma_start(p_small[:, :], ps).then_inc(p_loaded, 16)
                with sp.Fori(2, NF) as f:
                    for r in range(2):
                        n_parity[0] = r
                        load_unit(i, f * 2 + (U_UP + r), rows(w_up[0], 0, KD, bass.ds(f * P + FF * (1 - r), P)))
                with sp.Fori(0, KD // 2) as j:
                    for r in range(6):
                        n_parity[0] = r % 2
                        first, parts = DOWN_PARTS[r % 3]
                        load_unit(i, j * 6 + (U_DOWN + r),
                                  rows(w_down[0], first * P, parts, bass.ds(j * 2 * P + r // 3 * P, P)), parts)
                sp.wait_ge(act_s, act_.at(i, "conv_out"))
                sp.dma_start(conv_sample[0].rearrange("b t (f c) -> (b t f) c", f=NF)
                             [bass.ds(i * 88, 88), :], turned[0:88, 1, :]).then_inc(stored_conv, 16)
                for m in range(2):
                    sp.wait_ge(lo_made, i * UNITS + (U_PLE + m + 1))
                    dst = stage[m][:, :, :].rearrange("p (k c) d -> p k (c d)", k=2)
                    sp.dma_start(dst, w_ple[0, :, 512 * m:512 * m + 512].rearrange("(k p) c -> p k c", p=P))\
                      .then_inc(staged[m], 16)
                sp.wait_ge(ticks, tick(i, U_PLE - 1))
                sp.sem_inc(passed, 1)
                after = (i + 1) % TILES
                load_x(after, (0, 1), False)
                load_unit(i, U_GATE, rows(w_ple_gate[0], 0, KD, slice(0, P)))
                load_x(after, (2, 3), True)
                with sp.Fori(0, KD // 2 - 1) as j:
                    for r in (1, 2):
                        n_parity[0] = r % 2
                        load_unit(i, j * 2 + (U_GATE + r), rows(w_ple_gate[0], 0, KD, bass.ds(j * 2 * P + r * P, P)))
                load_unit(i, U_GATE + KD - 1, rows(w_ple_gate[0], 0, KD, slice(P * (KD - 1), P * KD)))
                load_unit(i, UNITS, rows(w_in[0], 0, KD, slice(W_IN_COLS[0], W_IN_COLS[0] + P)))
                sp.wait_ge(y_copied, i * 8 + 16)
                yp = y_prompt[0, bass.ds(i * TOK, TOK), :].rearrange("(g p) d -> p g d", p=P)
                sp.dma_start(yp, y_tok[:, :, :]).then_inc(stored_y, 16)
                ys = y_sample.rearrange("b s d -> s b d")[:, bass.ds(i * 2, 2), :]
                sp.dma_start(ys, y_small[:, :, :]).then_inc(stored_y, 16)

            sp.wait_ge(vec_s, vec_.at(TILES - 1, "state3"))
            sp.dma_start(gla_prompt[0, 0].rearrange("(d h) k v -> (h k) d v", h=2), S[:, :, :]).then_inc(stored_gla, 16)
            sp.wait_ge(last_copied, 1)
            sp.dma_start(pool_prompt[0, 0].rearrange("t (g c) -> (t g) c", g=POOLG),
                         turned[0:60, 0, :]).then_inc(stored_pool, 16)
            sp.wait_ge(last_copied, 2)
            sp.dma_start(conv_prompt[0, 0].rearrange("t (f c) -> (t f) c", f=NF),
                         turned[0:44, 1, :]).then_inc(stored_conv, 16)
            sp.wait_ge(states_loaded, TILES * 32 + 32)
            sp.wait_ge(stored_y, TILES * 32 + 32)
            sp.wait_ge(stored_pool, TILES * 16 + 32)
            sp.wait_ge(stored_gla, TILES * 16 + 32)
            sp.wait_ge(stored_conv, TILES * 16 + 32)

        @block.gpsimd
        def _(pool):
            n = [0]

            def build(instruction):
                n[0] += 1
                instruction.then_inc(built, 1)
                pool.wait_ge(built, n[0])

            build(pool.memset(ones[:, :], 1.0))
            build(pool.memset(ident[:, :], 0.0))
            build(pool.affine_select(out=ident[:, :], in_=ident[:, :], compare_op=ALU.not_equal, fill=1.0,
                                     base=0, pattern=[[-1, P]], channel_multiplier=1))
            sel = rms
            for n_level, h in enumerate(LEVELS):
                m = sel[:, 0:64].rearrange("p (n h) -> p n h", h=h)
                build(pool.memset(sel[:, 0:64], 1.0))
                build(pool.affine_select(out=m, in_=m, compare_op=ALU.is_ge, fill=0.0, base=0,
                                         pattern=[[-2 * h, 64 // h], [0, h]], channel_multiplier=1))
                build(pool.affine_select(out=m, in_=m, compare_op=ALU.is_ge, fill=0.0, base=h - 1,
                                         pattern=[[2 * h, 64 // h], [0, h]], channel_multiplier=-1))
                build(pool.tensor_copy(masks[:, n_level, :], sel[:, 0:64]))
            build(pool.memset(keep[:, :], 1.0))
            for a in range(2):
                for first in (0, P, HP):
                    build(pool.memset(keep[:, a * HALF + first:a * HALF + first + 1], 0.0))
            build(pool.memset(eps[:, :], EPS))
            for g, w in enumerate(WINDOWS):
                build(pool.memset(edge[:, g, :], 1.0 / w))
                for t in range(w - 1):
                    build(pool.memset(edge[:, g, t:t + 1], 1.0 / (t + 1)))
            build(pool.memset(z_past[:, :, :], 0.0))
            build(pool.memset(g_past[:, :, :], 0.0))
            build(pool.memset(S[:, :, :], 0.0))
            for w in (w_glow_hi, w_glow_lo):
                build(pool.memset(w[:, P:2 * P].bitcast(F32), 0.0))
            assert n[0] == BUILT, n

            with pool.Fori(0, TILES) as i:
                pool.wait_ge(y_turned, i * KD + 2)
                pool.sem_inc(passed, 1)
                for q in queries:
                    last = pool.memset(q[:, :, :, :, :].rearrange("p d a b t -> p (d a b t)"), 0.0)
                pool_.did(last, "query_zeros")
                pool.wait_ge(squared, i * SQUARES + KD)
                pool.sem_inc(passed, 1)
                pool.tensor_copy(xT[:, :, :], x_next[:, :, :]).then_inc(x_moved, 1)
                for o in (O_IN + 11, O_IN + 10):
                    pool.wait_ge(*evac(i, o))
                pool.wait_ge(vec_s, vec_.at(i, "states"))
                src, dst = Z, win_a
                for k, w in enumerate(WINDOWS):
                    if k:
                        pool.wait_ge(pool_s, pool_.at(i, f"window{WINDOWS[k - 1]}"))
                    pool_.did(pool.tensor_tensor(dst[:, k:, w - 1:], src[:, k:, w - 1:],
                                                 src[:, k:, w // 2 - 1:ZW - w // 2], ALU.add), f"window{w}")
                    src, dst = dst, (win_b if dst is win_a else win_a)
                tail = Z[:, :, ZS:].rearrange("p g (s t) -> p s t g", s=2)[:, :, 24 - HIST:, :]
                pool_.did(pool.tensor_copy(z_state[:, :].rearrange("p (s t g) -> p s t g", s=2, g=POOLG), tail),
                          "z_tail")
                pool_.did(pool.tensor_copy(z_past[:, :, 1:16], Z[:, :, ZS - HIST:ZS]), "z_history")
                pool.wait_ge(vec_s, vec_.at(i, "u_early"))
                pool.sem_inc(passed, 1)
                for g, w in enumerate(WINDOWS):
                    last = pool.memset(edge[:, g, :], 1.0 / w)
                pool_.did(last, "z_edges")

                pool.wait_ge(pe_s, pe_.at(i, "state_small"))
                pool.sem_inc(passed, 1)
                pool.wait_ge(x_moved, i + 1)
                for a in range(2):
                    for m in range(KD):
                        pool.wait_ge(vec_s, vec_.at(i, f"mixed_h{a}_{m}"))
                        pool_.did(pool.tensor_tensor(xT[:, m, half(a)], xT[:, m, half(a)], mixed[:, m, half(a)],
                                                     ALU.add), f"x_mixed_h{a}_{m}")
                for a in range(2):
                    for m in POOL_RESTS:
                        pool.wait_ge(act_s, act_.at(i, f"f_hi_h{a}_{m}"))
                        pool_.did(pool.tensor_tensor(h_lo[:, m, half(a)], normed_half(m),
                                                     h_hi[:, m, half(a)].bitcast(F32), ALU.subtract),
                                  f"f_lo_h{a}_{m}")
                with pool.Fori(0, NF) as f:
                    pool.wait_ge(tapped, i * 2 * NF + f * 2 + 2)
                    pool.tensor_copy(gx[:, 0, 0:2], g_past[:, :, bass.ds(f, 1)].rearrange("p t o -> p (t o)"))
                    pool.tensor_copy(gx[:, :, 258:260], g_state[:, :, :, bass.ds(f, 1)]
                                     .rearrange("p s t o -> p s (t o)")).then_inc(past_in, 1)
                    pool.wait_ge(gate_copied, i * NF + f + 1)
                    pool.sem_inc(passed, 1)
                    pool.tensor_copy(gx[:, 1, 0:2], gx[:, 0, 256:258]).then_inc(past_mid, 1)
                    pool.wait_ge(past_in, i * NF + f + 1)
                    pool.sem_inc(passed, 1)
                    pool.tensor_copy(g_past[:, :, bass.ds(f, 1)].rearrange("p t o -> p (t o)"), gx[:, 1, 256:258])
                    pool.tensor_copy(g_tail[:, :, :, bass.ds(f, 1)].rearrange("p s t o -> p s (t o)"),
                                     gx[:, :, 266:268]).then_inc(past_mid, 1)
                for m in POOL_ADDS:
                    pool.wait_ge(vec_s, vec_.at(i, f"ffn{m}"))
                    pool_.did(pool.tensor_tensor(xT[:, m, :], xT[:, m, :], ffn_out[:, m, :], ALU.add), f"x_ffn{m}")

            pool.wait_ge(pool_s, pool_.at(TILES - 1, "z_edges"))
            pool.tensor_copy(z_state[:, 0:60].rearrange("p (t g) -> p t g", g=POOLG),
                             z_past[:, :, 1:16].rearrange("p g t -> p t g")).then_inc(last_packed, 1)

        @block.scalar
        def _(act):
            def mod2(n):
                return n % 2 if isinstance(n, int) else parity[0]

            parity = [0]

            def split(i, n, free, parts=KD):
                s = mod2(n)
                act.wait_ge(staged[s], i * (UNITS // 2 * 16) + stage_count(n))
                act.wait_ge(ticks, tick(i, free))
                act.activation(w_hi[s][:, 0:parts, :], stage[s][:, 0:parts, :], ACT.Copy).then_inc(hi_made, 1)

            def stage_count(n):
                return (n // 2 + 1) * 16 if isinstance(n, int) else half_count[0]

            half_count = [0]

            def root(x, i, n, out=None, width=D):
                out = rms[:, :] if out is None else out
                act.activation(split2(out), halves(x), ACT.Ln, scale=1.0 / width, bias=eps[:, 0:1]).then_inc(logs, 1)
                act.wait_ge(logs, i * CHAIN + (n + 2))
                return act.activation(out, out, ACT.Exp, scale=-0.5)

            def root_half(x, a, i, n):
                out = rms[:, half(a)]
                act.activation(out, X[x][:, a, 0:HALF], ACT.Ln, scale=1.0 / D, bias=eps[:, 0:1]).then_inc(logs, 1)
                act.wait_ge(logs, i * CHAIN + (n + 2))
                return act.activation(out, out, ACT.Exp, scale=-0.5)

            def square_half(src, i, n, m, a):
                act.wait_ge(summed, i * SQUARES + (n + 1))
                act.activation(squares[:, m % 2, half(a)], src, ACT.Square).then_inc(squared, 1)

            def square(src, i, n):
                act.wait_ge(summed, i * SQUARES + (n + 1))
                dst = squares[:, n % 2 if isinstance(n, int) else parity[0], :]
                act.activation(dst if len(src.shape) == 2 else split2(dst), src, ACT.Square).then_inc(squared, 1)

            act.wait_ge(credited, 1)

            def take_x(i, k, number=None):
                act.wait_ge(x_turned, i * KD + (k + 1))
                x = X[(k + 1) % 2 if isinstance(k, int) else 1 - parity[0]]
                block_ = x_next[:, k, :] if isinstance(k, int) else \
                    x_next[:, bass.ds(k, 1), :].rearrange("p o c -> p (o c)")
                act.activation(split2(block_), halves(x), ACT.Copy)
                act.wait_ge(summed, i * SQUARES + (k + 1))
                act.activation(split2(squares[:, k % 2 if isinstance(k, int) else parity[0], :]), halves(x),
                               ACT.Square).then_inc(squared, 1)

            act.preload_act_table_set(LN_EXP)
            for k in range(KD):
                take_x(0, k)
            act.wait_ge(constants_loaded, 16 * CONSTANTS)
            act.activation(w_pool_hi[:, :, :], raw_pool[:, :, :], ACT.Copy).then_inc(split_once, 1)
            act.activation(w_glow_hi[:, 0:P], raw_glow[:, :, :].rearrange("p k c -> p (k c)"), ACT.Copy)\
               .then_inc(split_once, 1)
            act.wait_ge(staged[0], 16)
            act.activation(w_hi[0][:, :, :], stage[0][:, :, :], ACT.Copy).then_inc(hi_made, 1)
            act.wait_ge(built, BUILT)
            act.wait_ge(x_summed, 1)
            root(X[1], 0, -1).then_inc(x_rms, 1)
            with act.Fori(0, TILES) as i:
                act.wait_ge(ticks, tick(i, -1))
                for m in range(KD):
                    act.wait_ge(vec_s, vec_.at(i, f"h{m}"))
                    act_.did(act.activation(h_hi[:, m, :], normed[:, m % 2, :], ACT.Copy), f"h_hi{m}")

                act.wait_ge(pe_s, pe_.at(i, "states_turned"))
                act_.did(act.activation(z_in[:, :], X[0][:, 0, 0:2 * HIST * POOLG], ACT.Copy), "pool_history")
                act_.did(act.activation(g_state[:, :, :, :].rearrange("p s t f -> p (s t f)"),
                                        X[0][:, 1, 0:4 * NF], ACT.Copy), "conv_state")
                act.wait_ge(pe_s, pe_.at(i, "glow"))
                act_.did(act.activation(squares[0:RANK, 0, :].rearrange("p (a c) -> p a c", a=2),
                                        halves(X[1])[0:RANK], ACT.Copy), "glow")

                def extras(s):
                    if s == 1:
                        for d in range(2):
                            act.wait_ge(pe_s, pe_.at(i, f"gk{d}"))
                            last = act.activation(split2(opnd[0][:, d, :]), halves(X[d]), ACT.Abs,
                                                  bias=bias_gk[:, d:d + 1])
                        act_.did(last, "gk_abs")
                        act.wait_ge(act_s, act_.at(i, "gk_abs"))
                        act_.did(act.activation(opnd[0][:, :, :], opnd[0][:, :, :], ACT.Exp, scale=-1.0), "gk_exp")
                        act.wait_ge(act_s, act_.at(i, "gk_exp"))
                        act_.did(act.activation(opnd[0][:, :, :], opnd[0][:, :, :], ACT.Ln, bias=1.0), "gk_log")
                    if s in (9, 10):
                        if s == 9:
                            act.wait_ge(x_moved, i + 1)
                        act.wait_ge(pe_s, pe_.at(i, f"v_turned{s - 9}"))
                        act_.did(act.activation(v_tok[:, 2 * s - 18:2 * s - 16, :], G[(s + 1) % 2][:, :, :], ACT.Copy),
                                 f"v_copied{s - 9}")
                    if s == 11:
                        act.wait_ge(pe_s, pe_.at(i, "v_small_turned"))
                        act_.did(act.activation(v_small[:, :, :], G[0][0:SLEN, :, :], ACT.Copy), "v_small")
                    if 4 <= s <= 10:
                        h = LEVELS[s - 4]
                        act.wait_ge(vec_s, vec_.at(i, f"gap{h}"))
                        v = level_view(gap, h)
                        act.activation(v[:, :, :, 0:h], v[:, :, :, 0:h], ACT.Exp, scale=-1.0 / GATE_NORM)
                        act_.did(act.activation(v[:, :, :, h:], v[:, :, :, h:], ACT.Exp, scale=1.0 / GATE_NORM),
                                 f"decay{h}")
                    if s == 11:
                        act.wait_ge(vec_s, vec_.at(i, "kd_gap"))
                        act_.did(act.activation(gap[:, :, :], gap[:, :, :], ACT.Exp, scale=1.0 / GATE_NORM), "kd_decay")
                        act_.did(act.activation(cum[:, :, :], cum[:, :, :], ACT.Exp, scale=1.0 / GATE_NORM), "cum_decay")
                    if s == 12:
                        act.wait_ge(pe_s, pe_.at(i, "kd_turned"))
                        act_.did(act.activation(kd_tok[:, :, :, :].rearrange("p c d k -> p (c d k)"),
                                                X[1][:, :, :].rearrange("p b c -> p (b c)"), ACT.Copy), "kd_copied")
                        act.wait_ge(pe_s, pe_.at(i, "kd_small_turned"))
                        act_.did(act.activation(kd_small[:, :, :].rearrange("p a c -> p (a c)"), X[0][0:SLEN, 0, :],
                                                ACT.Copy), "kd_small")
                    if s == 13:
                        copy_out(0)
                    if s == 14:
                        copy_out(1)
                        u_split(0)
                        u_split(1)
                    if s == 15:
                        copy_out(2)
                        for m in (13, 14):
                            act.wait_ge(*evac(i, m))
                        act.activation(ogT[:, 0:3, :], ogT[:, 0:3, :], ACT.Silu)

                def copy_out(c):
                    act.wait_ge(pe_s, pe_.at(i, f"out{c}"))
                    act_.did(act.activation(outT[:, :, group_cols(c):group_cols(c) + P]
                                            .rearrange("p (d b) c -> p b d c", b=2),
                                            X[(c + 1) % 2][:, :, 0:2 * P].rearrange("p b (d c) -> p b d c", c=P),
                                            ACT.Copy), f"out{c}")

                def u_split(g):
                    act.wait_ge(vec_s, vec_.at(i, f"u{g}"))
                    if g >= 2:
                        act.wait_ge(pe_s, pe_.at(i, f"pool{g - 2}"))
                    w = win_a if g % 2 == 0 else win_b
                    act.activation(u_hi[:, g % 2, :].rearrange("p (a c) -> p a c", a=2)[:, :, 0:HP],
                                   w[:, g, 16:ZS].rearrange("p (a c) -> p a c", a=2), ACT.Copy)
                    act_.did(act.activation(u_hi[:, g % 2, :].rearrange("p (a c) -> p a c", a=2)[:, :, HP:],
                                            w[:, g, ZS:].rearrange("p (a c) -> p a c", a=2)[:, :, 16:], ACT.Copy),
                             f"u_hi{g}")

                def pool_split(g):
                    act.wait_ge(pe_s, pe_.at(i, f"pool{g}"))
                    act_.did(act.activation(split2(h_hi[:, g, :]), halves(X[1]), ACT.Copy,
                                            scale=scale_pool[:, g:g + 1]), f"mix_hi{g}")

                for m in range(16):
                    split(i, m + 1, tick_of(m - 1) if m else -1)
                    extras(m)
                    act.wait_ge(ticks, tick(i, m))
                    src = halves(G[m % 2])
                    if 8 <= m < 12:
                        g = m - 8
                        act.activation(Z[:, g, 16:ZS].rearrange("p (a c) -> p a c", a=2), src[:, :, 0:HP], ACT.Copy)
                        act.activation(Z[:, g, ZS:].rearrange("p (a c) -> p a c", a=2)[:, :, 16:],
                                       src[:, :, HP:], ACT.Copy).then_inc(evacuated[m % 2], 1)
                    else:
                        dst, at_, scale = ((kT, m, 1.0) if m < 2 else (qT, m - 2, KDIM ** -0.5) if m < 4
                                           else (vT, m - 4, 1.0) if m < 8 else (ogT, m - 12, 1.0))
                        act.activation(split2(dst[:, at_, :]), src, ACT.Copy, scale=scale)\
                           .then_inc(evacuated[m % 2], 1)
                split(i, U_O + 1, 15)
                act.wait_ge(*evac(i, 15))
                act_.did(act.activation(ogT[:, 3, :], ogT[:, 3, :], ACT.Silu), "silu")
                act.sem_inc(passed, 1)
                act.preload_act_table_set(LN_EXP)
                copy_out(3)
                pool_split(0)
                u_split(2)
                act.wait_ge(pe_s, pe_.at(i, "out_small"))
                for b in range(2):
                    last = act.activation(outT[:, b:HEADS:2, :].rearrange("p d (a c) -> p d a c", a=2)[:, :, :, HP:],
                                          X[0][:, b, 0:32].rearrange("p (d a c) -> p d a c", d=2, a=2), ACT.Copy)
                act_.did(last, "out_small")
                pool_split(1)
                u_split(3)
                act.wait_ge(act_s, act_.at(i, "out_small"))
                act.wait_ge(vec_s, vec_.at(i, "u_lo2"))
                act_.did(act.activation(out_sq[:, :, :], outT[:, :, :], ACT.Square), "out_squares")
                pool_split(2)

                def head_split(h):
                    act.wait_ge(vec_s, vec_.at(i, f"out_gated{h}"))
                    act_.did(act.activation(h_hi[:, 4 + h, :], outT[:, h, :], ACT.Copy), f"mix_hi{4 + h}")

                for h in range(HEADS):
                    act.wait_ge(pe_s, pe_.at(i, f"head{h}"))
                    if h >= 2:
                        act.wait_ge(vec_s, vec_.at(i, f"out_scaled{h - 2}"))
                    act_.did(root(X[HEAD_BANKS[h]], i, h, squares[:, h % 2, :], VDIM), f"rms_head{h}")
                    if h == 0:
                        pool_split(3)
                    else:
                        head_split(h - 1)
                head_split(HEADS - 1)
                act.wait_ge(pe_s, pe_.at(i, "pool_state_turned"))
                act.wait_ge(stored_pool, i * 16 + 16)
                act_.did(act.activation(turned[0:120, 0, :], X[1][0:120, 0, 0:P], ACT.Copy), "pool_state")

                with act.Fori(0, KD // 2 - 1) as j:
                    for r in range(2):
                        parity[0], half_count[0] = r, j * 16 + (U_O + r + 2) // 2 * 16 + 16
                        act.wait_ge(ticks, tick(i, j * 2 + (U_O + r)))
                        square(halves(G[r]), i, j * 2 + (SQ_MIX + r))
                        act.activation(split2(mixed[:, bass.ds(j * 2 + r, 1), :].rearrange("p o c -> p (o c)")),
                                       halves(G[r]), ACT.Copy).then_inc(evacuated[r], 1)
                        split(i, j * 2 + (U_O + r + 2), j * 2 + (U_O + r))
                act.wait_ge(pe_s, pe_.at(i, "o_half"))
                for r in range(2):
                    square_half(G[r][:, 0, 0:HALF], i, SQ_HALVES + r, r, 0)
                for r in range(2):
                    act.activation(mixed[:, KD - 2 + r, half(0)], G[r][:, 0, 0:HALF], ACT.Copy)
                act.wait_ge(summed, i * SQUARES + (SQ_HALVES + 2 + 2))
                act_.did(root_half(1, 0, i, 4), "rms_post_mix0")
                for r in range(2):
                    act.wait_ge(ticks, tick(i, U_O + KD - 2 + r))
                    square_half(G[r][:, 1, 0:HALF], i, SQ_HALVES + 2 + r, r, 1)
                    act.activation(mixed[:, KD - 2 + r, half(1)], G[r][:, 1, 0:HALF], ACT.Copy)\
                       .then_inc(evacuated[r], 1)
                    split(i, U_UP + r, U_O + KD - 2 + r)
                act.wait_ge(summed, i * SQUARES + (SQ_HALVES + 4 + 2))
                act_.did(root_half(1, 1, i, 5), "rms_post_mix1")
                def square_x(m, a):
                    act.wait_ge(pool_s, pool_.at(i, f"x_mixed_h{a}_{m}"))
                    square_half(xT[:, m, half(a)], i, SQ_X + KD * a + m, m, a)

                def f_split(m, a):
                    act.wait_ge(vec_s, vec_.at(i, f"f_h{a}_{m}"))
                    act_.did(act.activation(h_hi[:, m, half(a)], normed_half(m), ACT.Copy),
                             f"f_hi_h{a}_{m}")

                for m in range(KD):
                    square_x(m, 0)
                for m in range(KD):
                    square_x(m, 1)
                    if m == 1:
                        act.wait_ge(summed, i * SQUARES + (SQ_X + KD + 2))
                        act_.did(root_half(0, 0, i, 6), "rms_pre_ffn0")
                for m in range(KD):
                    f_split(m, 0)
                    if m == 1:
                        act.wait_ge(summed, i * SQUARES + (SQ_FFN + 2))
                        act_.did(root_half(0, 1, i, 7), "rms_pre_ffn1")
                for m in range(KD):
                    f_split(m, 1)

                act.sem_inc(passed, 1)
                act.preload_act_table(ACT.Gelu_apprx_tanh)
                def ffn_block(f, last=False):
                    parity[0], half_count[0] = 0, f * 16 + (U_UP + 2) // 2 * 16 + 16
                    split(i, f * 2 + (U_UP + 2), f * 2 + U_UP)
                    act.wait_ge(tapped, i * (2 * NF) + f * 2 + 2)
                    act.wait_ge(past_mid, i * (2 * NF) + f * 2 + 2)
                    act.activation(gx[:, :, 2:258], G[0][:, :, 0:HP], ACT.Copy)
                    act.activation(gx[:, :, 260:268], G[0][:, :, HP:HALF], ACT.Copy).then_inc(gate_copied, 1)
                    act.wait_ge(gate_copied, i * NF + f + 1)
                    act.wait_ge(past_in, i * NF + f + 1)
                    act.activation(cg[:, :, :], gx[:, :, 2:268], ACT.Identity,
                                   scale=taps[:, 2, bass.ds(f, 1)], bias=bias_conv[:, bass.ds(f, 1)])\
                       .then_inc(evacuated[0], 1)
                    act.wait_ge(tapped, i * (2 * NF) + f * 2 + 4)
                    act.activation(cg[:, :, :], cg[:, :, :], ACT.Gelu_apprx_tanh).then_inc(gelu_made, 1)
                    if not last:
                        parity[0], half_count[0] = 1, f * 16 + (U_UP + 3) // 2 * 16 + 16
                        split(i, f * 2 + (U_UP + 3), f * 2 + (U_UP + 1))
                    act.wait_ge(evacuated[1], i * (OUTS // 2) + f + ((O_UP + 1) // 2 + 2))
                    act.activation(y_hi[:, bass.ds(f, 1), :].rearrange("p o c -> p (o c)"), yf[:, :], ACT.Copy)\
                       .then_inc(hidden_hi, 1)

                with act.Fori(0, NF - 1) as f:
                    ffn_block(f)
                ffn_block(NF - 1, last=True)

                act.sem_inc(passed, 1)
                act.preload_act_table_set(LN_EXP)

                def down(j, r):
                    n, parts = U_DOWN + r + 1, DOWN_PARTS[(r + 1) % 3][1]
                    parity[0], half_count[0] = n % 2, j * 48 + (n // 2 + 1) * 16
                    split(i, j * 6 + n, j * 6 + (U_DOWN + r - 1), parts)
                    if r % 3 == 2:
                        act.wait_ge(ticks, tick(i, j * 6 + (U_DOWN + r)))
                        parity[0] = r // 3
                        square(halves(G[r // 3]), i, j * 2 + (SQ_FFN + r // 3))
                        act.activation(split2(ffn_out[:, bass.ds(j * 2 + r // 3, 1), :].rearrange("p o c -> p (o c)")),
                                       halves(G[r // 3]), ACT.Copy).then_inc(evacuated[r // 3], 1)

                def p_split(x, cols, name):
                    act.wait_ge(pe_s, pe_.at(i, f"p_turned{name}"))
                    for b in range(2):
                        last = act.activation(p_hi[:, :, cols[b]:cols[b] + P],
                                              X[x][:, b, 0:256].rearrange("p (k c) -> p k c", k=2), ACT.Copy)
                    act_.did(last, f"p_hi{name}")

                p_split(0, (group_cols(0), group_cols(1)), "01")
                act_.did(act.activation(p_hi[:, :, :].rearrange("p k (a c) -> p k a c", a=2)[:, :, :, HP:],
                                        X[0][:, 0, 256:288].rearrange("p (k a c) -> p k a c", k=2, a=2), ACT.Copy),
                         "p_hi_small")
                p_split(1, (group_cols(2), group_cols(3)), "23")
                act.wait_ge(stored_conv, i * 16 + 16)
                act_.did(act.activation(turned[0:88, 1, :], X[1][0:88, 0, 256:256 + P], ACT.Copy), "conv_out")
                with act.Fori(0, KD // 2) as j:
                    for r in range(6):
                        down(j, r)


                def copy_ple(m):
                    act.wait_ge(ticks, tick(i, U_PLE + m))
                    act.activation(split2(ple[:, m, :]), halves(G[m % 2]), ACT.Copy).then_inc(evacuated[m % 2], 1)

                def x_split(m):
                    if m in POOL_ADDS:
                        act.wait_ge(pool_s, pool_.at(i, f"x_ffn{m}"))
                    else:
                        act.wait_ge(vec_s, vec_.at(i, f"x_ffn{m}"))
                    act_.did(act.activation(h_hi[:, m, :], xT[:, m, :], ACT.Copy), f"x_hi{m}")

                split(i, U_PLE + 1, tick_of(U_PLE - 1))
                for m in range(KD):
                    copy_ple(m)
                    if m == 1:
                        act.wait_ge(pe_s, pe_.at(i, "sum_post_ffn"))
                        act_.did(root(X[0], i, 8), "rms_post_ffn")
                    if m == 3:
                        split(i, U_GATE, tick_of(U_PLE))
                    if m == KD - 1:
                        split(i, U_GATE + 1, tick_of(U_PLE + 1))
                    if m >= 3:
                        x_split(m - 3)
                for m in range(KD - 3, KD):
                    x_split(m)
                act.wait_ge(stored_y, i * 32 + 32)
                act.sem_inc(passed, 1)
                act.preload_act_table(ACT.Sigmoid)

                def gate(j, r):
                    act.wait_ge(ticks, tick(i, j * 2 + (tick_of(U_GATE) + r)))
                    act.wait_ge(y_turned, i * KD + j * 2 + (r + 1))
                    act.activation(split2(sig[:, r % 2, :]), halves(G[r % 2]), ACT.Sigmoid)\
                       .then_inc(evacuated[r % 2], 1)

                def copy_y(j, r):
                    act.wait_ge(y_turned, i * KD + j * 2 + (r + 3))
                    cols = bass.ds(j * (2 * P) + r * P, P)
                    act.activation(y_tok[:, :, cols], X[r % 2][:, 0, :].rearrange("p (g c) -> p g c", c=P), ACT.Copy)
                    act.activation(y_small[:, :, cols], X[r % 2][0:SLEN, 1, 0:2 * P].rearrange("p (a c) -> p a c", a=2),
                                   ACT.Copy).then_inc(y_copied, 1)

                gate(0, 0)
                split(i, U_GATE + 2, tick_of(U_GATE))
                gate(0, 1)
                for k in range(3):
                    take_x(i + 1, k)
                copy_y(0, 0)
                def gate_step(j, r):
                    n = U_GATE + r + 1
                    parity[0], half_count[0] = n % 2, j * 16 + (n // 2 + 1) * 16
                    split(i, j * 2 + n, j * 2 + (tick_of(U_GATE) + r - 1))
                    gate(j, r)

                with act.Fori(0, KD // 2 - 2) as j:
                    for r in (2, 3):
                        gate_step(j, r)
                        parity[0] = (r + 1) % 2
                        take_x(i + 1, j * 2 + (r + 1))
                        copy_y(j, r - 1)
                gate_step(0, 6)
                take_x(i + 1, 7)
                copy_y(0, 5)
                gate_step(0, 7)
                act.sem_inc(passed, 1)
                act.preload_act_table_set(LN_EXP)
                act.wait_ge(x_summed, i + 2)
                root(X[1], i, 9).then_inc(x_rms, 1)
                copy_y(0, 6)
                copy_y(0, 7)

            act.wait_ge(last_turned, 1)
            act.activation(turned[0:60, 0, :], X[0][0:60, 0, 0:P], ACT.Copy).then_inc(last_copied, 1)
            act.wait_ge(last_turned, 2)
            act.activation(turned[0:44, 1, :], X[1][0:44, 0, 0:P], ACT.Copy).then_inc(last_copied, 1)


        @block.vector
        def _(dve):
            par = [0]

            def slot(n):
                return n % 2 if isinstance(n, int) else par[0]

            def exact(t):
                return t.bitcast(F32)

            def split(i, n, parts=KD):
                s = slot(n)
                dve.wait_ge(hi_made, i * UNITS + (n + 1))
                dve.tensor_tensor(w_lo[s][:, 0:parts, :], stage[s][:, 0:parts, :], exact(w_hi[s][:, 0:parts, :]),
                                  ALU.subtract).then_inc(lo_made, 1)

            def step(instruction, name):
                vec_.did(instruction, name)

            def own(i, name):
                dve.wait_ge(vec_s, vec_.at(i, name))

            def add_square(i, n):
                dve.wait_ge(squared, i * SQUARES + (n + 1))
                dve.wait_ge(summed, i * SQUARES + (n + 2))
                dve.tensor_tensor(total[:, :], total[:, :], squares[:, slot(n), :], ALU.add).then_inc(summed, 1)

            def sum_x(i, n, k=None):
                if k == 0:
                    dve.wait_ge(squared, i * SQUARES + 1)
                    dve.tensor_copy(total[:, :], squares[:, 0, :]).then_inc(summed, 1)
                else:
                    add_square(i, n)

            starts = [(lo_made, 2), (ticks, 2), (evacuated[0], 1), (evacuated[1], 1), (summed, 2), (tapped, 2),
                      (past_mid, 2), (y_turned, 2), (y_copied, 8), (stored_y, 32), (stored_pool, 16), (stored_gla, 16),
                      (stored_conv, 16), (pe_s, len(PE_STEPS)), (act_s, len(ACT_STEPS)), (vec_s, len(VEC_STEPS)),
                      (pool_s, len(POOL_STEPS))]
            for n, (s_, value) in enumerate(starts):
                dve.memset(started[:, n:n + 1], 0.0).then_inc(s_, value)
            dve.memset(started[:, len(starts):len(starts) + 1], 0.0).then_inc(credited, 1)

            for k in range(KD):
                sum_x(0, k, k)
            dve.wait_ge(built, BUILT)
            dve.wait_ge(constants_loaded, 16 * CONSTANTS)
            dve.wait_ge(split_once, 2)
            dve.tensor_tensor(w_pool_lo[:, :, :], raw_pool[:, :, :], exact(w_pool_hi[:, :, :]), ALU.subtract)\
               .then_inc(split_once, 1)
            dve.tensor_tensor(w_glow_lo[:, 0:P], raw_glow[:, :, :].rearrange("p k c -> p (k c)"),
                              exact(w_glow_hi[:, 0:P]), ALU.subtract).then_inc(split_once, 1)
            split(0, 0)

            with dve.Fori(0, TILES) as i:
                def scaled(m, x, gain, name, before, ready=None):
                    if m >= 2:
                        dve.wait_ge(act_s, act_.at(i, f"{before}_hi{m - 2}"))
                        own(i, f"{before}_lo{m - 2}")
                    elif ready:
                        dve.wait_ge(act_s, act_.at(i, ready))
                    step(dve.scalar_tensor_tensor(normed[:, m % 2, :], x[:, m, :], gains[:, gain, m:m + 1],
                                                  rms[:, :], ALU.mult, ALU.mult), name)

                def rest(m, name, hi_name, own_name):
                    dve.wait_ge(act_s, act_.at(i, hi_name))
                    own(i, own_name)
                    step(dve.tensor_tensor(h_lo[:, m, :], normed[:, m % 2, :], exact(h_hi[:, m, :]),
                                           ALU.subtract), name)

                dve.wait_ge(x_rms, i + 1)
                dve.wait_ge(ticks, tick(i, -1))
                for s in range(KD + 1):
                    if s < KD:
                        scaled(s, x_next, 0, f"h{s}", "h")
                    if s:
                        rest(s - 1, f"h_lo{s - 1}", f"h_hi{s - 1}", f"h{s - 1}")

                def gap_step(h):
                    v = level_view(cum, h)
                    mid = v[:, :, :, h - 1:h].broadcast_to(list(v.shape))
                    step(dve.tensor_tensor(level_view(gap, h), v, mid, ALU.subtract), f"gap{h}")

                def operand_step(h, n):
                    dve.wait_ge(act_s, act_.at(i, f"decay{h}"))
                    if n >= 2:
                        dve.wait_ge(pe_s, pe_.at(i, f"scores{4 * h}" if 4 * h > 4 else f"small{4 * h}"))
                    elif n == 1:
                        dve.wait_ge(pe_s, pe_.at(i, "diag"))
                    dve.tensor_tensor(level_view(opnd[n % 2], h, 0), level_view(kT, h, 0), level_view(gap, h, 0), ALU.mult)
                    if h <= 4:
                        side = lambda t: t[:, :, :].rearrange("p d (a c) -> p (d a) c", a=2)[:, :, HP:]\
                            .rearrange("p s (n w) -> p s n w", w=2 * h)[:, :, :, h:]
                        dve.tensor_tensor(side(opnd[n % 2]), side(qT), side(gap), ALU.mult)
                    if n == 0:
                        dve.wait_ge(pool_s, pool_.at(i, "query_zeros"))
                    for b in range(2):
                        r = slice(64 * b, 64 * b + 64)
                        right = lambda t: t[r, :, :].rearrange("p d (a c) -> p (d a) c", a=2)[:, :, 0:HP]\
                            .rearrange("p s (n w) -> p s n w", w=2 * h)[:, :, :, h:]
                        out = queries[n % 2][r, :, :, b, :].rearrange("p d a (n h) -> p (d a) n h", h=h)
                        last = dve.tensor_tensor(out, right(qT), right(gap), ALU.mult)
                    step(last, f"operand{h}")

                def take_scores(h, x, before):
                    dve.wait_ge(pe_s, pe_.at(i, f"scores{h}"))
                    own(i, before)
                    dve.sem_inc(passed, 1)
                    nb = 64 // h
                    out = A[:, :, :].rearrange("p r (n w) -> p r n w", w=2 * h)[:, :, :, h:]
                    mask = masks[:, LEVELS.index(h), :].rearrange("p (o n h) -> p o n h", o=1, h=h)
                    data = X[x][:, :, :].rearrange("p d (r n h) -> p (d r) n h", n=nb, h=h)
                    step(dve.copy_predicated(out, mask.broadcast_to([P, 16, nb, h]), data), f"scores{h}")

                def take_small(h, x, before):
                    dve.wait_ge(pe_s, pe_.at(i, f"small{h}"))
                    own(i, before)
                    dve.sem_inc(passed, 1)
                    nb = SLEN // 2 // h
                    for b in range(2):
                        out = A_s[:, 4 * b:4 * b + 4, :].rearrange("p r (n w) -> p r n w", w=2 * h)[:, :, :, h:]
                        mask = masks[0:SLEN, LEVELS.index(h), 0:SLEN // 2].rearrange("p (o n h) -> p o n h", o=1, h=h)
                        data = X[x][0:SLEN, b, 0:16].rearrange("p (r n h) -> p r n h", n=nb, h=h)
                        last = dve.copy_predicated(out, mask.broadcast_to([SLEN, 4, nb, h]), data)
                    step(last, f"small{h}")

                def update_state(c):
                    dve.wait_ge(act_s, act_.at(i, f"out{c}"))
                    if c:
                        own(i, f"state{c - 1}")
                    col = group_cols(c) + P - 1
                    for d in range(2):
                        for b in range(2):
                            r = slice(64 * b, 64 * b + 64)
                            last = dve.scalar_tensor_tensor(
                                S[r, d, :], S[r, d, :], cum[r, d, col:col + 1],
                                X[(c + 1) % 2][r, d, 256 + P * b:256 + P * b + P], ALU.mult, ALU.add)
                    step(last, f"state{c}")

                def extras(s):
                    if s == 1:
                        dve.wait_ge(act_s, act_.at(i, "gk_abs"))
                        for d in range(2):
                            last = dve.tensor_scalar(split2(gap[:, d, :]), halves(X[d]), bias_gk[:, d:d + 1], 0.0,
                                                     ALU.add, ALU.min)
                        step(last, "gk_min")
                        own(i, "gk_min")
                        dve.wait_ge(act_s, act_.at(i, "gk_log"))
                        step(dve.tensor_tensor(gap[:, :, :], gap[:, :, :], opnd[0][:, :, :], ALU.subtract), "gk")
                        own(i, "gk")
                        for d in range(2):
                            step(dve.tensor_tensor_scan(cum[:, d, :], keep[:, :], gap[:, d, :], 0.0, ALU.mult, ALU.add),
                                 f"cumsum{d}")
                    if s == 2:
                        dve.wait_ge(stored_y, i * 32 + 32)
                        dve.wait_ge(act_s, act_.at(i, "pool_history"))
                        dve.wait_ge(pool_s, pool_.before(i, "z_history"))
                        dve.memset(Z[:, :, 0:1], 0.0)
                        dve.memset(Z[:, :, ZS:].rearrange("p g (s t) -> p g s t", s=2)[:, :, :, 0:1], 0.0)
                        dve.tensor_copy(Z[:, :, 1:16], z_past[:, :, 1:16])
                        for q in range(2):
                            last = dve.tensor_copy(Z[:, :, ZS + 24 * q + 1:ZS + 24 * q + 16],
                                                   z_in[:, 60 * q:60 * q + 60].rearrange("p (t g) -> p g t", g=POOLG))
                        step(last, "states")
                    if s == 4:
                        dve.wait_ge(x_moved, i + 1)
                        for o in (2, 3):
                            dve.wait_ge(*evac(i, o))
                        own(i, "cumsum1")
                        step(dve.tensor_tensor(opnd[1][:, :, :], qT[:, :, :], kT[:, :, :], ALU.mult), "qk")
                        gap_step(64)
                        operand_step(64, 0)
                    if s == 5:
                        own(i, "operand64")
                        gap_step(32)
                        dve.wait_ge(pe_s, pe_.at(i, "diag"))
                        diag = X[0][:, :, 0:8].unsqueeze(3).broadcast_to([P, 2, 8, P])
                        eye = ident[:, :].rearrange("p (o q c) -> p o q c", o=1, q=1).broadcast_to([P, 2, 8, P])
                        step(dve.tensor_tensor(A[:, :, :].rearrange("p (r b) t -> p b r t", b=2), eye, diag, ALU.mult),
                             "scores_diag")
                        diag = X[0][0:SLEN, :, 8:12].unsqueeze(3).broadcast_to([SLEN, 2, 4, SLEN])
                        eye = ident[0:SLEN, 0:SLEN].rearrange("p (o q c) -> p o q c", o=1, q=1)\
                            .broadcast_to([SLEN, 2, 4, SLEN])
                        step(dve.tensor_tensor(A_s[:, :, :].rearrange("p (b r) t -> p b r t", b=2), eye, diag, ALU.mult),
                             "scores_small_diag")
                        take_scores(64, 1, "scores_diag")
                        operand_step(32, 1)
                    if 6 <= s <= 10:
                        n = s - 4
                        h = LEVELS[n]
                        own(i, f"operand{2 * h}")
                        gap_step(h)
                        take_scores(2 * h, (n + 0) % 2, f"scores{4 * h}")
                        if 2 * h <= 4:
                            take_small(2 * h, (n + 1) % 2, f"small{4 * h}" if 4 * h <= 4 else "scores_small_diag")
                        operand_step(h, n)
                    if s == 11:
                        own(i, "operand1")
                        v = cum[:, :, :].rearrange("p d (a c) -> p (d a) c", a=2)
                        g = gap[:, :, :].rearrange("p d (a c) -> p (d a) c", a=2)
                        vp = v[:, :, 0:HP].rearrange("p s (b c) -> p s b c", c=P)
                        dve.tensor_tensor(g[:, :, 0:HP].rearrange("p s (b c) -> p s b c", c=P),
                                          vp[:, :, :, P - 1:P].broadcast_to([P, 4, 2, P]), vp, ALU.subtract)
                        step(dve.tensor_tensor(g[:, :, HP:], v[:, :, HALF - 1:HALF].broadcast_to([P, 4, SLEN]),
                                               v[:, :, HP:], ALU.subtract), "kd_gap")
                        take_scores(1, 1, "scores2")
                        take_small(1, 0, "small2")
                        dve.wait_ge(act_s, act_.at(i, "kd_decay"))
                        step(dve.tensor_tensor(gap[:, :, :], gap[:, :, :], kT[:, :, :], ALU.mult), "kd")
                        dve.wait_ge(act_s, act_.at(i, "cum_decay"))
                        step(dve.tensor_tensor(qT[:, :, :], qT[:, :, :], cum[:, :, :], ALU.mult), "qb")
                    if s == 13:
                        update_state(0)
                        pooled()
                    if s == 14:
                        update_state(1)
                        u_rest(0)
                        u_rest(1)
                    if s == 15:
                        update_state(2)

                def pooled():
                    dve.wait_ge(pool_s, pool_.at(i, "window16"))
                    for w_, first in ((win_a, 0), (win_b, 1)):
                        early = w_[:, first:POOLG:2, 16:32]
                        last = dve.tensor_tensor(early, early, edge[:, first:POOLG:2, :], ALU.mult)
                    step(last, "edges_scaled")
                    own(i, "edges_scaled")
                    for w_, first in ((win_a, 0), (win_b, 1)):
                        early = w_[:, first:POOLG:2, 16:32]
                        last = dve.tensor_tensor(early, early, Z[:, first:POOLG:2, 16:32], ALU.subtract)
                    step(last, "u_early")
                    for g, w in enumerate(WINDOWS):
                        dst = (win_a if g % 2 == 0 else win_b)[:, g, 32:]
                        step(dve.scalar_tensor_tensor(dst, dst, 1.0 / w, Z[:, g, 32:], ALU.mult, ALU.subtract), f"u{g}")

                def u_rest(g):
                    dve.wait_ge(act_s, act_.at(i, f"u_hi{g}"))
                    own(i, f"u{g}")
                    w = win_a if g % 2 == 0 else win_b
                    lo, hi = split2(u_lo[:, g % 2, :]), split2(exact(u_hi[:, g % 2, :]))
                    dve.tensor_tensor(lo[:, :, 0:HP], w[:, g, 16:ZS].rearrange("p (a c) -> p a c", a=2),
                                      hi[:, :, 0:HP], ALU.subtract)
                    step(dve.tensor_tensor(lo[:, :, HP:], w[:, g, ZS:].rearrange("p (a c) -> p a c", a=2)[:, :, 16:],
                                           hi[:, :, HP:], ALU.subtract), f"u_lo{g}")

                def pool_rest(g):
                    dve.wait_ge(act_s, act_.at(i, f"mix_hi{g}"))
                    step(dve.scalar_tensor_tensor(split2(h_lo[:, g, :]), halves(X[1]), scale_pool[:, g:g + 1],
                                                  split2(exact(h_hi[:, g, :])), ALU.mult, ALU.subtract), f"mix_lo{g}")

                for m in range(16):
                    split(i, m + 1)
                    extras(m)
                split(i, U_O + 1)
                update_state(3)
                pool_rest(0)
                u_rest(2)
                pool_rest(1)
                u_rest(3)
                dve.wait_ge(pe_s, pe_.at(i, "state_small"))
                for a in range(2):
                    for d in range(2):
                        for b in range(2):
                            r = slice(64 * b, 64 * b + 64)
                            col = HALF * a + HALF - 1
                            last = dve.scalar_tensor_tensor(
                                S_s[r, a, d, :], S_s[r, a, d, :], cum[r, d, col:col + 1],
                                X[0][r, a, 256 * d + P * b:256 * d + P * b + P], ALU.mult, ALU.add)
                step(last, "state_small")
                pool_rest(2)
                for h in range(HEADS + 1):
                    if h < HEADS:
                        dve.wait_ge(act_s, act_.at(i, f"rms_head{h}"))
                        step(dve.scalar_tensor_tensor(outT[:, h, :], outT[:, h, :], gain_head[:, 0:1],
                                                      squares[:, h % 2, :], ALU.mult, ALU.mult), f"out_scaled{h}")
                        own(i, f"out_scaled{h}")
                        step(dve.tensor_tensor(outT[:, h, :], outT[:, h, :], ogT[:, h, :], ALU.mult), f"out_gated{h}")
                    if h == 0:
                        pool_rest(3)
                    else:
                        dve.wait_ge(act_s, act_.at(i, f"mix_hi{3 + h}"))
                        step(dve.tensor_tensor(h_lo[:, 3 + h, :], outT[:, h - 1, :], exact(h_hi[:, 3 + h, :]),
                                               ALU.subtract), f"mix_lo{3 + h}")

                step(dve.memset(total[:, :], 0.0), "zeros_mix")
                own(i, "zeros_mix")
                dve.sem_inc(passed, 1)
                with dve.Fori(0, KD // 2 - 1) as j:
                    for r in range(2):
                        par[0] = r
                        add_square(i, j * 2 + (SQ_MIX + r))
                        split(i, j * 2 + (U_O + r + 2))

                def norm_mixed(a):
                    dve.wait_ge(act_s, act_.at(i, f"rms_post_mix{a}"))
                    for m in range(KD):
                        step(dve.scalar_tensor_tensor(mixed[:, m, half(a)], mixed[:, m, half(a)],
                                                      gains[:, 1, m:m + 1], rms[:, half(a)],
                                                      ALU.mult, ALU.mult), f"mixed_h{a}_{m}")

                def norm_x(a):
                    for s in range(KD + 1):
                        if s < KD:
                            if s >= 4:
                                dve.wait_ge(act_s, act_.at(i, f"f_hi_h{a}_{s - 4}"))
                                dve.wait_ge(*f_lo_done(i, a, s - 4))
                            elif s == 0:
                                dve.wait_ge(act_s, act_.at(i, f"rms_pre_ffn{a}"))
                            if a and s < 4:
                                dve.wait_ge(act_s, act_.at(i, f"f_hi_h0_{s + 4}"))
                                dve.wait_ge(*f_lo_done(i, 0, s + 4))
                            step(dve.scalar_tensor_tensor(normed_half(s), xT[:, s, half(a)],
                                                          gains[:, 2, s:s + 1], rms[:, half(a)],
                                                          ALU.mult, ALU.mult), f"f_h{a}_{s}")
                        if s and s - 1 not in POOL_RESTS:
                            dve.wait_ge(act_s, act_.at(i, f"f_hi_h{a}_{s - 1}"))
                            own(i, f"f_h{a}_{s - 1}")
                            step(dve.tensor_tensor(h_lo[:, s - 1, half(a)], normed_half(s - 1),
                                                   exact(h_hi[:, s - 1, half(a)]), ALU.subtract),
                                 f"f_lo_h{a}_{s - 1}")

                norm_mixed(0)
                split(i, U_UP)
                split(i, U_UP + 1)
                norm_mixed(1)
                norm_x(0)
                norm_x(1)

                def ffn_block(f, last=False):
                    par[0] = 0
                    split(i, f * 2 + (U_UP + 2))
                    dve.wait_ge(evacuated[0], i * (OUTS // 2) + f + (O_UP // 2 + 2))
                    dve.wait_ge(past_mid, i * (2 * NF) + f * 2 + 3)
                    for t in (1, 0):
                        dve.scalar_tensor_tensor(cg[:, :, :], gx[:, :, t:t + 266], taps[:, t, bass.ds(f, 1)], cg[:, :, :],
                                                 ALU.mult, ALU.add).then_inc(tapped, 1)
                        if t:
                            dve.wait_ge(tapped, i * (2 * NF) + f * 2 + 3)
                    dve.wait_ge(gelu_made, i * NF + f + 1)
                    dve.wait_ge(ticks, tick(i, f * 2 + (U_UP + 1)))
                    y2 = split2(yf[:, :])
                    dve.tensor_tensor(y2[:, :, 0:HP], cg[:, :, 0:HP], G[1][:, :, 0:HP], ALU.mult)
                    dve.tensor_tensor(y2[:, :, HP:], cg[:, :, HP + 2:], G[1][:, :, HP:HALF], ALU.mult)\
                       .then_inc(evacuated[1], 1)
                    if not last:
                        par[0] = 1
                        split(i, f * 2 + (U_UP + 3))
                    dve.wait_ge(hidden_hi, i * NF + f + 1)
                    dve.tensor_tensor(y_lo[:, bass.ds(f, 1), :].rearrange("p o c -> p (o c)"), yf[:, :],
                                      exact(y_hi[:, bass.ds(f, 1), :]).rearrange("p o c -> p (o c)"),
                                      ALU.subtract).then_inc(hidden_lo, 1)

                with dve.Fori(0, NF - 1) as f:
                    ffn_block(f)
                ffn_block(NF - 1, last=True)

                def p_rest(x, cols, name, last_read):
                    dve.wait_ge(act_s, act_.at(i, last_read))
                    for b in range(2):
                        last = dve.tensor_tensor(p_lo[:, :, cols[b]:cols[b] + P],
                                                 X[x][:, b, 0:256].rearrange("p (k c) -> p k c", k=2),
                                                 exact(p_hi[:, :, cols[b]:cols[b] + P]), ALU.subtract)
                    step(last, f"p_lo{name}")

                dve.wait_ge(past_mid, i * (2 * NF) + (2 * NF + 2))
                p_rest(0, (group_cols(0), group_cols(1)), "01", "p_hi_small")
                p_rest(1, (group_cols(2), group_cols(3)), "23", "conv_out")
                step(dve.tensor_tensor(p_lo[:, :, :].rearrange("p k (a c) -> p k a c", a=2)[:, :, :, HP:],
                                       X[0][:, 0, 256:288].rearrange("p (k a c) -> p k a c", k=2, a=2),
                                       exact(p_hi[:, :, :]).rearrange("p k (a c) -> p k a c", a=2)[:, :, :, HP:],
                                       ALU.subtract), "p_lo_small")
                step(dve.memset(total[:, :], 0.0), "zeros_ffn")
                own(i, "zeros_ffn")
                dve.sem_inc(passed, 1)
                with dve.Fori(0, KD // 2) as j:
                    for r in range(6):
                        par[0] = (r + 1) % 2
                        split(i, j * 6 + (U_DOWN + r + 1), DOWN_PARTS[(r + 1) % 3][1])
                        if r % 3 == 2:
                            par[0] = r // 3
                            add_square(i, j * 2 + (SQ_FFN + r // 3))
                split(i, U_PLE + 1)
                dve.wait_ge(act_s, act_.at(i, "rms_post_ffn"))
                for s in range(KD + 2):
                    if s == 3:
                        split(i, U_GATE)
                    if s == 6:
                        split(i, U_GATE + 1)
                    if s < KD:
                        step(dve.scalar_tensor_tensor(ffn_out[:, s, :], ffn_out[:, s, :], gains[:, 3, s:s + 1],
                                                      rms[:, :], ALU.mult, ALU.mult), f"ffn{s}")
                    if 1 <= s <= KD and s - 1 not in POOL_ADDS:
                        own(i, f"ffn{s - 1}")
                        step(dve.tensor_tensor(xT[:, s - 1, :], xT[:, s - 1, :], ffn_out[:, s - 1, :], ALU.add),
                             f"x_ffn{s - 1}")
                    if s >= 2:
                        dve.wait_ge(act_s, act_.at(i, f"x_hi{s - 2}"))
                        step(dve.tensor_tensor(h_lo[:, s - 2, :], xT[:, s - 2, :], exact(h_hi[:, s - 2, :]),
                                               ALU.subtract), f"x_lo{s - 2}")

                def gate(j, r):
                    if isinstance(j, int):
                        flat = lambda t: t[:, r, :]
                    else:
                        flat = lambda t: t[:, bass.ds(j * 2 + r, 1), :].rearrange("p o c -> p (o c)")
                    dve.wait_ge(evacuated[r % 2], i * (OUTS // 2) + j + ((O_GATE + r) // 2 + 2))
                    dve.tensor_tensor(sig[:, r % 2, :], sig[:, r % 2, :], flat(ple), ALU.mult).then_inc(gated, 1)
                    dve.wait_ge(gated, i * KD + j * 2 + (r + 1))
                    dve.tensor_tensor(sig[:, r % 2, :], flat(xT), sig[:, r % 2, :], ALU.add).then_inc(added, 1)

                gate(0, 0)
                split(i, U_GATE + 2)
                gate(0, 1)
                for k in range(3):
                    sum_x(i + 1, k, k)
                with dve.Fori(0, KD // 2 - 2) as j:
                    for r in (2, 3):
                        par[0] = (r + 1) % 2
                        split(i, j * 2 + (U_GATE + r + 1))
                        gate(j, r)
                        sum_x(i + 1, j * 2 + (r + 1))
                split(i, U_GATE + 7)
                gate(0, 6)
                sum_x(i + 1, 7, 7)
                split(i, UNITS)
                gate(0, 7)

        @block.tensor
        def _(pe):
            drained = {0: None, 1: None}

            def use(i, x, steps, name):
                if drained[x]:
                    s, n = drained[x]
                    pe.wait_ge(s.sem, s.at(i, n))
                drained[x] = (steps, name)

            def product(ps, lhs_hi, lhs_lo, rhs_hi, rhs_lo, start=True, stop=True):
                for n, (l, r) in enumerate(((lhs_hi, rhs_hi), (lhs_lo, rhs_hi), (lhs_hi, rhs_lo))):
                    for a in range(2):
                        last = pe.matmul(ps[:, a, 0:HALF], l, r[:, HALF * a:HALF * a + HALF],
                                         start=start and n == 0, stop=stop and n == 2)
                return last

            def product_half(ps, a, lhs_hi, lhs_lo, rhs_hi, rhs_lo, start, stop):
                for n, (l, r) in enumerate(((lhs_hi, rhs_hi), (lhs_lo, rhs_hi), (lhs_hi, rhs_lo))):
                    last = pe.matmul(ps[:, a, 0:HALF], l, r[:, half(a)], start=start and n == 0,
                                     stop=stop and n == 2)
                return last

            def half_block(s, k, a):
                return product_half(G[s], a, w_hi[s][:, k, :], w_lo[s][:, k, :], h_hi[:, k, :], h_lo[:, k, :],
                                    k == 0, k == KD - 1)

            def slot_ready(s, i, n, o):
                pe.wait_ge(lo_made, i * UNITS + (n + s + 3))
                pe.wait_ge(evacuated[s], i * (OUTS // 2) + out_of(o)[1])

            def unit(i, n, s, o, hi, lo, first=0, parts=KD, start=True, stop=True, ready=None):
                pe.wait_ge(lo_made, i * UNITS + (n + 3))
                if start:
                    pe.wait_ge(evacuated[o[0]], i * (OUTS // 2) + o[1])
                for k in range(parts):
                    if ready:
                        pe.wait_ge(vec_s, vec_.at(i, ready(k)))
                    last = product(G[o[0]], w_hi[s][:, k, :], w_lo[s][:, k, :], hi[:, first + k, :],
                                   lo[:, first + k, :], start and k == 0, stop and k == parts - 1)
                last.then_inc(ticks, 1)

            def unit_pair(i, n, o, hi, lo, ready):
                for t in range(KD + LAG):
                    if t < KD:
                        pe.wait_ge(vec_s, vec_.at(i, ready(t)))
                    for s, k in ((0, t), (1, t - LAG)):
                        if k == 0:
                            slot_ready(s, i, n, o)
                        if 0 <= k < KD:
                            last = product(G[s], w_hi[s][:, k, :], w_lo[s][:, k, :], hi[:, k, :], lo[:, k, :],
                                           k == 0, k == KD - 1)
                            if k == KD - 1:
                                last.then_inc(ticks, 1)

            def out_of(o):
                return o % 2, o // 2 + 1

            def ones_sum(x, src):
                for a in range(2):
                    last = pe.matmul(X[x][:, a, 0:HALF], ones[:, :], src[:, HALF * a:HALF * a + HALF],
                                     start=True, stop=True)
                return last

            def turn(out, in_, n=P):
                return pe.transpose(out, in_, ident[0:n, 0:n])

            pe.wait_ge(built, 3)
            pe.wait_ge(credited, 1)

            def turn_x(k, x):
                cols = slice(k * P, k * P + P)
                for g in range(NG):
                    turn(X[x][:, g // 2, P * (g % 2):P * (g % 2) + P], x_tok[:, g, cols])
                for a in range(2):
                    last = turn(X[x][:, a, HP:HALF], x_small[:, a, cols], SLEN)
                last.then_inc(x_turned, 1)

            pe.wait_ge(x_loaded, 16 * (NG + 1))
            for k in range(KD):
                if k >= 2:
                    pe.wait_ge(squared, k - 1)
                turn_x(k, (k + 1) % 2)
            pe.wait_ge(summed, 8 + 2)
            ones_sum(1, total).then_inc(x_summed, 1)
            pe.wait_ge(built, BUILT)
            pe.wait_ge(split_once, 4)

            with pe.Fori(0, TILES) as i:
                drained[0] = drained[1] = None
                pe.wait_ge(states_loaded, i * 32 + 32)
                pe.wait_ge(y_copied, i * 8 + 8)
                use(i, 0, act_, "conv_state")
                turn(X[0][:, 0, 0:120], z_state_tok[:, :], 120)
                pe_.did(turn(X[0][:, 1, 0:4 * NF], g_state_tok[:, :], 4 * NF), "states_turned")
                use(i, 1, act_, "glow")
                pe.wait_ge(x_rms, i + 1)
                pe.wait_ge(lo_made, i * UNITS + 3)
                pe.wait_ge(evacuated[0], i * (OUTS // 2) + 1)
                for k in range(KD):
                    pe.wait_ge(vec_s, vec_.at(i, f"h_lo{k}"))
                    last = product(X[1], w_glow_hi[:, RANK * k:RANK * k + P], w_glow_lo[:, RANK * k:RANK * k + P],
                                   h_hi[:, k, :], h_lo[:, k, :], k == 0, k == KD - 1)
                    if k == KD - 1:
                        pe_.did(last, "glow")
                    last = product(G[0], w_hi[0][:, k, :], w_lo[0][:, k, :], h_hi[:, k, :], h_lo[:, k, :],
                                   k == 0, k == KD - 1)
                last.then_inc(ticks, 1)

                def head_rows(b):
                    return slice(64 * b, 64 * b + 64)

                def scores(h, x):
                    use(i, x, vec_, f"scores{h}")
                    n = LEVELS.index(h) % 2
                    pe.wait_ge(vec_s, vec_.at(i, f"operand{h}"))
                    for d in range(2):
                        for c in range(NG):
                            last = pe.matmul(X[x][:, d, P * c:P * c + P].rearrange("p (b t) -> p b t", b=2),
                                             opnd[n][:, d, group_cols(c):group_cols(c) + P],
                                             queries[n][:, d, c // 2, :, 64 * (c % 2):64 * (c % 2) + 64],
                                             start=True, stop=True)
                    pe_.did(last, f"scores{h}")

                def small_tokens(t, b, d, a):
                    return t[head_rows(b), d, HALF * a + HP:HALF * a + HALF]

                def small_scores(h, x):
                    use(i, x, vec_, f"small{h}")
                    pe.sem_inc(passed, 1)
                    t = opnd[LEVELS.index(h) % 2]
                    for d in range(2):
                        for a in range(2):
                            for b in range(2):
                                keys = small_tokens(t, b, d, a)
                                queries = keys.rearrange("p (n w) -> p n w", w=2 * h)[:, :, h:]
                                col = 4 * (2 * d + a)
                                last = pe.matmul(X[x][0:SLEN, b, col:col + 4], keys, queries, start=True, stop=True)
                    pe_.did(last, f"small{h}")

                def out_chunk(c):
                    x = (c + 1) % 2
                    use(i, x, act_, f"out{c}")
                    pe.wait_ge(vec_s, vec_.at(i, f"state{c - 1}" if c else "qb"))
                    cols = slice(group_cols(c), group_cols(c) + P)
                    for h in range(HEADS):
                        d, b = h // 2, h % 2
                        out = X[x][:, b, P * d:P * d + P]
                        pe.matmul(out, v_tok[:, c, P * h:P * h + P], A[:, 8 * d + 2 * c + b, :],
                                  start=True, stop=False)
                        pe.matmul(out, S[head_rows(b), d, :], qT[head_rows(b), d, cols], start=False, stop=True)
                    for d in range(2):
                        last = pe.matmul(X[x][:, d, 256:512], kd_tok[:, c, d, :],
                                         v_tok[:, c, 256 * d:256 * d + 256], start=True, stop=True)
                    pe_.did(last, f"out{c}")

                def pool_group(g, ready=None):
                    use(i, 1, vec_, f"mix_lo{g}")
                    if ready:
                        pe.wait_ge(vec_s, vec_.at(i, ready))
                    pe_.did(product(X[1], w_pool_hi[:, g, :], w_pool_lo[:, g, :], u_hi[:, g % 2, :], u_lo[:, g % 2, :]),
                            f"pool{g}")

                def extras(s):
                    if s == 0:
                        pe.wait_ge(act_s, act_.at(i, "glow"))
                        for d in range(2):
                            use(i, d, vec_, "gk_min")
                            for a in range(2):
                                last = pe.matmul(X[d][:, a, 0:HALF], w_gk[:, P * d:P * d + P],
                                                 squares[0:RANK, 0, HALF * a:HALF * a + HALF], start=True, stop=True)
                            pe_.did(last, f"gk{d}")
                    if s == 4:
                        use(i, 0, vec_, "scores_small_diag")
                        pe.wait_ge(vec_s, vec_.at(i, "qk"))
                        for d in range(2):
                            for c in range(NG):
                                for b in range(2):
                                    pe.matmul(X[0][:, b, 4 * d + c:4 * d + c + 1],
                                              opnd[1][head_rows(b), d, group_cols(c):group_cols(c) + P],
                                              ones[head_rows(b), 0:1], start=True, stop=True)
                            for a in range(2):
                                for b in range(2):
                                    col = 8 + 2 * d + a
                                    last = pe.matmul(X[0][0:SLEN, b, col:col + 1], small_tokens(opnd[1], b, d, a),
                                                     ones[head_rows(b), 0:1], start=True, stop=True)
                        pe_.did(last, "diag")
                        scores(64, 1)
                    if 5 <= s <= 10:
                        n = s - 4
                        h = LEVELS[n]
                        scores(h, (n + 1) % 2)
                        if h <= 4:
                            small_scores(h, n % 2)
                    if s in (8, 9):
                        if s == 8:
                            for o in (6, 7):
                                pe.wait_ge(*evac(i, o))
                        pe.wait_ge(*evac(i, s))
                        for c in (2 * s - 16, 2 * s - 15):
                            for h in range(HEADS):
                                last = turn(G[s % 2][:, c % 2, P * h:P * h + P],
                                            vT[:, h, group_cols(c):group_cols(c) + P])
                        pe_.did(last, f"v_turned{s - 8}")
                    if s == 10:
                        pe.wait_ge(*evac(i, s))
                        for a in range(2):
                            for h in range(HEADS):
                                last = turn(G[0][0:SLEN, a, P * h:P * h + P], vT[:, h, HALF * a + HP:HALF * a + HALF])
                        pe_.did(last, "v_small_turned")
                    if s == 11:
                        use(i, 1, act_, "kd_copied")
                        pe.wait_ge(vec_s, vec_.at(i, "kd"))
                        for c in range(NG):
                            for d in range(2):
                                last = turn(X[1][:, c // 2, P * (2 * (c % 2) + d):P * (2 * (c % 2) + d) + P],
                                            gap[:, d, group_cols(c):group_cols(c) + P])
                        pe_.did(last, "kd_turned")
                        use(i, 0, act_, "kd_small")
                        for a in range(2):
                            for d in range(2):
                                col = P * (2 * a + d)
                                last = turn(X[0][0:SLEN, 0, col:col + P], gap[:, d, HALF * a + HP:HALF * a + HALF])
                        pe_.did(last, "kd_small_turned")
                    if s >= 12:
                        out_chunk(s - 12)

                for m in range(16):
                    if 10 <= m <= 12:
                        pe.wait_ge(act_s, act_.at(i, ("v_copied0", "v_copied1", "v_small")[m - 10]))
                    if m:
                        unit(i, m, m % 2, out_of(m), h_hi, h_lo)
                    extras(m)
                pool_group(0, "state2")
                use(i, 0, act_, "out_small")
                pe.wait_ge(vec_s, vec_.at(i, "state3"))
                pe.wait_ge(s_loaded, i * 16 + 16)
                for h in range(HEADS):
                    d, b = h // 2, h % 2
                    for a in range(2):
                        out = X[0][:, b, 16 * d + 8 * a:16 * d + 8 * a + 8]
                        pe.matmul(out, v_small[:, a, P * h:P * h + P], A_s[:, 4 * b + 2 * d + a, :],
                                  start=True, stop=False)
                        last = pe.matmul(out, S_s[head_rows(b), a, d, :],
                                         qT[head_rows(b), d, HALF * a + HP:HALF * a + HALF], start=False, stop=True)
                pe_.did(last, "out_small")
                pool_group(1)
                use(i, 0, vec_, "state_small")
                for a in range(2):
                    for d in range(2):
                        last = pe.matmul(X[0][:, a, 256 * d:256 * d + 256], kd_small[:, a, P * d:P * d + P],
                                         v_small[:, a, 256 * d:256 * d + 256], start=True, stop=True)
                pe_.did(last, "state_small")
                pool_group(2)
                for h in range(HEADS):
                    use(i, HEAD_BANKS[h], act_, f"rms_head{h}")
                    if h == 0:
                        pe.wait_ge(act_s, act_.at(i, "out_squares"))
                    pe_.did(ones_sum(HEAD_BANKS[h], out_sq[:, h, :]), f"head{h}")
                    if h == 0:
                        pool_group(3)
                use(i, 1, act_, "pool_state")
                pe.wait_ge(pool_s, pool_.at(i, "z_tail"))
                pe_.did(turn(X[1][0:120, 0, 0:P], z_state[:, :]), "pool_state_turned")

                def mixed_block(k):
                    return f"mix_lo{k}"

                unit_pair(i, U_O, O_O, h_hi, h_lo, mixed_block)
                with pe.Fori(0, KD // 2 - 2) as j:
                    for r in (2, 3):
                        unit(i, j * 2 + (U_O + r), r % 2, (r % 2, j + ((O_O + r) // 2 + 1)), h_hi, h_lo)
                def half_sum(a):
                    pe.matmul(X[1][:, a, 0:HALF], ones[:, :], total[:, half(a)], start=True, stop=False)
                    for r in range(2):
                        pe.wait_ge(squared, i * SQUARES + (SQ_HALVES + 2 * a + r + 1))
                        last = pe.matmul(X[1][:, a, 0:HALF], ones[:, :], squares[:, r, half(a)],
                                         start=False, stop=r == 1)
                        last.then_inc(summed, 1)

                def half_unit(s, a, blocks=range(KD)):
                    for k in blocks:
                        last = half_block(s, k, a)
                    return last

                use(i, 1, act_, "rms_post_mix1")
                slot_ready(0, i, U_O + KD - 2, O_O + KD - 2)
                half_unit(0, 0)
                half_unit(0, 1, range(KD // 2))
                slot_ready(1, i, U_O + KD - 2, O_O + KD - 2)
                pe_.did(half_unit(1, 0), "o_half")
                half_unit(0, 1, range(KD // 2, KD)).then_inc(ticks, 1)
                pe.wait_ge(summed, i * SQUARES + (SQ_HALVES + 2))
                half_sum(0)
                half_unit(1, 1).then_inc(ticks, 1)
                half_sum(1)
                use(i, 0, act_, "rms_pre_ffn1")
                for a in range(2):
                    for m in range(KD):
                        pe.wait_ge(squared, i * SQUARES + (SQ_X + KD * a + m + 1))
                        pe.matmul(X[0][:, a, 0:HALF], ones[:, :], squares[:, m % 2, half(a)],
                                  start=m == 0, stop=m == KD - 1).then_inc(summed, 1)

                for s in range(2):
                    slot_ready(s, i, U_UP, O_UP)
                for k in range(KD):
                    pe.wait_ge(*f_lo_done(i, 0, k))
                    for s in range(2):
                        half_block(s, k, 0)
                for s in range(2):
                    for k in range(KD):
                        if s == 0:
                            pe.wait_ge(*f_lo_done(i, 1, k))
                        last = half_block(s, k, 1)
                    last.then_inc(ticks, 1)
                with pe.Fori(0, NF - 1) as f:
                    for r in (2, 3):
                        unit(i, f * 2 + (U_UP + r), r % 2, (r % 2, f + ((O_UP + r) // 2 + 1)), h_hi, h_lo)

                pe.wait_ge(p_loaded, i * 32 + 32)
                use(i, 0, vec_, "p_lo_small")
                use(i, 1, act_, "conv_out")
                for n in range(2):
                    for b in range(2):
                        for k in range(2):
                            last = turn(X[n][:, b, P * k:P * k + P], p_tok[:, 2 * n + b, P * k:P * k + P])
                    if n == 0:
                        for k in range(2):
                            last = turn(X[0][:, 0, 256 + 16 * k:272 + 16 * k], p_small[:, P * k:P * k + P], 16)
                    else:
                        pe.wait_ge(past_mid, i * (2 * NF) + (2 * NF + 2))
                        last = turn(X[1][0:88, 0, 256:256 + P], g_tail[:, :, :, :].rearrange("p s t f -> p (s t f)"))
                    pe_.did(last, f"p_turned{'01' if n == 0 else '23'}")
                pe.wait_ge(hidden_lo, i * NF + (NF - 1))
                pe.sem_inc(passed, 1)
                with pe.Fori(0, KD // 2) as j:
                    for r in range(6):
                        first, parts = DOWN_PARTS[r % 3]
                        if r == 2:
                            pe.wait_ge(hidden_lo, i * NF + NF)
                        unit(i, j * 6 + (U_DOWN + r), r % 2, (r // 3, j + (O_DOWN // 2 + 1)), y_hi, y_lo,
                             first, parts, r % 3 == 0, r % 3 == 2)
                use(i, 0, act_, "rms_post_ffn")
                for m in range(KD):
                    s, q = m // 4, m % 4
                    if q == 0:
                        pe.wait_ge(lo_made, i * UNITS + (U_PLE + s + 3))
                    if m == 1:
                        pe.wait_ge(summed, i * SQUARES + (SQUARES + 2))
                        pe_.did(ones_sum(0, total), "sum_post_ffn")
                    pair, free = out_of(O_PLE + m)
                    pe.wait_ge(evacuated[pair], i * (OUTS // 2) + free)
                    for k in range(2):
                        last = product(G[pair], w_hi[s][:, 4 * k + q, :], w_lo[s][:, 4 * k + q, :],
                                       p_hi[:, k, :], p_lo[:, k, :], k == 0, k == 1)
                    last.then_inc(ticks, 1)

                def turn_y(r):
                    pe.wait_ge(added, i * KD + (r + 1))
                    if r < KD - 1:
                        pe.wait_ge(squared, (i + 1) * SQUARES + (r + 2))
                    x = r % 2
                    block_ = sig[:, x, :]
                    for c in range(NG):
                        turn(X[x][:, 0, P * c:P * c + P], block_[:, group_cols(c):group_cols(c) + P])
                    for a in range(2):
                        last = turn(X[x][0:SLEN, 1, P * a:P * a + P], block_[:, HALF * a + HP:HALF * a + HALF])
                    last.then_inc(y_turned, 1)

                unit_pair(i, U_GATE, O_GATE, h_hi, h_lo, lambda k: f"x_lo{k}")
                for x in range(2):
                    steps, n = drained[x]
                    pe.wait_ge(steps.sem, steps.at(i, n))
                pe.sem_inc(passed, 1)
                pe.wait_ge(x_loaded, (i + 2) * (16 * (NG + 1)))
                turn_x(0, 1)
                turn_x(1, 0)
                pe.wait_ge(squared, (i + 1) * SQUARES + 1)
                turn_x(2, 1)
                turn_y(0)
                for m in range(2, KD):
                    unit(i, U_GATE + m, m % 2, out_of(O_GATE + m), h_hi, h_lo)
                    pe.wait_ge(y_copied, i * 8 + (m + 7))
                    if m < KD - 1:
                        turn_x(m + 1, m % 2)
                    else:
                        pe.wait_ge(summed, (i + 1) * SQUARES + (8 + 2))
                        ones_sum(1, total).then_inc(x_summed, 1)
                    turn_y(m - 1)
                pe.wait_ge(x_rms, i + 2)
                turn_y(7)

            pe.wait_ge(y_copied, TILES * 8 + 8)
            pe.wait_ge(last_packed, 1)
            turn(X[0][0:60, 0, 0:P], z_state[:, 0:60]).then_inc(last_turned, 1)
            turn(X[1][0:44, 0, 0:P], g_past[:, :, :].rearrange("p t f -> p (t f)")).then_inc(last_turned, 1)


_INS = ['x_prompt', 'x_sample', 'state_pool', 'state_gla', 'state_conv', 'p_prompt', 'p_sample', 'g_pre_mix',
        'w_in', 'w_gk2', 'b_gk2', 'w_pool', 'pool_scale', 'gla_norm', 'w_o', 'g_post_mix', 'g_pre_ffn', 'w_up',
        'w_conv', 'b_conv', 'w_down', 'g_post_ffn', 'w_ple', 'w_ple_gate']
_OUTS = [(1, SEQ, D), (NSEQ, SLEN, D), (1, 1, HIST, POOLW), (1, 1, HEADS, KDIM, VDIM), (1, 1, 2, FF),
         (1, NSEQ, HIST, POOLW), (1, NSEQ, HEADS, KDIM, VDIM), (1, NSEQ, 2, FF)]


def kernel(**inputs):
    import numpy as _np
    import concourse.bacc as _bacc
    from concourse.bass_utils import run_bass_kernel_spmd as _run

    nc = _bacc.Bacc("TRN2", target_bir_lowering=False, num_devices=1)
    arrays, args = {}, []
    for name in _INS:
        a = _np.ascontiguousarray(inputs[name])
        arrays[f"in_{name}_dram"] = a
        args.append(nc.dram_tensor(f"in_{name}_dram", a.shape, F32, kind="ExternalInput").ap())
    for n, shape in enumerate(_OUTS):
        args.append(nc.dram_tensor(f"out_{n}_dram", shape, F32, kind="ExternalOutput").ap())
    hybrid_layer(nc, *args)
    r = _run(nc, [arrays], core_ids=[0])
    return tuple(r.results[0][f"out_{n}_dram"] for n in range(len(_OUTS)))
```
